# Optimizing a Trainium2 kernel written in Bass

```python
import math
import jax, jax.numpy as jnp
from jax import lax
import numpy as np

D_MODEL = 1024
BATCH = 1
SEQ = 1024
DEPTH = 2

GRID_W = 64
CTX_LEN = 256
HEAD_DIM = 64
HG_HEADS = 4
HG_DK = 64
HG_DV = 64
HG_CHUNK = 64
GQA_HEADS = 6
GQA_KV_HEADS = 2
NA_HEADS = 6
NA_KH_MAX = 8
NA_KW = 16
ATTN_BLOCK = 128
ROPE_THETA = 10000.0
NORM_EPS = 1e-6
N_MOD = 6

HG_W = HG_HEADS * HG_DV
GQA_W = GQA_HEADS * HEAD_DIM
GQA_KV_W = GQA_KV_HEADS * HEAD_DIM
NA_W = NA_HEADS * HEAD_DIM
MIX_W = HG_W + GQA_W + NA_W
IN_SIZES = (HG_W, HG_W, HG_W, HG_W, HG_W, GQA_W, GQA_KV_W, GQA_KV_W, NA_W, NA_W, NA_W)
IN_W = sum(IN_SIZES)
FFN_HIDDEN = ((8 * D_MODEL + 3 * 256 - 1) // (3 * 256)) * 256
DN_ALPHA = (2 * DEPTH) ** 0.25
DN_BETA = (8 * DEPTH) ** -0.25

kernel_name = 'hybrid_hgrn2_gqa_natten_deepnorm_dit'

def rms_norm(x, g):
    x = x.astype(jnp.float32)
    return x * lax.rsqrt(jnp.mean(x * x, -1, keepdims=True) + NORM_EPS) * g

def layer_norm(x, g, b):
    x = x.astype(jnp.float32)
    xc = x - jnp.mean(x, -1, keepdims=True)
    return xc * lax.rsqrt(jnp.mean(xc * xc, -1, keepdims=True) + NORM_EPS) * g + b

def heads(a, n):
    return a.reshape(a.shape[:-1] + (n, a.shape[-1] // n))

def adaln(cv, w, b):
    return jax.nn.silu(cv) @ w + b

def modulate(x, shift, scale):
    return x * (1.0 + scale) + shift

def axial_rope_tables(n_tokens):
    t = jnp.arange(n_tokens, dtype=jnp.int32)
    row = (t // GRID_W).astype(jnp.float32)
    col = (t % GRID_W).astype(jnp.float32)
    n_pairs = HEAD_DIM // 4
    inv_freq = jnp.exp(-math.log(ROPE_THETA) * jnp.arange(n_pairs, dtype=jnp.float32) / n_pairs)
    ang = jnp.concatenate([row[:, None] * inv_freq, col[:, None] * inv_freq], -1)
    return jnp.cos(ang)[None, :, None, :], jnp.sin(ang)[None, :, None, :]

def apply_rope(x, cos, sin):
    x1, x2 = x[..., 0::2], x[..., 1::2]
    return jnp.stack([x1 * cos - x2 * sin, x1 * sin + x2 * cos], -1).reshape(x.shape)

def hgrn_lower_bounds(logits):
    p = jax.nn.softmax(logits.astype(jnp.float32), axis=0)
    return jnp.clip(jnp.cumsum(p, axis=0) - p[0], 0.0, 1.0)

def gla_chunk_scan(q, k, logf, v, s0, with_output):
    b_, n, h, _ = q.shape
    dv = v.shape[-1]
    nc = n // HG_CHUNK

    def to_chunks(a):
        return a.reshape(b_, nc, HG_CHUNK, h, a.shape[-1]).transpose(1, 0, 3, 2, 4)

    incl = jnp.tril(jnp.ones((HG_CHUNK, HG_CHUNK), bool))[:, :, None]

    def step(s, inp):
        qc, kc, gc, vc = inp
        cum = jnp.cumsum(gc, axis=2)
        tot = cum[:, :, -1:, :]
        s_new = jnp.exp(tot)[:, :, 0, :, None] * s + jnp.einsum('bhsk,bhsv->bhkv', kc * jnp.exp(tot - cum), vc)
        if not with_output:
            return s_new, None
        diff = cum[:, :, :, None, :] - cum[:, :, None, :, :]
        pair = jnp.where(incl, jnp.exp(jnp.minimum(diff, 0.0)), 0.0)
        att = jnp.einsum('bhtk,bhsk,bhtsk->bhts', qc, kc, pair)
        o = jnp.einsum('bhts,bhsv->bhtv', att, vc) + jnp.einsum('bhtk,bhkv->bhtv', qc * jnp.exp(cum), s)
        return s_new, o

    s_fin, o = lax.scan(step, s0, (to_chunks(q), to_chunks(k), to_chunks(logf), to_chunks(v)))
    if with_output:
        o = o.transpose(1, 0, 3, 2, 4).reshape(b_, n, h, dv)
    return o, s_fin

def hgrn2_mix(p_lat, p_ctx, lb, norm_g, need_ctx):
    def prep(p):
        q, f_fwd, f_bwd, i, g = p
        logf = [heads(jnp.log(lb[d] + (1.0 - lb[d]) * jax.nn.sigmoid(f)), HG_HEADS)
                for d, f in enumerate((f_fwd, f_bwd))]
        return heads(jax.nn.silu(q), HG_HEADS), heads(i, HG_HEADS), g, logf

    q_c, i_c, g_c, lf_c = prep(p_ctx)
    q_l, i_l, g_l, lf_l = prep(p_lat)
    s0 = jnp.zeros((q_l.shape[0], HG_HEADS, HG_DK, HG_DV), jnp.float32)
    rev = lambda a: jnp.flip(a, axis=1)
    o_cf, s_cf = gla_chunk_scan(q_c, -jnp.expm1(lf_c[0]), lf_c[0], i_c, s0, need_ctx)
    o_lf, _ = gla_chunk_scan(q_l, -jnp.expm1(lf_l[0]), lf_l[0], i_l, s_cf, True)
    o_cb, s_cb = gla_chunk_scan(rev(q_c), -jnp.expm1(rev(lf_c[1])), rev(lf_c[1]), rev(i_c), s0, need_ctx)
    o_lb, _ = gla_chunk_scan(rev(q_l), -jnp.expm1(rev(lf_l[1])), rev(lf_l[1]), rev(i_l), s_cb, True)

    def readout(o, g):
        return rms_norm(o, norm_g).reshape(g.shape) * jax.nn.silu(g)

    y_lat = readout(o_lf + rev(o_lb), g_l)
    y_ctx = readout(o_cf + rev(o_cb), g_c) if need_ctx else None
    return y_lat, y_ctx

def attend(q, k, v):
    s = jnp.einsum('bqkgd,bskd->bkgqs', q, k) * (q.shape[-1] ** -0.5)
    p = jax.nn.softmax(s.astype(jnp.float32), axis=-1)
    return jnp.einsum('bkgqs,bskd->bqkgd', p, v)

def blocked_attention(q, k, v):
    b_, n, h, dh = q.shape
    hkv = k.shape[2]
    nb = n // ATTN_BLOCK
    qb = q.reshape(b_, nb, ATTN_BLOCK, hkv, h // hkv, dh).transpose(1, 0, 2, 3, 4, 5)
    o = lax.map(lambda blk: attend(blk, k, v), qb)
    return o.transpose(1, 0, 2, 3, 4, 5).reshape(b_, n, h * dh)

def dense_attention(q, k, v):
    b_, n, h, dh = q.shape
    hkv = k.shape[2]
    return attend(q.reshape(b_, n, hkv, h // hkv, dh), k, v).reshape(b_, n, h * dh)

def gqa_mix(p_lat, p_ctx, q_norm, k_norm, cos, sin, need_ctx):
    def prep(p):
        q, k, v = p
        return (rms_norm(heads(q, GQA_HEADS), q_norm), rms_norm(heads(k, GQA_KV_HEADS), k_norm),
                heads(v, GQA_KV_HEADS))

    q_l, k_l, v_l = prep(p_lat)
    q_c, k_c, v_c = prep(p_ctx)
    q_l, k_l = apply_rope(q_l, cos, sin), apply_rope(k_l, cos, sin)
    k_all = jnp.concatenate([k_l, k_c], axis=1)
    v_all = jnp.concatenate([v_l, v_c], axis=1)
    y_lat = blocked_attention(q_l, k_all, v_all)
    y_ctx = dense_attention(q_c, k_c, v_c) if need_ctx else None
    return y_lat, y_ctx

def na_mix(p_lat, p_ctx, rpb, need_ctx):
    q_l, k_l, v_l = [heads(a, NA_HEADS) for a in p_lat]
    q_c, k_c, v_c = [heads(a, NA_HEADS) for a in p_ctx]
    b_, n = q_l.shape[:2]
    rows = n // GRID_W
    kh = min(NA_KH_MAX, rows)
    scale = HEAD_DIM ** -0.5
    cols = jnp.arange(GRID_W)
    col_idx = jnp.clip(cols - NA_KW // 2, 0, GRID_W - NA_KW)[:, None] + jnp.arange(NA_KW)
    dc = col_idx - cols[:, None] + (NA_KW - 1)
    n_loc = kh * NA_KW

    def row_block(r):
        row_idx = jnp.clip(r - kh // 2, 0, rows - kh) + jnp.arange(kh)
        idx = row_idx[None, :, None] * GRID_W + col_idx[:, None, :]
        kg, vg = k_l[:, idx], v_l[:, idx]
        qr = lax.dynamic_slice_in_dim(q_l, r * GRID_W, GRID_W, axis=1) * scale
        bias = rpb[:, (row_idx - r + NA_KH_MAX - 1)[None, :, None], dc[:, None, :]]
        s_loc = jnp.einsum('bchd,bcijhd->bhcij', qr, kg) + bias
        s_ctx = jnp.einsum('bchd,blhd->bhcl', qr, k_c)
        s = jnp.concatenate([s_loc.reshape(b_, NA_HEADS, GRID_W, n_loc), s_ctx], -1)
        p = jax.nn.softmax(s.astype(jnp.float32), axis=-1)
        p_loc = p[..., :n_loc].reshape(b_, NA_HEADS, GRID_W, kh, NA_KW)
        return (jnp.einsum('bhcij,bcijhd->bchd', p_loc, vg)
                + jnp.einsum('bhcl,blhd->bchd', p[..., n_loc:], v_c))

    o = lax.map(row_block, jnp.arange(rows))
    y_lat = o.transpose(1, 0, 2, 3, 4).reshape(b_, n, NA_W)
    y_ctx = dense_attention(q_c, k_c, v_c) if need_ctx else None
    return y_lat, y_ctx

def mixing_sublayer(h_lat, h_ctx, w_in, lb, hg_norm, q_norm, k_norm, rpb, w_out, cos, sin, need_ctx):
    split_at = np.cumsum(IN_SIZES)[:-1].tolist()
    p_lat = jnp.split((h_lat @ w_in).astype(jnp.float32), split_at, axis=-1)
    p_ctx = jnp.split((h_ctx @ w_in).astype(jnp.float32), split_at, axis=-1)
    hg_l, hg_c = hgrn2_mix(p_lat[0:5], p_ctx[0:5], lb, hg_norm, need_ctx)
    gq_l, gq_c = gqa_mix(p_lat[5:8], p_ctx[5:8], q_norm, k_norm, cos, sin, need_ctx)
    na_l, na_c = na_mix(p_lat[8:11], p_ctx[8:11], rpb, need_ctx)
    y_lat = jnp.concatenate([hg_l, gq_l, na_l], axis=-1) @ w_out
    y_ctx = jnp.concatenate([hg_c, gq_c, na_c], axis=-1) @ w_out if need_ctx else None
    return y_lat, y_ctx

def swiglu(h, w1, w2):
    gate, up = jnp.split(h @ w1, 2, axis=-1)
    return (jax.nn.silu(gate) * up) @ w2

def setup_inputs(seed: int = 0) -> dict:
    key = jax.random.key(seed)
    ks = jax.random.split(key, 17)
    f32 = jnp.float32

    def nrm(k, shape, s):
        return jax.random.normal(k, shape, f32) * s

    return {
        'x': nrm(ks[0], (BATCH, SEQ, D_MODEL), 1.0),
        'c': nrm(ks[1], (BATCH, D_MODEL), 1.0),
        'ctx': nrm(ks[2], (BATCH, CTX_LEN, D_MODEL), 1.0),
        'c_ctx': nrm(ks[3], (D_MODEL,), 1.0),
        'w_ada': nrm(ks[4], (DEPTH, D_MODEL, N_MOD * D_MODEL), 0.5 * D_MODEL ** -0.5),
        'b_ada': nrm(ks[5], (DEPTH, N_MOD * D_MODEL), 0.02),
        'w_in': nrm(ks[6], (DEPTH, D_MODEL, IN_W), D_MODEL ** -0.5),
        'hgrn_lb_logits': nrm(ks[7], (DEPTH, 2, HG_W), 1.0),
        'hgrn_norm': 1.0 + nrm(ks[8], (DEPTH, HG_DV), 0.02),
        'gqa_q_norm': 1.0 + nrm(ks[9], (DEPTH, HEAD_DIM), 0.02),
        'gqa_k_norm': 1.0 + nrm(ks[10], (DEPTH, HEAD_DIM), 0.02),
        'na_rpb': nrm(ks[11], (DEPTH, NA_HEADS, 2 * NA_KH_MAX - 1, 2 * NA_KW - 1), 0.1),
        'w_out': nrm(ks[12], (DEPTH, MIX_W, D_MODEL), DN_BETA * MIX_W ** -0.5),
        'w_ffn_in': nrm(ks[13], (DEPTH, D_MODEL, 2 * FFN_HIDDEN), D_MODEL ** -0.5),
        'w_ffn_out': nrm(ks[14], (DEPTH, FFN_HIDDEN, D_MODEL), DN_BETA * FFN_HIDDEN ** -0.5),
        'ln_g': 1.0 + nrm(ks[15], (DEPTH, 2, D_MODEL), 0.02),
        'ln_b': nrm(ks[16], (DEPTH, 2, D_MODEL), 0.02),
    }

def reference(x, c, ctx, c_ctx, w_ada, b_ada, w_in, hgrn_lb_logits, hgrn_norm, gqa_q_norm, gqa_k_norm,
              na_rpb, w_out, w_ffn_in, w_ffn_out, ln_g, ln_b):
    cos, sin = axial_rope_tables(x.shape[1])
    lbs = hgrn_lower_bounds(hgrn_lb_logits)
    x_lat, x_ctx = x, ctx
    for l in range(DEPTH):
        need_ctx = l < DEPTH - 1
        m_lat = jnp.split(adaln(c, w_ada[l], b_ada[l])[:, None, :], N_MOD, axis=-1)
        m_ctx = jnp.split(adaln(c_ctx, w_ada[l], b_ada[l]), N_MOD, axis=-1)
        y_lat, y_ctx = mixing_sublayer(
            modulate(x_lat, m_lat[0], m_lat[1]), modulate(x_ctx, m_ctx[0], m_ctx[1]),
            w_in[l], lbs[l], hgrn_norm[l], gqa_q_norm[l], gqa_k_norm[l], na_rpb[l], w_out[l],
            cos, sin, need_ctx)
        x_lat = layer_norm(DN_ALPHA * x_lat + m_lat[2] * y_lat, ln_g[l, 0], ln_b[l, 0])
        f_lat = swiglu(modulate(x_lat, m_lat[3], m_lat[4]), w_ffn_in[l], w_ffn_out[l])
        x_lat = layer_norm(DN_ALPHA * x_lat + m_lat[5] * f_lat, ln_g[l, 1], ln_b[l, 1])
        if need_ctx:
            x_ctx = layer_norm(DN_ALPHA * x_ctx + m_ctx[2] * y_ctx, ln_g[l, 0], ln_b[l, 0])
            f_ctx = swiglu(modulate(x_ctx, m_ctx[3], m_ctx[4]), w_ffn_in[l], w_ffn_out[l])
            x_ctx = layer_norm(DN_ALPHA * x_ctx + m_ctx[5] * f_ctx, ln_g[l, 1], ln_b[l, 1])
    return x_lat


_drawn_inputs = setup_inputs


def setup_inputs(seed=0):
    import zlib

    import numpy as np

    out = dict(_drawn_inputs(seed))
    spreads = {}
    factors = {'ctx': 6.798,
     'c_ctx': 3.203,
     'b_ada': 5.751,
     'hgrn_lb_logits': 8.0,
     'hgrn_norm': 43.927,
     'gqa_q_norm': 8.0,
     'gqa_k_norm': 8.0,
     'na_rpb': 64.0}
    for name, (base, spread) in spreads.items():
        noise = np.random.default_rng([zlib.crc32(name.encode()), seed]).standard_normal(out[name].shape)
        drawn = base * np.exp(spread * noise) if base else spread * noise
        out[name] = __import__('jax').numpy.asarray(drawn.astype(out[name].dtype))
    for name, factor in factors.items():
        out[name] = (out[name] * factor).astype(out[name].dtype)
    return out
```

```python
from contextlib import ExitStack

import concourse.bass as bass
from concourse import mybir
import numpy as np

F32 = mybir.dt.float32
F32R = mybir.dt.float32r
ALU = mybir.AluOpType
ACT = mybir.ActivationFunctionType
AX = mybir.AxisListType

P = 128
D = 1024
KB = D // P
SEQ, CTX = 1024, 256
NT = SEQ + CTX
TT = NT // P
DEPTH = 2
HD = 64
GRID_W = 64
ROWS = SEQ // GRID_W
FFN = ((8 * D + 3 * 256 - 1) // (3 * 256)) * 256
HB = FFN // P
N_MOD = 6
MB = N_MOD * KB
IN_W = 3072
ALPHA = (2 * DEPTH) ** 0.25
EPS = 1e-6
SCALE = HD ** -0.5
CHUNK = 64
LEVELS = 6
NL = LEVELS + 1
LOG_SHIFT = 64
NEG = -1e30
HG_COL, GQ_COL, NA_COL = 0, 1280, 1920
NA_KH, NA_KW = 8, 16
SLOTS = 14
MID = 9
CHUNKS = [(0, 512), (512, 512), (1024, 256)]


class Sem:

    def __init__(self, nc, stack, name):
        self.h = stack.enter_context(nc.semaphore(name))
        self.base = 0

    def at(self, n):
        return n + self.base

    def done(self, n):
        self.base += n


def token_chunks(tokens):
    return [c for c in CHUNKS if c[0] < tokens]


def in_pairs(e, n, body):
    if n // 2 > 1:
        with e.Fori(0, n // 2) as i:
            for s in range(2):
                body(i * 2 + s, s, i)
    else:
        for u in range(n // 2 * 2):
            body(u, u % 2, u // 2)
    if n % 2:
        body(n - 1, (n - 1) % 2, (n - 1) // 2)


class Kernel:
    def __init__(self, nc, stack, a, out):
        self.nc, self.a, self.out = nc, a, out
        self.stack = stack
        self.sems = {}
        self.tensors = 0
        sb, dram = self.sb, self.dram
        self.x_dram = dram("x_cm", [P, KB, NT])
        self.pj_dram = dram("proj_cm", [P, IN_W // P, NT])
        self.y_dram = dram("y_cm", [P, KB, NT])
        self.rpb_dram = dram("rpb_pad", [90, P])
        self.rpb_skew = dram("rpb_skew", [90, GRID_W, GRID_W])
        self.ident = sb(stack, "ident", [P, P])
        self.mean_d = sb(stack, "mean_d", [P, P])
        self.mean_h = sb(stack, "mean_h", [P, P])
        self.rot = sb(stack, "rot", [P, P])
        self.vecs = sb(stack, "vecs", [P, 96])
        self.b_ada = sb(stack, "b_ada", [P, DEPTH * MB])
        self.mods = sb(stack, "mods", [P, DEPTH, MB, 2])
        self.lb = sb(stack, "lb", [P, DEPTH, 4])
        self.omlb = sb(stack, "omlb", [P, DEPTH, 4])
        self.lbs = sb(stack, "lbs", [P, DEPTH, 4])
        self.fbias = sb(stack, "fbias", [P, 1])
        self.psum = stack.enter_context(nc.psum_tensor("psum", [P, 8, 512], F32))
        self.set_a = self.psum[:, 0:3].rearrange("p a b -> p (a b)")
        self.set_b = self.psum[:, 3:6].rearrange("p a b -> p (a b)")

    def sb(self, stack, name, shape, dt=F32):
        self.tensors += 1
        return stack.enter_context(self.nc.sbuf_tensor(f"{name}_{self.tensors}", shape, dt))

    def dram(self, name, shape):
        return self.nc.dram_tensor(name, shape, F32, kind="Internal").ap()

    def sem(self, name):
        if name not in self.sems:
            self.sems[name] = Sem(self.nc, self.stack, name)
        return self.sems[name]


V_C, V_LNG, V_LNB, V_LBL, V_QN, V_KN, V_HN = 0, 16, 48, 80, 88, 90, 92
V_ROWS = 94


def setup(k):
    nc, a = k.nc, k.a
    with ExitStack() as st:
        rows = k.sb(st, "vec_rows", [V_ROWS, P])
        ada = k.sb(st, "ada_rows", [DEPTH * MB, P])
        tmp = k.sb(st, "lb_tmp", [P, 8, 4])
        s_in, s_t, s_v, s_e, s_pad = k.sem("rows_loaded"), k.sem("rows_turned"), k.sem("vec_step"), k.sem("lb_exp"), k.sem("const_loaded")
        with nc.Block() as block:
            @block.sync
            def _(sp):
                for dst, src in (
                    (rows[V_C:V_C + 8], a["c"].rearrange("a (j p) -> (a j) p", p=P)),
                    (rows[V_C + 8:V_C + 16], a["c_ctx"].rearrange("(j p) -> j p", p=P)),
                    (rows[V_LNG:V_LNG + 32], a["ln_g"].rearrange("l w (j p) -> (l w j) p", p=P)),
                    (rows[V_LNB:V_LNB + 32], a["ln_b"].rearrange("l w (j p) -> (l w j) p", p=P)),
                    (rows[V_LBL:V_LBL + 8], a["hgrn_lb_logits"].rearrange("l d (j p) -> (l d j) p", p=P)),
                    (ada[:], a["b_ada"].rearrange("l (j p) -> (l j) p", p=P)),
                    (k.ident[:], a["c_ident"]), (k.mean_d[:], a["c_mean_d"]),
                    (k.mean_h[:], a["c_mean_h"]), (k.rot[:], a["c_rot"]),
                ):
                    sp.dma_start(dst, src).then_inc(s_in.h, 16)
                for row, name in ((V_QN, "gqa_q_norm"), (V_KN, "gqa_k_norm"), (V_HN, "hgrn_norm")):
                    for half in range(2):
                        sp.dma_start(rows[row:row + DEPTH, half * HD:(half + 1) * HD], a[name]).then_inc(s_in.h, 16)

            @block.tensor
            def _(pe):
                pe.wait_ge(s_in.h, 16 * 16)
                nc.tensor.transpose(k.psum[:, 0, 0:V_ROWS], rows[:], k.ident[0:V_ROWS, 0:V_ROWS])
                nc.tensor.transpose(k.psum[:, 1, 0:DEPTH * MB], ada[:], k.ident[0:DEPTH * MB, 0:DEPTH * MB]).then_inc(s_t.h, 1)

            @block.scalar
            def _(act):
                act.wait_ge(s_v.h, 3)
                nc.scalar.activation(tmp[:, 2:4], tmp[:, 0:2], ACT.Exp).then_inc(s_e.h, 1)
                act.wait_ge(s_v.h, 1)
                nc.scalar.activation(k.vecs[:, V_C:V_C + 16], k.vecs[:, V_C:V_C + 16], ACT.Silu).then_inc(s_e.h, 1)

            @block.vector
            def _(dve):
                n = [0]

                def step(ins):
                    ins.then_inc(s_v.h, 1)
                    n[0] += 1
                    dve.wait_ge(s_v.h, n[0])
                dve.wait_ge(s_t.h, 1)
                step(nc.vector.tensor_copy(k.vecs[:, 0:V_ROWS], k.psum[:, 0, 0:V_ROWS]))
                lg = k.vecs[:, V_LBL:V_LBL + 8].rearrange("p (l q) -> p l q", l=DEPTH)
                step(nc.vector.tensor_tensor(tmp[:, 4], lg[:, 0], lg[:, 1], ALU.max))
                step(nc.vector.tensor_tensor(tmp[:, 0:2], lg, tmp[:, 4:5].to_broadcast([P, 2, 4]), ALU.subtract))
                dve.wait_ge(s_e.h, 1)
                step(nc.vector.tensor_tensor(tmp[:, 4], tmp[:, 2], tmp[:, 3], ALU.add))
                step(nc.vector.reciprocal(tmp[:, 5], tmp[:, 4]))
                step(nc.vector.tensor_tensor(tmp[:, 0:2], tmp[:, 2:4], tmp[:, 5:6].to_broadcast([P, 2, 4]), ALU.mult))
                step(nc.vector.tensor_tensor(tmp[:, 6], tmp[:, 0], tmp[:, 1], ALU.add))
                step(nc.vector.tensor_tensor(k.lb[:, 0], tmp[:, 0], tmp[:, 0], ALU.subtract))
                step(nc.vector.tensor_tensor(k.lb[:, 1], tmp[:, 6], tmp[:, 0], ALU.subtract))
                step(nc.vector.tensor_scalar(k.lb[:], k.lb[:], 0.0, 1.0, ALU.max, ALU.min))
                step(nc.vector.tensor_scalar(k.omlb[:], k.lb[:], -1.0, 1.0, ALU.mult, ALU.add))
                step(nc.vector.tensor_scalar(k.lbs[:], k.lb[:], 2.0 ** LOG_SHIFT, None, ALU.mult))
                step(nc.vector.memset(k.fbias[:], -LOG_SHIFT * float(np.log(2.0))))
                step(nc.vector.tensor_copy(k.b_ada[:], k.psum[:, 1, 0:DEPTH * MB]))



def modulation(k, l):
    nc = k.nc
    W = 256
    n = N_MOD * D // W
    with ExitStack() as st:
        w = k.sb(st, "ada_w", [P, 2, KB, W])
        src = k.a["w_ada"][l].rearrange("(j p) n -> p j n", p=P)
        s_w = [k.sem(f"ada_w_loaded{s}") for s in range(2)]
        s_mm, s_v = k.sem("ada_mm"), k.sem("ada_out")
        sc = k.vecs[:, V_C:V_C + 16].rearrange("p (t j) -> p j t", t=2)
        credit = 2
        with nc.Block() as block:
            @block.sync
            def _(sp):
                def load(u, s, turn):
                    sp.wait_ge(s_mm.h, s_mm.at(1) + u)
                    sp.dma_start(w[:, s], src[:, :, bass.ds(u * W, W)]).then_inc(s_w[s].h, 16)
                in_pairs(sp, n, load)

            @block.tensor
            def _(pe):
                pe.sem_inc(s_mm.h, credit)

                def use(u, s, turn):
                    pe.wait_ge(s_w[s].h, s_w[s].at(16) + turn * 16)
                    for h in range(W // P):
                        o = k.psum[:, 0, bass.ds((u * (W // P) + h) * 2, 2)]
                        for j in range(KB):
                            ins = nc.tensor.matmul(o, w[:, s, j, h * P:(h + 1) * P], sc[:, j],
                                                   start=(j == 0), stop=(j == KB - 1))
                    ins.then_inc(s_mm.h, 1)
                in_pairs(pe, n, use)

            @block.vector
            def _(dve):
                dve.wait_ge(s_mm.h, s_mm.at(n + credit))
                nc.vector.tensor_tensor(
                    k.mods[:, l], k.psum[:, 0, 0:2 * MB].rearrange("p (j t) -> p j t", t=2),
                    k.b_ada[:, l * MB:(l + 1) * MB].unsqueeze(2).to_broadcast([P, MB, 2]), ALU.add).then_inc(s_v.h, 1)
                dve.wait_ge(s_v.h, s_v.at(1))
                for m in (1, 4):
                    nc.vector.tensor_scalar(k.mods[:, l, m * KB:(m + 1) * KB], k.mods[:, l, m * KB:(m + 1) * KB],
                                            1.0, None, ALU.add).then_inc(s_v.h, 1)
    for s in range(2):
        s_w[s].done(16 * (n // 2))
    s_mm.done(n + credit)
    s_v.done(3)


def turn_in(k, h_hi, h_lo):
    nc = k.nc
    with ExitStack() as st:
        rows = k.sb(st, "x_rows", [P, 2, D])
        xc = k.sb(st, "x_cm_tile", [P, 2, KB, P])
        hm = k.sb(st, "h_mod", [P, 2, KB, P])
        s_in = [k.sem(f"x_rows_loaded{s}") for s in range(2)]
        s_out = [k.sem(f"x_cm_stored{s}") for s in range(2)]
        s_t, s_x, s_m, s_hi, s_lo = (k.sem(x) for x in ("x_turned", "x_copied", "x_modulated", "x_hi", "x_lo"))
        with nc.Block() as block:
            @block.sync
            def _(sp):
                for t in range(TT):
                    if t >= 2:
                        sp.wait_ge(s_t.h, t - 1)
                    src = k.a["x"][0, t * P:(t + 1) * P] if t < SEQ // P else k.a["ctx"][0, t * P - SEQ:(t + 1) * P - SEQ]
                    sp.dma_start(rows[:, t % 2], src).then_inc(s_in[t % 2].h, 16)
                    if t >= 1:
                        sp.wait_ge(s_x.h, t)
                        sp.dma_start(k.x_dram[:, :, (t - 1) * P:t * P], xc[:, (t - 1) % 2]).then_inc(s_out[(t - 1) % 2].h, 16)
                sp.wait_ge(s_x.h, TT)
                sp.dma_start(k.x_dram[:, :, (TT - 1) * P:TT * P], xc[:, (TT - 1) % 2]).then_inc(s_out[(TT - 1) % 2].h, 16)
                for s in range(2):
                    sp.wait_ge(s_out[s].h, 16 * TT // 2)

            @block.tensor
            def _(pe):
                for t in range(TT):
                    pe.wait_ge(s_in[t % 2].h, 16 * (t // 2 + 1))
                    if t >= 2:
                        pe.wait_ge(s_x.h, t - 1)
                    for j in range(KB):
                        ins = nc.tensor.transpose(k.psum[:, 2 * (t % 2) + j // 4, (j % 4) * P:(j % 4 + 1) * P],
                                                  rows[:, t % 2, j * P:(j + 1) * P], k.ident[:])
                    ins.then_inc(s_t.h, 1)

            @block.vector
            def _(dve):
                for t in range(TT):
                    c = 0 if t < SEQ // P else 1
                    dve.wait_ge(s_t.h, t + 1)
                    if t >= 2:
                        dve.wait_ge(s_out[t % 2].h, 16 * (t // 2))
                    nc.vector.tensor_copy(xc[:, t % 2].rearrange("p j q -> p (j q)"),
                                          k.psum[:, 2 * (t % 2):2 * (t % 2) + 2].rearrange("p a b -> p (a b)")).then_inc(s_x.h, 1)
                    dve.wait_ge(s_x.h, t + 1)
                    if t >= 2:
                        dve.wait_ge(s_lo.h, t - 1)
                    for j in range(KB):
                        ins = nc.vector.tensor_scalar(hm[:, t % 2, j], xc[:, t % 2, j], k.mods[:, 0, KB + j, c:c + 1],
                                                      k.mods[:, 0, j, c:c + 1], ALU.mult, ALU.add)
                    ins.then_inc(s_m.h, 1)
                    dve.wait_ge(s_hi.h, t + 1)
                    nc.vector.tensor_tensor(h_lo[:, :, t * P:(t + 1) * P], hm[:, t % 2],
                                            h_hi[:, :, t * P:(t + 1) * P].bitcast(F32), ALU.subtract).then_inc(s_lo.h, 1)

            @block.scalar
            def _(act):
                for t in range(TT):
                    act.wait_ge(s_m.h, t + 1)
                    nc.scalar.copy(h_hi[:, :, t * P:(t + 1) * P], hm[:, t % 2]).then_inc(s_hi.h, 1)


def three_products(nc, out, chunks, w_hi, w_lo, h_hi, h_lo, start, stop):
    for n, (w, h) in enumerate(((w_hi, h_hi), (w_hi, h_lo), (w_lo, h_hi))):
        for t0, tn in chunks:
            ins = nc.tensor.matmul(out[:, t0:t0 + tn], w, h[:, t0:t0 + tn],
                                   start=start and n == 0, stop=stop and n == 2)
    return ins


def linear(k, src, units, tokens, h_hi, h_lo, y):
    nc = k.nc
    chunks = token_chunks(tokens)
    with ExitStack() as st:
        raw = k.sb(st, "w_raw", [P, 2, D])
        w_hi = k.sb(st, "w_hi", [P, 2, D], F32R)
        w_lo = k.sb(st, "w_lo", [P, 2, D], F32R)
        s_w = [k.sem(f"w_loaded{s}") for s in range(2)]
        s_hi, s_lo, s_mm, s_ev = (k.sem(x) for x in ("w_hi", "w_lo", "lin_products", "lin_out"))
        sets = (k.set_a, k.set_b)
        stage = k.sb(st, "lin_stage", [P, 2, NT]) if y is None else None
        s_st = [k.sem(f"lin_stored{s}") for s in range(2)]
        with nc.Block() as block:
            if y is None:
                @block.gpsimd
                def _(pool):
                    def store(u, s, turn):
                        pool.wait_ge(s_ev.h, s_ev.at(3) + u)
                        pool.dma_start(k.pj_dram[:, bass.ds(u, 1), 0:tokens].rearrange("p a t -> p (a t)"),
                                       stage[:, s, 0:tokens]).then_inc(s_st[s].h, 16)
                    in_pairs(pool, units, store)
                    for s in range(2):
                        pool.wait_ge(s_st[s].h, s_st[s].at(16 * ((units + 1 - s) // 2)))

            @block.sync
            def _(sp):
                def load(u, s, turn):
                    sp.wait_ge(s_lo.h, s_lo.at(1) + u)
                    sp.dma_start(raw[:, s].rearrange("p (j q) -> p j q", j=KB), src(u)).then_inc(s_w[s].h, 16)
                in_pairs(sp, units, load)

            @block.scalar
            def _(act):
                def hi(u, s, turn):
                    act.wait_ge(s_w[s].h, s_w[s].at(16) + turn * 16)
                    act.wait_ge(s_mm.h, s_mm.at(1) + u)
                    nc.scalar.copy(w_hi[:, s], raw[:, s]).then_inc(s_hi.h, 1)
                in_pairs(act, units, hi)

            @block.vector
            def _(dve):
                dve.sem_inc(s_lo.h, 2)
                dve.sem_inc(s_ev.h, 2)

                def lo(u, s):
                    dve.wait_ge(s_hi.h, s_hi.at(1) + u)
                    nc.vector.tensor_tensor(w_lo[:, s], raw[:, s], w_hi[:, s].bitcast(F32), ALU.subtract).then_inc(s_lo.h, 1)

                def evac(u, s):
                    dve.wait_ge(s_mm.h, s_mm.at(3) + u)
                    if y is None:
                        if not (isinstance(u, int) and u < 2):
                            dve.wait_ge(s_st[s].h, s_st[s].at(-8 * s) + u * 8)
                        dst = stage[:, s, 0:tokens]
                    else:
                        dst = y[:, bass.ds(u, 1), 0:tokens].rearrange("p a t -> p (a t)")
                    nc.vector.tensor_copy(dst, sets[s][:, 0:tokens]).then_inc(s_ev.h, 1)
                lo(0, 0)
                lo(1, 1)
                for s in range(2):
                    evac(s, s)
                    lo(s + 2, s)
                with dve.Fori(1, (units - 2) // 2) as i:
                    for s in range(2):
                        evac(i * 2 + s, s)
                        lo(i * 2 + s + 2, s)
                for u in range((units - 2) // 2 * 2, units):
                    evac(u, u % 2)
                    if u + 2 < units:
                        lo(u + 2, u % 2)

            @block.tensor
            def _(pe):
                pe.sem_inc(s_mm.h, 2)

                def unit(u, s, turn):
                    pe.wait_ge(s_lo.h, s_lo.at(3) + u)
                    pe.wait_ge(s_ev.h, s_ev.at(1) + u)
                    for j in range(KB):
                        cols = slice(j * P, (j + 1) * P)
                        ins = three_products(nc, sets[s], chunks, w_hi[:, s, cols], w_lo[:, s, cols],
                                             h_hi[:, j], h_lo[:, j], j == 0, j == KB - 1)
                    ins.then_inc(s_mm.h, 1)
                in_pairs(pe, units, unit)
    for s in range(2):
        s_w[s].done(16 * ((units + 1 - s) // 2))
        if y is None:
            s_st[s].done(16 * ((units + 1 - s) // 2))
    s_hi.done(units)
    for x in (s_lo, s_mm, s_ev):
        x.done(units + 2)


def residual_norm(k, l, sub, tokens, y, h_hi, h_lo, last):
    nc = k.nc
    chunks = token_chunks(tokens)
    n_c = len(chunks)
    gate = k.mods[:, l, (2 + 3 * sub) * KB:]
    if not last:
        l2, m2 = (l, 3) if sub == 0 else (l + 1, 0)
        shift, scale = k.mods[:, l2, m2 * KB:], k.mods[:, l2, (m2 + 1) * KB:]
    vec = V_LNG + (2 * l + sub) * KB
    g_ln, b_ln = k.vecs[:, vec:], k.vecs[:, vec + V_LNB - V_LNG:]
    with ExitStack() as st:
        xa = k.sb(st, "ln_x", [P, KB, 512])
        sq = k.sb(st, "ln_sq", [P, 2, 512])
        rs = k.sb(st, "ln_rstd", [P, 512])
        hm = k.sb(st, "ln_h", [P, 2, 512])
        rows_out = k.sb(st, "out_rows", [P, 2, D])
        s_st = [k.sem(f"out_stored{s}") for s in range(2)]
        s_in, s_out = k.sem("ln_loaded"), k.sem("ln_stored")
        names = ("ln_alpha", "ln_z", "ln_mean", "ln_centred", "ln_square", "ln_var", "ln_var_eps", "ln_root", "ln_rstd", "ln_scaled",
                 "ln_new_x", "ln_modulated", "ln_hi", "ln_lo", "ln_turned", "ln_rows")
        (s_al, s_z, s_mu, s_zc, s_sq, s_var, s_ve, s_root, s_rs, s_sc, s_x, s_m, s_hi, s_lo, s_t, s_r) = (k.sem(x) for x in names)
        with nc.Block() as block:
            @block.sync
            def _(sp):
                for c, (t0, tn) in enumerate(chunks):
                    if c:
                        if last:
                            sp.wait_ge(s_t.h, 4 * c)
                        else:
                            sp.wait_ge(s_out.h, s_out.at(16 * c))
                            sp.wait_ge(s_m.h, s_m.at(KB * c))
                    sp.dma_start(xa[:, :, 0:tn], k.x_dram[:, :, t0:t0 + tn]).then_inc(s_in.h, 16)
                    if not last:
                        sp.wait_ge(s_x.h, s_x.at(KB * (c + 1)))
                        sp.dma_start(k.x_dram[:, :, t0:t0 + tn], xa[:, :, 0:tn]).then_inc(s_out.h, 16)
                    else:
                        for t in range(tn // P):
                            g = c * 4 + t
                            sp.wait_ge(s_r.h, s_r.at(g + 1))
                            sp.dma_start(k.out[0, t0 + t * P:t0 + (t + 1) * P], rows_out[:, g % 2]).then_inc(s_st[g % 2].h, 16)
                if last:
                    for s in range(2):
                        sp.wait_ge(s_st[s].h, 16 * SEQ // P // 2)
                else:
                    sp.wait_ge(s_out.h, s_out.at(16 * n_c))

            @block.scalar
            def _(act):
                for c, (t0, tn) in enumerate(chunks):
                    act.wait_ge(s_in.h, s_in.at(16 * (c + 1)))
                    for j in range(KB):
                        nc.scalar.mul(xa[:, j, 0:tn], xa[:, j, 0:tn], ALPHA).then_inc(s_al.h, 1)
                    for j in range(KB):
                        n = c * KB + j
                        act.wait_ge(s_zc.h, s_zc.at(n + 1))
                        if n >= 2:
                            act.wait_ge(s_var.h, s_var.at(n - 1))
                        nc.scalar.activation(sq[:, j % 2, 0:tn], y[:, j, t0:t0 + tn], ACT.Square).then_inc(s_sq.h, 1)
                    act.wait_ge(s_ve.h, s_ve.at(c + 1))
                    nc.scalar.activation(rs[:, 0:tn], rs[:, 0:tn], ACT.Sqrt).then_inc(s_root.h, 1)
                    for j in range(KB):
                        n = c * KB + j
                        act.wait_ge(s_sc.h, s_sc.at(n + 1))
                        nc.scalar.activation(xa[:, j, 0:tn], y[:, j, t0:t0 + tn], ACT.Identity,
                                             bias=b_ln[:, j:j + 1], scale=g_ln[:, j:j + 1]).then_inc(s_x.h, 1)
                    if not last:
                        for j in range(KB):
                            act.wait_ge(s_m.h, s_m.at(c * KB + j + 1))
                            nc.scalar.copy(h_hi[:, j, t0:t0 + tn], hm[:, j % 2, 0:tn]).then_inc(s_hi.h, 1)

            @block.tensor
            def _(pe):
                for c, (t0, tn) in enumerate(chunks):
                    for j in range(KB):
                        pe.wait_ge(s_z.h, s_z.at(c * KB + j + 1))
                        ins = nc.tensor.matmul(k.psum[:, 0, 0:tn], k.mean_d[:], y[:, j, t0:t0 + tn], start=j == 0, stop=j == KB - 1)
                    ins.then_inc(s_mu.h, 1)
                    for j in range(KB):
                        pe.wait_ge(s_sq.h, s_sq.at(c * KB + j + 1))
                        nc.tensor.matmul(k.psum[:, 1, 0:tn], k.mean_d[:], sq[:, j % 2, 0:tn], start=j == 0, stop=j == KB - 1).then_inc(s_var.h, 1)
                    if last:
                        pe.wait_ge(s_x.h, s_x.at(KB * (c + 1)))
                        for t in range(tn // P):
                            g = c * 4 + t
                            if g >= 2:
                                pe.wait_ge(s_r.h, s_r.at(g - 1))
                            for j in range(KB):
                                ins = nc.tensor.transpose(k.psum[:, 2 + 2 * (g % 2) + j // 4, (j % 4) * P:(j % 4 + 1) * P],
                                                          xa[:, j, t * P:(t + 1) * P], k.ident[:])
                            ins.then_inc(s_t.h, 1)

            @block.vector
            def _(dve):
                for c, (t0, tn) in enumerate(chunks):
                    m = 0 if t0 < SEQ else 1
                    for j in range(KB):
                        dve.wait_ge(s_al.h, s_al.at(c * KB + j + 1))
                        nc.vector.scalar_tensor_tensor(out=y[:, j, t0:t0 + tn], in0=y[:, j, t0:t0 + tn], scalar=gate[:, j, m:m + 1],
                                                       in1=xa[:, j, 0:tn], op0=ALU.mult, op1=ALU.add).then_inc(s_z.h, 1)
                    dve.wait_ge(s_mu.h, s_mu.at(c + 1))
                    for j in range(KB):
                        nc.vector.tensor_tensor(y[:, j, t0:t0 + tn], y[:, j, t0:t0 + tn], k.psum[:, 0, 0:tn], ALU.subtract).then_inc(s_zc.h, 1)
                    dve.wait_ge(s_var.h, s_var.at(KB * (c + 1)))
                    if c:
                        dve.wait_ge(s_sc.h, s_sc.at(KB * c))
                    nc.vector.tensor_scalar(rs[:, 0:tn], k.psum[:, 1, 0:tn], EPS, None, ALU.add).then_inc(s_ve.h, 1)
                    dve.wait_ge(s_root.h, s_root.at(c + 1))
                    nc.vector.reciprocal(rs[:, 0:tn], rs[:, 0:tn]).then_inc(s_rs.h, 1)
                    dve.wait_ge(s_rs.h, s_rs.at(c + 1))
                    for j in range(KB):
                        nc.vector.tensor_tensor(y[:, j, t0:t0 + tn], y[:, j, t0:t0 + tn], rs[:, 0:tn], ALU.mult).then_inc(s_sc.h, 1)
                    if last:
                        for t in range(tn // P):
                            g = c * 4 + t
                            dve.wait_ge(s_t.h, s_t.at(g + 1))
                            if g >= 2:
                                dve.wait_ge(s_st[g % 2].h, 16 * (g // 2))
                            nc.vector.tensor_copy(rows_out[:, g % 2], k.psum[:, 2 + 2 * (g % 2):4 + 2 * (g % 2)].rearrange("p a b -> p (a b)")).then_inc(s_r.h, 1)
                        continue
                    for j in range(KB):
                        n = c * KB + j
                        dve.wait_ge(s_x.h, s_x.at(n + 1))
                        if n >= 2:
                            dve.wait_ge(s_lo.h, s_lo.at(n - 1))
                        nc.vector.tensor_scalar(hm[:, j % 2, 0:tn], xa[:, j, 0:tn], scale[:, j, m:m + 1], shift[:, j, m:m + 1],
                                                ALU.mult, ALU.add).then_inc(s_m.h, 1)
                        dve.wait_ge(s_hi.h, s_hi.at(n + 1))
                        nc.vector.tensor_tensor(h_lo[:, j, t0:t0 + tn], hm[:, j % 2, 0:tn], h_hi[:, j, t0:t0 + tn].bitcast(F32), ALU.subtract).then_inc(s_lo.h, 1)
    n = n_c * KB
    for x in (s_al, s_z, s_zc, s_sq, s_var, s_sc, s_x):
        x.done(n)
    for x in (s_mu, s_ve, s_root, s_rs):
        x.done(n_c)
    s_in.done(16 * n_c)
    if not last:
        s_out.done(16 * n_c)
        for x in (s_m, s_hi, s_lo):
            x.done(n)


def swiglu(k, l, tokens, h_hi, h_lo, y):
    nc = k.nc
    chunks = token_chunks(tokens)
    w1 = k.a["w_ffn_in"][l].rearrange("(j p) n -> p j n", p=P)
    w2 = k.a["w_ffn_out"][l]
    with ExitStack() as st:
        raw = k.sb(st, "f_raw", [P, 3, D])
        w_hi = k.sb(st, "f_whi", [P, 3, D], F32R)
        w_lo = k.sb(st, "f_wlo", [P, 3, D], F32R)
        act_g = k.sb(st, "f_silu", [P, NT])
        hid = k.sb(st, "f_hid", [P, NT])
        u_hi = k.sb(st, "f_uhi", [P, 2, NT], F32R)
        u_lo = k.sb(st, "f_ulo", [P, 2, NT], F32R)
        kinds = ("gate", "up", "down")
        s_w = [k.sem(f"{x}_loaded") for x in kinds]
        s_hi = [k.sem(f"{x}_hi") for x in kinds]
        s_lo = [k.sem(f"{x}_lo") for x in kinds]
        s_mm = [k.sem(f"{x}_products") for x in kinds]
        s_silu, s_h, s_uhi, s_ulo, s_acc, s_out = (k.sem(x) for x in ("silu_done", "hidden_done", "hidden_hi", "hidden_lo", "acc_done", "down_out"))

        def sets(q):
            return (k.set_a, k.set_b)[q % 2][:, 0:tokens]
        with nc.Block() as block:
            @block.gpsimd
            def _(pool):
                for j in range(KB):
                    nc.gpsimd.memset(y[:, j, 0:tokens], 0.0).then_inc(k.sem("y_zero").h, 1)

            @block.sync
            def _(sp):
                def loads(j, first=False):
                    for n in range(3):
                        if not first:
                            sp.wait_ge(s_lo[n].h, s_lo[n].at(0) + j)
                        if n < 2:
                            cols = bass.ds(j * P + n * FFN, P)
                            sp.dma_start(raw[:, n].rearrange("p (j q) -> p j q", j=KB), w1[:, :, cols]).then_inc(s_w[n].h, 16)
                        else:
                            sp.dma_start(raw[:, n], w2[bass.ds(j * P, P), :]).then_inc(s_w[n].h, 16)
                loads(0, True)
                with sp.Fori(1, HB) as j:
                    loads(j)

            @block.scalar
            def _(act):
                def hi(n, j, first=False):
                    act.wait_ge(s_w[n].h, s_w[n].at(16) + j * 16)
                    if not first and n < 2:
                        act.wait_ge(s_mm[n].h, s_mm[n].at(0) + j)
                    elif not first:
                        act.wait_ge(s_out.h, s_out.at(0) + j * KB)
                    nc.scalar.copy(w_hi[:, n], raw[:, n]).then_inc(s_hi[n].h, 1)

                def block_j(j, q, first=False, more=True):
                    act.wait_ge(s_mm[0].h, s_mm[0].at(1) + j)
                    if not first:
                        act.wait_ge(s_h.h, s_h.at(0) + j)
                    nc.scalar.activation(act_g[:, 0:tokens], sets(0), ACT.Silu).then_inc(s_silu.h, 1)
                    if more:
                        hi(0, j + 1)
                        hi(1, j + 1)
                    act.wait_ge(s_h.h, s_h.at(1) + j)
                    if not (isinstance(j, int) and j < 2):
                        act.wait_ge(s_out.h, s_out.at(-KB) + j * KB)
                    nc.scalar.copy(u_hi[:, q, 0:tokens], hid[:, 0:tokens]).then_inc(s_uhi.h, 1)
                    hi(2, j, first)
                for n in range(2):
                    hi(n, 0, True)
                block_j(0, 0, True)
                block_j(1, 1)
                with act.Fori(1, HB // 2 - 1) as i:
                    for q in range(2):
                        block_j(i * 2 + q, q)
                block_j(HB - 2, 0)
                block_j(HB - 1, 1, more=False)

            @block.vector
            def _(dve):
                def lo(n, j):
                    dve.wait_ge(s_hi[n].h, s_hi[n].at(1) + j)
                    nc.vector.tensor_tensor(w_lo[:, n], raw[:, n], w_hi[:, n].bitcast(F32), ALU.subtract).then_inc(s_lo[n].h, 1)

                def gather(j):
                    for o in range(KB):
                        dve.wait_ge(s_out.h, s_out.at(1 + o) + j * KB)
                        nc.vector.tensor_tensor(y[:, o, 0:tokens], y[:, o, 0:tokens], sets(o), ALU.add).then_inc(s_acc.h, 1)

                def block_j(j, q, more=True):
                    if more:
                        lo(0, j + 1)
                    dve.wait_ge(s_silu.h, s_silu.at(1) + j)
                    dve.wait_ge(s_mm[1].h, s_mm[1].at(1) + j)
                    if not (isinstance(j, int) and j < 1):
                        dve.wait_ge(s_ulo.h, s_ulo.at(0) + j)
                    nc.vector.tensor_tensor(hid[:, 0:tokens], act_g[:, 0:tokens], sets(1), ALU.mult).then_inc(s_h.h, 1)
                    if more:
                        lo(1, j + 1)
                    dve.wait_ge(s_uhi.h, s_uhi.at(1) + j)
                    nc.vector.tensor_tensor(u_lo[:, q, 0:tokens], hid[:, 0:tokens], u_hi[:, q, 0:tokens].bitcast(F32), ALU.subtract).then_inc(s_ulo.h, 1)
                    if not (isinstance(j, int) and j < 1):
                        gather(j - 1)
                    lo(2, j)
                dve.wait_ge(k.sem("y_zero").h, k.sem("y_zero").at(KB))
                for n in range(2):
                    lo(n, 0)
                block_j(0, 0)
                block_j(1, 1)
                with dve.Fori(1, HB // 2 - 1) as i:
                    for q in range(2):
                        block_j(i * 2 + q, q)
                block_j(HB - 2, 0)
                block_j(HB - 1, 1, more=False)
                gather(HB - 1)

            @block.tensor
            def _(pe):
                def up(n, j):
                    pe.wait_ge(s_lo[n].h, s_lo[n].at(1) + j)
                    for b in range(KB):
                        cols = slice(b * P, (b + 1) * P)
                        ins = three_products(nc, sets(n), chunks, w_hi[:, n, cols], w_lo[:, n, cols], h_hi[:, b], h_lo[:, b], b == 0, b == KB - 1)
                    ins.then_inc(s_mm[n].h, 1)

                def down(j, q, last=False):
                    pe.wait_ge(s_lo[2].h, s_lo[2].at(1) + j)
                    pe.wait_ge(s_ulo.h, s_ulo.at(1) + j)
                    for o in range(KB):
                        if o == 0 and not last:
                            pe.wait_ge(s_silu.h, s_silu.at(2) + j)
                        elif o == 1 and not last:
                            pe.wait_ge(s_h.h, s_h.at(2) + j)
                        else:
                            pe.wait_ge(s_acc.h, s_acc.at(o - 1) + j * KB)
                        cols = slice(o * P, (o + 1) * P)
                        ins = three_products(nc, sets(o), chunks, w_hi[:, 2, cols], w_lo[:, 2, cols], u_hi[:, q], u_lo[:, q], True, True)
                        ins.then_inc(s_out.h, 1)

                def block_j(j, q):
                    if isinstance(j, int) and j == 1:
                        pe.wait_ge(s_silu.h, s_silu.at(1))
                    if not (isinstance(j, int) and j < 2):
                        pe.wait_ge(s_acc.h, s_acc.at(-2 * KB + KB - 1) + j * KB)
                    up(0, j)
                    if isinstance(j, int) and j == 1:
                        pe.wait_ge(s_h.h, s_h.at(1))
                    if not (isinstance(j, int) and j < 2):
                        pe.wait_ge(s_acc.h, s_acc.at(-KB) + j * KB)
                    up(1, j)
                    if not (isinstance(j, int) and j < 1):
                        down(j - 1, 1 - q)
                block_j(0, 0)
                block_j(1, 1)
                with pe.Fori(1, HB // 2) as i:
                    for q in range(2):
                        block_j(i * 2 + q, q)
                down(HB - 1, (HB - 1) % 2, last=True)
    for n in range(3):
        s_w[n].done(16 * HB)
        for x in (s_hi, s_lo, s_mm)[:3 if n < 2 else 2]:
            x[n].done(HB)
    for x in (s_silu, s_h, s_uhi, s_ulo):
        x.done(HB)
    for x in (s_acc, s_out):
        x.done(HB * KB)
    k.sem("y_zero").done(KB)



def window_start(pair):
    lo = min(max(2 * pair - NA_KH // 2, 0), ROWS - NA_KH)
    hi = min(max(2 * pair + 1 - NA_KH // 2, 0), ROWS - NA_KH)
    return lo, hi != lo


def gqa_tiles(ctx):
    tiles = [(q, [(0, 0, 512), (512, 512, 512), (1024, 1024, 256)], [(t * P, P, t) for t in range(TT)], None)
             for q in range(SEQ // P)]
    return tiles + (ctx_tiles() if ctx else [])


def ctx_tiles():
    return [(q, [(0, SEQ, CTX)], [(i * P, P, SEQ // P + i) for i in range(CTX // P)], None)
            for q in range(SEQ // P, TT)]


def na_tiles(ctx):
    tiles = []
    for pair in range(ROWS // 2):
        k0, differ = window_start(pair)
        local = (NA_KH + differ) * GRID_W
        pieces = [(0, k0 * GRID_W, 512)] + [(512, (k0 + NA_KH) * GRID_W, GRID_W)] * differ + [(local, SEQ, CTX)]
        keys = [(i * P, P, k0 // 2 + i) for i in range(4)]
        keys += [(local + i * P, P, SEQ // P + i) for i in range(CTX // P)] + [(512, GRID_W, k0 // 2 + 4)] * differ
        slot = SLOTS if differ else k0 - 2 * pair + NA_KH - 2
        tiles.append((pair, pieces, keys, (local, slot)))
    return tiles + (ctx_tiles() if ctx else [])


def attention(k, tiles, q_block, k_rows, v_all, bias, y_block):
    nc = k.nc
    work = [(half, t) for half in range(2) for t in tiles]
    n_t = len(work)
    groups = []
    for n, (_, t) in enumerate(work):
        groups += [(n, t[2][i:i + 4]) for i in range(0, len(t[2]), 4)]
    n_g = len(groups)
    assert n_t % 2 == 0 and n_g % 2 == 0
    of_tile = [[x for x in range(n_g) if groups[x][0] == n] for n in range(n_t)]
    n_q = max(t[0] for t in tiles) + 1
    copier = ["act", "act" if bias is not None else "dve"]
    stage_at = 1
    with ExitStack() as st:
        raw = k.sb(st, "att_raw", [P, 2, 2, NT])
        qst = k.sb(st, "att_q", [P, 2, NT], F32R)
        khi = k.sb(st, "att_khi", [P, 2, NT], F32R)
        klo = k.sb(st, "att_klo", [P, 2, NT], F32R)
        vs = k.sb(st, "att_v", [P, 2, TT, HD])
        pr = k.sb(st, "att_p", [P, 2, NT])
        pt = k.sb(st, "att_pt", [P, 2, 512])
        o_n = k.sb(st, "att_o", [P, 3, n_q, P])
        nb = k.sb(st, "att_negmax", [P, 2])
        rsum = k.sb(st, "att_sum", [P, 2])
        rinv = k.sb(st, "att_inv", [P, 2])
        yb = k.sb(st, "att_y", [P, 2, NT])
        names = ("scores", "score_bias", "score_negmax", "probs", "p_turned", "pv", "sum_inv", "o_done", "y_turned", "y_copied")
        s_s, s_b, s_nb, s_p, s_t, s_pv, s_ri, s_o, s_yt, s_y = (k.sem(x) for x in names)
        s_pt = [k.sem(f"pt_copied{s}") for s in range(2)]
        s_st = [k.sem(f"y_stored{s}") for s in range(2)]
        s_raw = [k.sem(f"head_loaded{s}") for s in range(2)]
        s_hi = [k.sem(f"head_hi{s}") for s in range(2)]
        s_lo = [k.sem(f"head_lo{s}") for s in range(2)]
        s_v = [k.sem(f"head_v{s}") for s in range(2)]

        def score(slot):
            return (k.set_a, k.set_b)[slot]

        def width(t):
            return t[1][-1][0] + t[1][-1][2]
        n_bias = sum(t[3] is not None for _, t in work)
        before = [sum(t[3] is not None for _, t in work[:n]) for n in range(n_t)]
        o_cols = slice(1280 + HD, 1280 + 2 * HD)

        def blocks(e, body):
            with e.Fori(0, 2) as b:
                body(b, False)
            body(2, True)

        def staging(b, n, last, stage):
            if n == stage_at:
                stage(b, 1)
            if n == n_t // 2 + stage_at and not last:
                stage(b + 1, 0)

        with nc.Block() as block:
            @block.sync
            def _(sp):
                def load(b, half):
                    sp.wait_ge(s_lo[half].h, s_lo[half].at(1) + b)
                    k_p, k_b = k_rows(b, half)
                    for part in range(2):
                        rows = slice(part * HD, (part + 1) * HD)
                        sp.dma_start(raw[rows, half, 0], k.pj_dram[half * HD:(half + 1) * HD, bass.ds(q_block + b, 1)]
                                     .rearrange("p a t -> p (a t)")).then_inc(s_raw[half].h, 16)
                        sp.dma_start(raw[rows, half, 1], k.pj_dram[bass.ds(k_p, HD), bass.ds(k_b, 1)]
                                     .rearrange("p a t -> p (a t)")).then_inc(s_raw[half].h, 16)
                with sp.Fori(0, 3) as b:
                    load(b, 0)
                    load(b, 1)
                for b in range(3):
                    sp.wait_ge(s_y.h, s_y.at(b + 1))
                    sp.dma_start(k.y_dram[:, y_block + b, 0:n_q * P], yb[:, b % 2, 0:n_q * P]).then_inc(s_st[b % 2].h, 16)
                sp.wait_ge(s_st[0].h, s_st[0].at(32))
                sp.wait_ge(s_st[1].h, s_st[1].at(16))

            @block.gpsimd
            def _(pool):
                def stage(b, half):
                    if not isinstance(b, int):
                        pool.wait_ge(s_o.h, s_o.at(2 + (half + 1) * n_t // 2 - n_t) + b * n_t)
                    nc.gpsimd.tensor_copy(vs[:, half], v_all[:, :, bass.ds(b, 1), half * HD:(half + 1) * HD]
                                          .rearrange("p t a d -> p t (a d)")).then_inc(s_v[half].h, 1)
                stage(0, 0)
                stage(0, 1)
                with pool.Fori(1, 3) as b:
                    stage(b, 0)
                    stage(b, 1)

            @block.tensor
            def _(pe):
                pe.sem_inc(s_s.h, n_t)
                pe.sem_inc(s_pv.h, 2)
                pe.sem_inc(s_t.h, n_g)

                def scores(b, n):
                    half, t = work[n]
                    if n % (n_t // 2) == 0:
                        pe.wait_ge(s_lo[half].h, s_lo[half].at(2) + b)
                    pe.wait_ge(s_o.h, s_o.at(1 + n) + b * n_t)
                    q = qst[:, half, t[0] * P:(t[0] + 1) * P]
                    for col, tok, cnt in t[1]:
                        nc.tensor.matmul(score(n % 2)[:, col:col + cnt], q, khi[:, half, tok:tok + cnt], start=True, stop=False)
                        ins = nc.tensor.matmul(score(n % 2)[:, col:col + cnt], q, klo[:, half, tok:tok + cnt], start=False, stop=True)
                    ins.then_inc(s_s.h, 1)

                def turn(b, x):
                    n, keys = groups[x]
                    if x == of_tile[n][0]:
                        pe.wait_ge(s_p.h, s_p.at(3 + n) + b * n_t)
                    pe.wait_ge(s_pt[x % 2].h, s_pt[x % 2].at(1 + x // 2) + b * (n_g // 2))
                    for i, (col, rows, _) in enumerate(keys):
                        ins = nc.tensor.transpose(k.psum[0:rows, 6 + x % 2, i * P:(i + 1) * P], pr[:, n % 2, col:col + rows], k.ident[:])
                    ins.then_inc(s_t.h, 1)

                def product(b, x):
                    n, keys = groups[x]
                    half = work[n][0]
                    if x == of_tile[half * n_t // 2][0]:
                        pe.wait_ge(s_v[half].h, s_v[half].at(1) + b)
                    pe.wait_ge(s_pt[x % 2].h, s_pt[x % 2].at(2 + x // 2) + b * (n_g // 2))
                    for i, (_, rows, tile) in enumerate(keys):
                        ins = nc.tensor.matmul(score(n % 2)[:, o_cols], pt[0:rows, x % 2, i * P:(i + 1) * P], vs[0:rows, half, tile],
                                               start=x == of_tile[n][0] and i == 0, stop=x == of_tile[n][-1] and i == len(keys) - 1)
                    ins.then_inc(s_pv.h, 1)

                def body(b, last):
                    for n in range(n_t):
                        xs = of_tile[n]
                        turn(b, xs[0])
                        if n + 1 < n_t:
                            scores(b, n + 1)
                        elif not last:
                            scores(b + 1, 0)
                        for x in xs[1:]:
                            turn(b, x)
                            product(b, x - 1)
                        product(b, xs[-1])
                scores(0, 0)
                blocks(pe, body)
                pe.wait_ge(s_o.h, s_o.at(2 + 3 * n_t))
                for b in range(3):
                    if b:
                        pe.wait_ge(s_y.h, s_y.at(b))
                    for q in range(n_q):
                        ins = nc.tensor.transpose(score(0)[:, q * P:(q + 1) * P], o_n[:, b, q], k.ident[:])
                    ins.then_inc(s_yt.h, 1)

            def copy(e, op, b, x):
                keys = groups[x][1]
                e.wait_ge(s_t.h, s_t.at(1 + n_g + x) + b * n_g)
                e.wait_ge(s_pv.h, s_pv.at(1 + x) + b * n_g)
                for c0, c1, rows in spans(keys):
                    ins = op(pt[0:rows, x % 2, c0:c1], k.psum[0:rows, 6 + x % 2, c0:c1])
                ins.then_inc(s_pt[x % 2].h, 1)

            @block.scalar
            def _(act):
                act.sem_inc(s_pt[0].h, 1)
                act.sem_inc(s_p.h, 2)

                def stage(b, half):
                    act.wait_ge(s_raw[half].h, s_raw[half].at(64) + b * 64)
                    act.wait_ge(s_s.h, s_s.at((half + 1) * n_t // 2) + b * n_t)
                    nc.scalar.mul(qst[:, half], raw[:, half, 0], SCALE)
                    nc.scalar.copy(khi[:, half], raw[:, half, 1]).then_inc(s_hi[half].h, 1)

                def probs(b, n):
                    t = work[n][1]
                    act.wait_ge(s_nb.h, s_nb.at(1 + n) + b * n_t)
                    if t[3] is None:
                        prev = of_tile[n - 2][-1] - (n_g if n < 2 else 0)
                        act.wait_ge(s_t.h, s_t.at(1 + prev + n_g) + b * n_g)
                    src = pr[:, n % 2, 0:width(t)] if t[3] else score(n % 2)[:, 0:width(t)]
                    nc.scalar.activation(pr[:, n % 2, 0:width(t)], src, ACT.Exp, bias=nb[:, n % 2:n % 2 + 1],
                                         accum_out=rsum[:, n % 2:n % 2 + 1]).then_inc(s_p.h, 1)

                def body(b, last):
                    for n in range(n_t):
                        xs = of_tile[n]
                        if copier[xs[0] % 2] == "act":
                            copy(act, nc.scalar.copy, b, xs[0])
                        if n + 1 < n_t:
                            probs(b, n + 1)
                        elif not last:
                            probs(b + 1, 0)
                        for x in xs[1:]:
                            if copier[x % 2] == "act":
                                copy(act, nc.scalar.copy, b, x)
                        staging(b, n, last, stage)
                stage(0, 0)
                probs(0, 0)
                blocks(act, body)

            @block.vector
            def _(dve):
                dve.sem_inc(s_pt[1].h, 1)
                dve.sem_inc(s_o.h, 2)
                for s in range(2):
                    dve.sem_inc(s_lo[s].h, 1)

                def stage(b, half):
                    dve.wait_ge(s_hi[half].h, s_hi[half].at(1) + b)
                    low = slice(HD, P)
                    nc.vector.scalar_tensor_tensor(out=qst[low, half], in0=raw[low, half, 0], scalar=SCALE, in1=qst[low, half].bitcast(F32),
                                                   op0=ALU.mult, op1=ALU.subtract)
                    nc.vector.tensor_tensor(klo[:, half], raw[:, half, 1], khi[:, half].bitcast(F32), ALU.subtract).then_inc(s_lo[half].h, 1)

                def negmax(b, n):
                    t = work[n][1]
                    dve.wait_ge(s_s.h, s_s.at(1 + n + n_t) + b * n_t)
                    dve.wait_ge(s_p.h, s_p.at(1 + n) + b * n_t)
                    if t[3]:
                        local, slot = t[3]
                        prev = of_tile[n - 2][-1] - (n_g if n < 2 else 0)
                        dve.wait_ge(s_t.h, s_t.at(1 + prev + n_g) + b * n_g)
                        head = bias[:, bass.ds(b, 1), work[n][0], slot * GRID_W:slot * GRID_W + local].rearrange("p a t -> p (a t)")
                        nc.vector.tensor_tensor(pr[:, n % 2, 0:local], score(n % 2)[:, 0:local], head, ALU.add)
                        nc.vector.tensor_copy(pr[:, n % 2, local:width(t)], score(n % 2)[:, local:width(t)]).then_inc(s_b.h, 1)
                        dve.wait_ge(s_b.h, s_b.at(1 + before[n]) + b * n_bias)
                    src = pr[:, n % 2, 0:width(t)] if t[3] else score(n % 2)[:, 0:width(t)]
                    nc.vector.tensor_reduce(nb[:, n % 2:n % 2 + 1], src, axis=AX.X, op=ALU.max, negate=True).then_inc(s_nb.h, 1)

                def result(b, n):
                    half, t = work[n]
                    dve.wait_ge(s_p.h, s_p.at(3 + n) + b * n_t)
                    nc.vector.reciprocal(rinv[:, n % 2:n % 2 + 1], rsum[:, n % 2:n % 2 + 1]).then_inc(s_ri.h, 1)
                    dve.wait_ge(s_ri.h, s_ri.at(1 + n) + b * n_t)
                    dve.wait_ge(s_pv.h, s_pv.at(3 + of_tile[n][-1]) + b * n_g)
                    nc.vector.tensor_scalar(o_n[:, bass.ds(b, 1), t[0], half * HD:(half + 1) * HD].rearrange("p a t -> p (a t)"),
                                            score(n % 2)[:, o_cols], rinv[:, n % 2:n % 2 + 1], None, ALU.mult).then_inc(s_o.h, 1)

                def body(b, last):
                    for n in range(n_t):
                        xs = of_tile[n]
                        if copier[xs[0] % 2] == "dve":
                            copy(dve, nc.vector.tensor_copy, b, xs[0])
                        if n + 1 < n_t:
                            negmax(b, n + 1)
                        elif not last:
                            negmax(b + 1, 0)
                        for x in xs[1:]:
                            if copier[x % 2] == "dve":
                                copy(dve, nc.vector.tensor_copy, b, x)
                        result(b, n)
                        staging(b, n, last, stage)
                stage(0, 0)
                negmax(0, 0)
                blocks(dve, body)
                for b in range(3):
                    dve.wait_ge(s_yt.h, s_yt.at(b + 1))
                    if b >= 2:
                        dve.wait_ge(s_st[0].h, s_st[0].at(16))
                    nc.vector.tensor_copy(yb[:, b % 2, 0:n_q * P], score(0)[:, 0:n_q * P]).then_inc(s_y.h, 1)
    s_s.done(4 * n_t)
    s_b.done(3 * n_bias)
    s_nb.done(3 * n_t)
    s_p.done(2 + 3 * n_t)
    s_t.done(4 * n_g)
    s_pv.done(2 + 3 * n_g)
    s_ri.done(3 * n_t)
    s_o.done(2 + 3 * n_t)
    s_yt.done(3)
    s_y.done(3)
    for s in range(2):
        s_pt[s].done(1 + 3 * n_g // 2)
        s_st[s].done(32 - 16 * s)
        s_raw[s].done(3 * 64)
        s_hi[s].done(3)
        s_lo[s].done(4)
        s_v[s].done(3)


def spans(keys):
    out = []
    for i, (_, rows, _) in enumerate(keys):
        if out and out[-1][2] == rows:
            out[-1] = (out[-1][0], (i + 1) * P, rows)
        else:
            out.append((i * P, (i + 1) * P, rows))
    return out


def gqa_prepare(k, l, pj, v6):
    nc = k.nc
    N = 4
    items = [(i, c) for i in range(N) for c in range(len(CHUNKS))]
    lat = [(i, c) for i, c in items if c < 2]
    with ExitStack() as st:
        cos = k.sb(st, "cos", [P, SEQ])
        sin = k.sb(st, "sin", [P, SEQ])
        sq = k.sb(st, "qk_sq", [P, 2, 512])
        rs = k.sb(st, "qk_rstd", [P, N, NT])
        t1 = k.sb(st, "rot_sin", [P, 2, 512])
        s_c, s_kd = k.sem("tables_loaded"), k.sem("qk_stored")
        s_sq, s_ms, s_e, s_rt, s_rc, s_n, s_ro, s_t1, s_cs, s_q, s_vt, s_v = (k.sem(x) for x in (
            "qk_square", "qk_mean", "qk_eps", "qk_root", "qk_rstd", "qk_normed", "qk_rotated", "rot_sin", "qk_cos", "qk_done", "v_turned", "v_copied"))
        with nc.Block() as block:
            @block.sync
            def _(sp):
                sp.dma_start(cos[:], k.a["c_cos"]).then_inc(s_c.h, 16)
                sp.dma_start(sin[:], k.a["c_sin"]).then_inc(s_c.h, 16)
                sp.wait_ge(s_q.h, s_q.at(len(lat)))
                for i in range(N):
                    sp.dma_start(k.pj_dram[:, GQ_COL // P + i], pj[:, i]).then_inc(s_kd.h, 16)
                sp.wait_ge(s_kd.h, s_kd.at(N * 16))

            @block.scalar
            def _(act):
                for n, (i, c) in enumerate(items):
                    t0, tn = CHUNKS[c]
                    if n >= 2:
                        act.wait_ge(s_ms.h, s_ms.at(n - 1))
                    nc.scalar.activation(sq[:, n % 2, 0:tn], pj[:, i, t0:t0 + tn], ACT.Square).then_inc(s_sq.h, 1)
                act.wait_ge(s_e.h, s_e.at(len(items)))
                nc.scalar.activation(rs[:], rs[:], ACT.Sqrt).then_inc(s_rt.h, 1)

            @block.tensor
            def _(pe):
                for n, (i, c) in enumerate(items):
                    tn = CHUNKS[c][1]
                    pe.wait_ge(s_sq.h, s_sq.at(n + 1))
                    if n >= 2:
                        pe.wait_ge(s_e.h, s_e.at(n - 1))
                    nc.tensor.matmul(k.psum[:, n % 2, 0:tn], k.mean_h[:], sq[:, n % 2, 0:tn], start=True, stop=True).then_inc(s_ms.h, 1)
                for t in range(TT):
                    if t >= 2:
                        pe.wait_ge(s_v.h, s_v.at(2 * (t - 1)))
                    nc.tensor.transpose(k.psum[:, 4 + t % 2, 0:P], pj[:, 4, t * P:(t + 1) * P], k.ident[:]).then_inc(s_vt.h, 1)
                for n, (i, c) in enumerate(lat):
                    t0, tn = CHUNKS[c]
                    pe.wait_ge(s_n.h, s_n.at(items.index((i, c)) + 1))
                    if n >= 2:
                        pe.wait_ge(s_t1.h, s_t1.at(n - 1))
                    nc.tensor.matmul(k.psum[:, 2 + n % 2, 0:tn], k.rot[:], pj[:, i, t0:t0 + tn], start=True, stop=True).then_inc(s_ro.h, 1)

            @block.vector
            def _(dve):
                for n, (i, c) in enumerate(items):
                    t0, tn = CHUNKS[c]
                    dve.wait_ge(s_ms.h, s_ms.at(n + 1))
                    nc.vector.tensor_scalar(rs[:, i, t0:t0 + tn], k.psum[:, n % 2, 0:tn], EPS, None, ALU.add).then_inc(s_e.h, 1)
                for t in range(TT):
                    dve.wait_ge(s_vt.h, s_vt.at(t + 1))
                    for kv in range(2):
                        dst = v6[:, t].rearrange("p a (h d) -> p (a h) d", h=2)[:, 3 * kv:3 * kv + 3]
                        nc.vector.tensor_copy(dst, k.psum[:, 4 + t % 2, kv * HD:(kv + 1) * HD].unsqueeze(1).to_broadcast([P, 3, HD])).then_inc(s_v.h, 1)
                dve.wait_ge(s_rt.h, s_rt.at(1))
                nc.vector.reciprocal(rs[:], rs[:]).then_inc(s_rc.h, 1)
                dve.wait_ge(s_rc.h, s_rc.at(1))
                for n, (i, c) in enumerate(items):
                    t0, tn = CHUNKS[c]
                    col = (V_QN if i < 3 else V_KN) + l
                    nc.vector.scalar_tensor_tensor(out=pj[:, i, t0:t0 + tn], in0=pj[:, i, t0:t0 + tn], scalar=k.vecs[:, col:col + 1],
                                                   in1=rs[:, i, t0:t0 + tn], op0=ALU.mult, op1=ALU.mult).then_inc(s_n.h, 1)
                dve.wait_ge(s_c.h, s_c.at(32))
                for n, (i, c) in enumerate(lat):
                    t0, tn = CHUNKS[c]
                    dve.wait_ge(s_ro.h, s_ro.at(n + 1))
                    nc.vector.tensor_tensor(t1[:, n % 2, 0:tn], k.psum[:, 2 + n % 2, 0:tn], sin[:, t0:t0 + tn], ALU.mult).then_inc(s_t1.h, 1)
                    nc.vector.tensor_tensor(pj[:, i, t0:t0 + tn], pj[:, i, t0:t0 + tn], cos[:, t0:t0 + tn], ALU.mult).then_inc(s_cs.h, 1)
                    dve.wait_ge(s_cs.h, s_cs.at(n + 1))
                    nc.vector.tensor_tensor(pj[:, i, t0:t0 + tn], pj[:, i, t0:t0 + tn], t1[:, n % 2, 0:tn], ALU.add).then_inc(s_q.h, 1)
    for x in (s_sq, s_ms, s_e, s_n):
        x.done(len(items))
    for x in (s_ro, s_t1, s_cs, s_q):
        x.done(len(lat))
    s_rt.done(1)
    s_rc.done(1)
    s_vt.done(TT)
    s_v.done(2 * TT)
    s_c.done(32)
    s_kd.done(N * 16)


def na_prepare(k, l, pj, v6, bias):
    nc = k.nc
    n_s = SLOTS + MID
    with ExitStack() as st:
        rows = k.sb(st, "rpb_rows", [90, P])
        colm = k.sb(st, "col_mask", [P, GRID_W])
        midm = k.sb(st, "mid_mask", [P, MID, GRID_W])
        s_sk = k.sem("rpb_skewed")
        s_z, s_r, s_pad, s_b, s_m, s_cm, s_mid, s_vt, s_v = (k.sem(x) for x in (
            "rpb_zero", "rpb_loaded", "rpb_padded", "bias_loaded", "masks_loaded", "bias_masked", "bias_middle", "nv_turned", "nv_copied"))
        b4 = bias.rearrange("p a h (s c) -> p (a h) s c", c=GRID_W)
        with nc.Block() as block:
            @block.gpsimd
            def _(pool):
                nc.gpsimd.memset(rows[:], 0.0).then_inc(s_z.h, 1)

            @block.sync
            def _(sp):
                sp.dma_start(colm[:], k.a["c_colmask"]).then_inc(s_m.h, 16)
                sp.dma_start(midm[:], k.a["c_midmask"].rearrange("p (s c) -> p s c", s=MID)).then_inc(s_m.h, 16)
                sp.wait_ge(s_z.h, s_z.at(1))
                mid = GRID_W - 1 - (NA_KW - 1)
                sp.dma_start(rows[:, mid:mid + 2 * NA_KW - 1], k.a["na_rpb"][l].rearrange("h r c -> (h r) c")).then_inc(s_r.h, 16)
                sp.wait_ge(s_r.h, s_r.at(16))
                sp.dma_start(k.rpb_dram, rows[:]).then_inc(s_pad.h, 16)
                sp.wait_ge(s_pad.h, s_pad.at(16))
                skewed = bass.AP(k.rpb_dram.tensor, GRID_W - 1, [[P, 90], [-1, GRID_W], [1, GRID_W]])
                sp.dma_start(k.rpb_skew, skewed).then_inc(s_sk.h, 16)
                sp.wait_ge(s_sk.h, s_sk.at(16))
                for h in range(6):
                    for par in range(2):
                        src = k.rpb_skew[h * 15 + 1 - par:h * 15 + 1 - par + SLOTS].rearrange("s c j -> c s j")
                        sp.dma_start(b4[par * GRID_W:(par + 1) * GRID_W, h, 0:SLOTS], src).then_inc(s_b.h, 16)
                sp.wait_ge(s_b.h, s_b.at(12 * 16))

            @block.tensor
            def _(pe):
                for t in range(TT):
                    if t >= 2:
                        pe.wait_ge(s_v.h, s_v.at(t - 1))
                    for b in range(3):
                        ins = nc.tensor.transpose(k.psum[:, t % 2, b * P:(b + 1) * P], pj[:, b, t * P:(t + 1) * P], k.ident[:])
                    ins.then_inc(s_vt.h, 1)

            @block.vector
            def _(dve):
                for t in range(TT):
                    dve.wait_ge(s_vt.h, s_vt.at(t + 1))
                    nc.vector.tensor_copy(v6[:, t].rearrange("p a d -> p (a d)"), k.psum[:, t % 2, 0:3 * P]).then_inc(s_v.h, 1)
                dve.wait_ge(s_m.h, s_m.at(32))
                dve.wait_ge(s_b.h, s_b.at(12 * 16))
                for h in range(6):
                    nc.vector.tensor_tensor(b4[:, h, 0:SLOTS], b4[:, h, 0:SLOTS], colm[:].unsqueeze(1).to_broadcast([P, SLOTS, GRID_W]), ALU.add).then_inc(s_cm.h, 1)
                for h in range(6):
                    dve.wait_ge(s_cm.h, s_cm.at(h + 1))
                    nc.vector.tensor_tensor(b4[:, h, SLOTS:n_s], b4[:, h, 2:2 + MID], midm[:], ALU.add).then_inc(s_mid.h, 1)
    s_z.done(1)
    s_r.done(16)
    s_pad.done(16)
    s_sk.done(16)
    s_b.done(12 * 16)
    s_m.done(32)
    s_cm.done(6)
    s_mid.done(6)
    s_vt.done(TT)
    s_v.done(TT)


def split_y(k, tokens, h_hi, h_lo):
    nc = k.nc
    with ExitStack() as st:
        yt = k.sb(st, "y_in", [P, 2, NT])
        s_in = [k.sem(f"y_loaded{s}") for s in range(2)]
        s_hi, s_lo = k.sem("y_hi"), k.sem("y_lo")
        with nc.Block() as block:
            @block.sync
            def _(sp):
                for j in range(KB):
                    if j >= 2:
                        sp.wait_ge(s_lo.h, s_lo.at(j - 1))
                    sp.dma_start(yt[:, j % 2, 0:tokens], k.y_dram[:, j, 0:tokens]).then_inc(s_in[j % 2].h, 16)

            @block.scalar
            def _(act):
                for j in range(KB):
                    act.wait_ge(s_in[j % 2].h, s_in[j % 2].at(16 * (j // 2 + 1)))
                    nc.scalar.copy(h_hi[:, j, 0:tokens], yt[:, j % 2, 0:tokens]).then_inc(s_hi.h, 1)

            @block.vector
            def _(dve):
                for j in range(KB):
                    dve.wait_ge(s_hi.h, s_hi.at(j + 1))
                    nc.vector.tensor_tensor(h_lo[:, j, 0:tokens], yt[:, j % 2, 0:tokens], h_hi[:, j, 0:tokens].bitcast(F32), ALU.subtract).then_inc(s_lo.h, 1)
    for s in range(2):
        s_in[s].done(16 * KB // 2)
    s_hi.done(KB)
    s_lo.done(KB)


GROUP = 4 * CHUNK
N_G = NT // GROUP


def hgrn_gates(k, l, pj, kk, vt, o_acc):
    nc = k.nc
    with ExitStack() as st:
        e = k.sb(st, "gate_exp", [P, 2, NT])
        r = k.sb(st, "gate_inv", [P, 2, NT])
        keep = k.sb(st, "keep", [P, NT])
        s_k, s_si, s_cl, s_e, s_ln, s_st, s_vt, s_v, s_o = (k.sem(x) for x in (
            "keep_loaded", "silu_qg", "gate_clamped", "gate_exp", "gate_logs", "gate_step", "hv_turned", "hv_copied", "o_zero"))
        shift = 2.0 ** LOG_SHIFT
        n_steps = 4 * 9
        with nc.Block() as block:
            @block.gpsimd
            def _(pool):
                for t in range(TT):
                    nc.gpsimd.memset(o_acc[:, t], 0.0).then_inc(s_o.h, 1)

            @block.sync
            def _(sp):
                sp.dma_start(keep[:], k.a["c_keep"]).then_inc(s_k.h, 16)

            @block.scalar
            def _(act):
                for b in (0, 1, 8, 9):
                    nc.scalar.activation(pj[:, b], pj[:, b], ACT.Silu).then_inc(s_si.h, 1)

                def exp(i):
                    act.wait_ge(s_cl.h, s_cl.at(i + 1))
                    nc.scalar.activation(e[:, i % 2], pj[:, 2 + i], ACT.Exp, scale=-1.0, bias=k.fbias[:]).then_inc(s_e.h, 1)
                exp(0)
                exp(1)
                for i in range(4):
                    act.wait_ge(s_st.h, s_st.at(9 * i + 6))
                    nc.scalar.activation(e[:, i % 2], e[:, i % 2], ACT.Ln)
                    nc.scalar.activation(r[:, i % 2], r[:, i % 2], ACT.Ln).then_inc(s_ln.h, 1)
                    if i + 2 < 4:
                        act.wait_ge(s_st.h, s_st.at(9 * i + 7))
                        exp(i + 2)

            @block.tensor
            def _(pe):
                for t in range(TT):
                    if t >= 2:
                        pe.wait_ge(s_v.h, s_v.at(t - 1))
                    for b in range(2):
                        ins = nc.tensor.transpose(k.psum[:, t % 2, b * P:(b + 1) * P], pj[:, 6 + b, t * P:(t + 1) * P], k.ident[:])
                    ins.then_inc(s_vt.h, 1)

            @block.vector
            def _(dve):
                n = [0]

                def step(ins):
                    ins.then_inc(s_st.h, 1)
                    n[0] += 1
                    dve.wait_ge(s_st.h, s_st.at(n[0]))
                for i in range(4):
                    nc.vector.tensor_scalar(pj[:, 2 + i], pj[:, 2 + i], -88.0, None, ALU.max).then_inc(s_cl.h, 1)
                for t in range(TT):
                    dve.wait_ge(s_vt.h, s_vt.at(t + 1))
                    nc.vector.tensor_copy(vt[:, t], k.psum[:, t % 2, 0:2 * P]).then_inc(s_v.h, 1)
                dve.wait_ge(s_k.h, s_k.at(16))
                for i in range(4):
                    ei, ri = e[:, i % 2], r[:, i % 2]
                    omlb, lbs = k.omlb[:, l, i:i + 1], k.lbs[:, l, i:i + 1]
                    dve.wait_ge(s_e.h, s_e.at(i + 1))
                    step(nc.vector.tensor_scalar(ri, ei, 1.0 / shift, None, ALU.add))
                    step(nc.vector.reciprocal(ri, ri))
                    step(nc.vector.scalar_tensor_tensor(out=kk[:, i], in0=ei, scalar=omlb, in1=ri, op0=ALU.mult, op1=ALU.mult))
                    step(nc.vector.tensor_scalar(ri, ri, omlb, lbs, ALU.mult, ALU.add))
                    step(nc.vector.tensor_scalar(ei, ri, 1.0 / shift, 1.0 / shift, ALU.mult, ALU.max))
                    step(nc.vector.tensor_scalar(ri, ri, 1.0, None, ALU.min))
                    dve.wait_ge(s_ln.h, s_ln.at(i + 1))
                    step(nc.vector.tensor_tensor(pj[:, 2 + i], ei, ri, ALU.add))
                    step(nc.vector.tensor_scalar(pj[:, 2 + i], pj[:, 2 + i], 0.0, None, ALU.min))
                    f = pj[:, 2 + i] if i < 2 else pj[:, 2 + i][:, ::-1]
                    step(nc.vector.tensor_tensor_scan(f, keep[:], f, 0.0, ALU.mult, ALU.add))
                dve.wait_ge(s_si.h, s_si.at(4))
    s_k.done(16)
    s_si.done(4)
    s_cl.done(4)
    s_e.done(4)
    s_ln.done(4)
    s_st.done(n_steps)
    s_vt.done(TT)
    s_v.done(TT)
    s_o.done(TT)


def hgrn_scan(k, pj, kk, vt, o_acc):
    nc = k.nc
    with ExitStack() as st:
        z = k.sb(st, "z", [P, LEVELS, 2, GROUP])
        qd = k.sb(st, "q_decayed", [P, 2, GROUP])
        kd = k.sb(st, "k_decayed", [P, 2, GROUP])
        qs = k.sb(st, "q_group", [P, 2, GROUP])
        ks = k.sb(st, "k_group", [P, 2, GROUP])
        vs = k.sb(st, "v_group", [P, 2, 2 * P])
        kt = k.sb(st, "k_turned", [P, 2, 2 * P])
        et = k.sb(st, "chunk_decay", [P, 2, 4])
        mask = k.sb(st, "level_masks", [P, 2, NL * CHUNK])
        am = k.sb(st, "att_masked", [P, 2, NL * CHUNK])
        at = k.sb(st, "att_hg", [P, 4, CHUNK])
        state = k.sb(st, "state", [P, 2, 2, HD])
        s_mk, s_g, s_d, s_x, s_kd, s_z, s_kt, s_kc, s_att, s_am, s_at, s_ds, s_os, s_oa, s_st, s_ad, s_s0 = (k.sem(x) for x in (
            "masks_in", "group_staged", "distances", "decays", "k_decayed", "z_ready", "k_turned", "k_copied", "att_ready", "att_masked",
            "att_summed", "state_add", "out_state", "out_att", "state_new", "out_added", "state_zero"))
        PAIRS = 2

        def view(x, lvl):
            return x.rearrange("p a (n s b) -> p (a n) s b", s=2, b=1 << lvl)

        def loop(e, body):
            body(0, 0, SEQ)
            body(0, 1, SEQ)
            for i in range(1, N_G):
                body(i, 0, (i - 1) * GROUP)
                body(i, 1, (N_G - 1 - i) * GROUP)

        def cum(d, tok):
            return pj[:, 2 + 2 * d:4 + 2 * d, bass.ds(tok, GROUP)]
        with nc.Block() as block:
            @block.sync
            def _(sp):
                sp.dma_start(mask[:], k.a["c_levels"].rearrange("d p n -> p d n")).then_inc(s_mk.h, 16)

            @block.gpsimd
            def _(pool):
                nc.gpsimd.memset(state[:], 0.0).then_inc(s_s0.h, 1)

                def stage(i, d, tok):
                    q = 2 * i + d
                    pool.wait_ge(s_oa.h, s_oa.at(PAIRS) + q * PAIRS)
                    pool.wait_ge(s_z.h, s_z.at(1) + q)
                    nc.gpsimd.tensor_copy(qs[:], pj[:, 0:2, bass.ds(tok, GROUP)]).then_inc(s_g.h, 1)
                    nc.gpsimd.tensor_copy(ks[:], kk[:, 2 * d:2 * d + 2, bass.ds(tok, GROUP)]).then_inc(s_g.h, 1)
                    tile = tok // P
                    nc.gpsimd.tensor_copy(vs[:], vt[:, bass.ds(tile, 2)]).then_inc(s_g.h, 1)
                loop(pool, stage)

            @block.scalar
            def _(act):
                def decays(i, d, tok):
                    q = 2 * i + d
                    act.wait_ge(s_d.h, s_d.at(LEVELS + 1) + q * (LEVELS + 1))
                    nc.scalar.activation(kd[:], kd[:], ACT.Exp, scale=-1.0)
                    end = CHUNK - 1 if d == 0 else 0
                    nc.scalar.activation(et[:], cum(d, tok).rearrange("p a (n c) -> p a n c", c=CHUNK)[:, :, :, end], ACT.Exp).then_inc(s_x.h, 1)
                    act.wait_ge(s_os.h, s_os.at(PAIRS * 2) + q * PAIRS * 2)
                    nc.scalar.activation(qd[:], cum(d, tok), ACT.Exp).then_inc(s_x.h, 1)
                    for lvl in range(LEVELS):
                        zl = view(z[:, lvl], lvl)
                        for part in range(2):
                            late = part == (1 if d == 0 else 0)
                            ins = nc.scalar.activation(zl[:, :, part], zl[:, :, part], ACT.Exp, scale=1.0 if late else -1.0)
                        ins.then_inc(s_x.h, 1)

                def turned(i, d, tok):
                    q = 2 * i + d
                    act.wait_ge(s_kt.h, s_kt.at(2) + q)
                    nc.scalar.copy(kt[:].rearrange("p a b -> p (a b)"), k.psum[:, 7]).then_inc(s_kc.h, 1)

                def body(i, d, tok):
                    decays(i, d, tok)
                    turned(i, d, tok)
                loop(act, body)

            @block.vector
            def _(dve):
                dve.sem_inc(s_z.h, 1)
                dve.sem_inc(s_am.h, 4)
                dve.sem_inc(s_ad.h, 4)
                dve.wait_ge(s_mk.h, s_mk.at(16))

                def body(i, d, tok):
                    q = 2 * i + d
                    c3 = cum(d, tok)
                    end = CHUNK - 1 if d == 0 else 0
                    chunks = c3.rearrange("p a (n c) -> p a n c", c=CHUNK)
                    dve.wait_ge(s_kt.h, s_kt.at(1) + q)
                    for blk in range(2):
                        ins = nc.vector.tensor_tensor(kd[:, blk].rearrange("p (n c) -> p n c", c=CHUNK), chunks[:, blk],
                                                      chunks[:, blk, :, end:end + 1].to_broadcast([P, 4, CHUNK]), ALU.subtract)
                    ins.then_inc(s_d.h, 1)
                    dve.wait_ge(s_att.h, s_att.at(PAIRS * 4) + q * PAIRS * 4)
                    for lvl in range(LEVELS):
                        b = 1 << lvl
                        seam = b - 1 if d == 0 else b
                        for blk in range(2):
                            c4 = c3[:, blk].rearrange("p (n c) -> p n c", c=2 * b)
                            ins = nc.vector.tensor_tensor(z[:, lvl, blk].rearrange("p (n c) -> p n c", c=2 * b), c4,
                                                          c4[:, :, seam:seam + 1].to_broadcast([P, GROUP // (2 * b), 2 * b]), ALU.subtract)
                        ins.then_inc(s_d.h, 1)
                    dve.wait_ge(s_g.h, s_g.at(3) + q * 3)
                    dve.wait_ge(s_x.h, s_x.at(1) + q * (LEVELS + 2))
                    nc.vector.tensor_tensor(kd[:], kd[:], ks[:], ALU.mult).then_inc(s_kd.h, 1)
                    dve.wait_ge(s_x.h, s_x.at(2) + q * (LEVELS + 2))
                    nc.vector.tensor_tensor(qd[:], qd[:], qs[:], ALU.mult)
                    for lvl in range(LEVELS):
                        dve.wait_ge(s_x.h, s_x.at(3 + lvl) + q * (LEVELS + 2))
                        zl = view(z[:, lvl], lvl)
                        for part in range(2):
                            late = part == (1 if d == 0 else 0)
                            ins = nc.vector.tensor_tensor(zl[:, :, part], zl[:, :, part], view((qs if late else ks)[:], lvl)[:, :, part], ALU.mult)
                    ins.then_inc(s_z.h, 1)
                    for w in range(PAIRS):
                        pr = w if d == 0 else PAIRS - 1 - w
                        n = q * PAIRS + w
                        for u in range(4):
                            dve.wait_ge(s_att.h, s_att.at(PAIRS * 4 + 1 + w * 4 + u) + q * (PAIRS * 4))
                            nc.vector.tensor_tensor(am[:, u % 2], k.psum[:, u, 0:NL * CHUNK], mask[:, d], ALU.mult).then_inc(s_am.h, 1)
                            dve.wait_ge(s_am.h, s_am.at(5 + w * 4 + u) + q * (PAIRS * 4))
                            dve.wait_ge(s_oa.h, s_oa.at(PAIRS + w) + q * PAIRS)
                            nc.vector.tensor_reduce(at[:, u], am[:, u % 2].rearrange("p (l t) -> p t l", l=NL), axis=AX.X, op=ALU.add).then_inc(s_at.h, 1)
                        for m in range(2):
                            c = m if d == 0 else 1 - m
                            dve.wait_ge(s_ds.h, s_ds.at(1 + w) + q * PAIRS)
                            dve.wait_ge(s_os.h, s_os.at(PAIRS * 2 + 1 + w * 2 + m) + q * PAIRS * 2)
                            for blk in range(2):
                                ins = nc.vector.scalar_tensor_tensor(out=state[:, d, blk], in0=state[:, d, blk], scalar=et[:, blk, 2 * pr + c:2 * pr + c + 1],
                                                                     in1=k.psum[:, 4 + c, 384 + blk * HD:384 + (blk + 1) * HD], op0=ALU.mult, op1=ALU.add)
                            ins.then_inc(s_st.h, 1)
                        dve.wait_ge(s_oa.h, s_oa.at(PAIRS + 1 + w) + q * PAIRS)
                        tile = tok // P + pr
                        for c in range(2):
                            rows = slice(c * CHUNK, (c + 1) * CHUNK)
                            o = o_acc[rows, bass.ds(tile, 1)].rearrange("p a t -> p (a t)")
                            nc.vector.tensor_tensor(o, o, k.psum[rows, 4 + c, 0:256], ALU.add).then_inc(s_ad.h, 1)
                        dve.wait_ge(s_ad.h, s_ad.at(6 + w * 4) + q * PAIRS * 4)
                        for hh in range(2):
                            o = o_acc[:, bass.ds(tile, 1)].rearrange("p a (b h v) -> p (a b) h v", b=2, h=2)[:, :, hh]
                            nc.vector.tensor_tensor(o, o, k.psum[:, 4 + hh, 256:384].rearrange("p (b v) -> p b v", b=2), ALU.add).then_inc(s_ad.h, 1)
                loop(dve, body)

            @block.tensor
            def _(pe):
                pe.sem_inc(s_kt.h, 1)
                pe.sem_inc(s_att.h, PAIRS * 4)
                pe.sem_inc(s_os.h, PAIRS * 2)
                pe.sem_inc(s_oa.h, PAIRS)
                pe.wait_ge(s_s0.h, s_s0.at(1))

                def body(i, d, tok):
                    q = 2 * i + d
                    pe.wait_ge(s_kd.h, s_kd.at(1) + q)
                    if not (isinstance(i, int) and q == 0):
                        pe.wait_ge(s_kc.h, s_kc.at(0) + q)
                    for tile in range(2):
                        for blk in range(2):
                            ins = nc.tensor.transpose(k.psum[:, 7, (tile * 2 + blk) * P:(tile * 2 + blk + 1) * P],
                                                      kd[:, blk, tile * P:(tile + 1) * P], k.ident[:])
                    ins.then_inc(s_kt.h, 1)
                    pe.wait_ge(s_z.h, s_z.at(2) + q)
                    for w in range(PAIRS):
                        pr = w if d == 0 else PAIRS - 1 - w
                        for u in range(4):
                            blk, hh = u // 2, u % 2
                            rows = slice(hh * HD, (hh + 1) * HD)
                            pe.wait_ge(s_am.h, s_am.at(1 + w * 4 + u) + q * (PAIRS * 4))
                            for c in range(2):
                                toks = slice((2 * pr + c) * CHUNK, (2 * pr + c + 1) * CHUNK)
                                out = k.psum[c * CHUNK:(c + 1) * CHUNK, u]
                                for lvl in range(LEVELS):
                                    zz = z[rows, lvl, blk, toks]
                                    nc.tensor.matmul(out[:, lvl * CHUNK:(lvl + 1) * CHUNK], zz, zz, start=True, stop=True)
                                ins = nc.tensor.matmul(out[:, LEVELS * CHUNK:NL * CHUNK], ks[rows, blk, toks], qs[rows, blk, toks], start=True, stop=True)
                            ins.then_inc(s_att.h, 1)
                        if w == 0:
                            pe.wait_ge(s_kc.h, s_kc.at(1) + q)
                        pe.wait_ge(s_ad.h, s_ad.at(4 + w * 4) + q * PAIRS * 4)
                        for c in range(2):
                            rows = slice(c * CHUNK, (c + 1) * CHUNK)
                            for u in range(4):
                                blk, hh = u // 2, u % 2
                                cols = slice(u * HD, (u + 1) * HD)
                                ins = nc.tensor.matmul(k.psum[hh * HD:(hh + 1) * HD, 4 + c, 384 + blk * HD:384 + (blk + 1) * HD],
                                                       kt[rows, pr, cols], vs[rows, pr, cols], start=True, stop=True)
                        ins.then_inc(s_ds.h, 1)
                        for m in range(2):
                            c = m if d == 0 else 1 - m
                            toks = slice((2 * pr + c) * CHUNK, (2 * pr + c + 1) * CHUNK)
                            if not (isinstance(i, int) and i == 0 and w == 0 and m == 0):
                                last = s_st.at(w * 2 + m) + q * PAIRS * 2 if w or m else s_st.at(-PAIRS * 2) + q * PAIRS * 2
                                pe.wait_ge(s_st.h, last)
                            for u in range(4):
                                blk, hh = u // 2, u % 2
                                rows = slice(hh * HD, (hh + 1) * HD)
                                ins = nc.tensor.matmul(k.psum[c * CHUNK:(c + 1) * CHUNK, 4 + hh, 256 + blk * HD:256 + (blk + 1) * HD],
                                                       qd[rows, blk, toks], state[rows, d, blk], start=True, stop=True)
                            ins.then_inc(s_os.h, 1)
                        pe.wait_ge(s_st.h, s_st.at(2 + w * 2) + q * PAIRS * 2)
                        pe.wait_ge(s_at.h, s_at.at(4 + w * 4) + q * PAIRS * 4)
                        for c in range(2):
                            rows = slice(c * CHUNK, (c + 1) * CHUNK)
                            for u in range(4):
                                ins = nc.tensor.matmul(k.psum[rows, 4 + c, u * HD:(u + 1) * HD], at[rows, u], vs[rows, pr, u * HD:(u + 1) * HD],
                                                       start=True, stop=True)
                        ins.then_inc(s_oa.h, 1)
                loop(pe, body)
    n = 2 * N_G
    s_mk.done(16)
    s_g.done(3 * n)
    s_d.done(n * (LEVELS + 1))
    s_x.done(n * (LEVELS + 2))
    s_kd.done(n)
    s_z.done(n + 1)
    s_kt.done(n + 1)
    s_kc.done(n)
    s_att.done((n + 1) * PAIRS * 4)
    s_am.done(4 + n * PAIRS * 4)
    s_at.done(n * PAIRS * 4)
    s_ds.done(n * PAIRS)
    s_os.done((n + 1) * PAIRS * 2)
    s_oa.done((n + 1) * PAIRS)
    s_st.done(n * PAIRS * 2)
    s_ad.done(4 + n * PAIRS * 4)
    s_s0.done(1)


def hgrn_readout(k, l, pj, o_acc, tokens):
    nc = k.nc
    n_t = tokens // P
    with ExitStack() as st:
        sq = k.sb(st, "o_sq", [P, TT, 2 * P])
        ms = k.sb(st, "o_ms", [P, TT * 4])
        yb = k.sb(st, "hg_y", [P, 2, NT])
        s_v, s_rt, s_t, s_y, s_st = k.sem("ro_step"), k.sem("ro_root"), k.sem("ro_turned"), k.sem("ro_done"), k.sem("ro_stored")
        work = [(b, t0) for b in range(2) for t0 in range(0, n_t, 4)]
        o4 = o_acc[:, 0:n_t].rearrange("p t (h v) -> p (t h) v", v=HD)
        q4 = sq[:, 0:n_t].rearrange("p t (h v) -> p (t h) v", v=HD)
        m = ms[:, 0:4 * n_t]
        with nc.Block() as block:
            @block.vector
            def _(dve):
                nc.vector.tensor_tensor(q4, o4, o4, ALU.mult).then_inc(s_v.h, 1)
                dve.wait_ge(s_v.h, s_v.at(1))
                nc.vector.tensor_reduce(m, q4, axis=AX.X, op=ALU.add).then_inc(s_v.h, 1)
                dve.wait_ge(s_v.h, s_v.at(2))
                nc.vector.tensor_scalar(m, m, 1.0 / HD, EPS, ALU.mult, ALU.add).then_inc(s_v.h, 1)
                dve.wait_ge(s_rt.h, s_rt.at(1))
                nc.vector.reciprocal(m, m).then_inc(s_v.h, 1)
                dve.wait_ge(s_v.h, s_v.at(4))
                nc.vector.tensor_tensor(o4, o4, m.unsqueeze(2).to_broadcast([P, 4 * n_t, HD]), ALU.mult).then_inc(s_v.h, 1)
                for n, (b, t0) in enumerate(work):
                    cnt = min(4, n_t - t0) * P
                    dve.wait_ge(s_t.h, s_t.at(n + 1))
                    nc.vector.scalar_tensor_tensor(out=yb[:, b, t0 * P:t0 * P + cnt], in0=k.psum[:, n % 2, 0:cnt], scalar=k.vecs[:, V_HN + l:V_HN + l + 1],
                                                   in1=pj[:, 8 + b, t0 * P:t0 * P + cnt], op0=ALU.mult, op1=ALU.mult).then_inc(s_y.h, 1)

            @block.scalar
            def _(act):
                act.wait_ge(s_v.h, s_v.at(3))
                nc.scalar.activation(m, m, ACT.Sqrt).then_inc(s_rt.h, 1)

            @block.tensor
            def _(pe):
                pe.wait_ge(s_v.h, s_v.at(5))
                for n, (b, t0) in enumerate(work):
                    if n >= 2:
                        pe.wait_ge(s_y.h, s_y.at(n - 1))
                    for t in range(t0, min(t0 + 4, n_t)):
                        ins = nc.tensor.transpose(k.psum[:, n % 2, (t - t0) * P:(t - t0 + 1) * P], o_acc[:, t, b * P:(b + 1) * P], k.ident[:])
                    ins.then_inc(s_t.h, 1)

            @block.sync
            def _(sp):
                sp.wait_ge(s_y.h, s_y.at(len(work)))
                sp.dma_start(k.y_dram[:, 0:2, 0:tokens], yb[:, :, 0:tokens]).then_inc(s_st.h, 16)
                sp.wait_ge(s_st.h, s_st.at(16))
    s_v.done(5)
    s_rt.done(1)
    s_t.done(len(work))
    s_y.done(len(work))
    s_st.done(16)


def load_blocks(k, dst, first):
    n = dst.shape[1]
    s = k.sem("blocks_loaded")
    with k.nc.Block() as block:
        @block.sync
        def _(sp):
            for i in range(n):
                sp.dma_start(dst[:, i], k.pj_dram[:, first + i]).then_inc(s.h, 16)
            sp.wait_ge(s.h, s.at(16 * n))
    s.done(16 * n)


def project_in(k, l, h_hi, h_lo):
    w_in = k.a["w_in"][l].rearrange("(j p) n -> p j n", p=P)
    linear(k, lambda u: w_in[:, :, bass.ds(u * P, P)], IN_W // P, NT, h_hi, h_lo, None)


def mix(k, l, ctx):
    with ExitStack() as st:
        pj = k.sb(st, "hg_pj", [P, 10, NT])
        kk = k.sb(st, "hg_kk", [P, 4, NT])
        vt = k.sb(st, "hg_v", [P, TT, 2 * P])
        o_acc = k.sb(st, "hg_o", [P, TT, 2 * P])
        load_blocks(k, pj, HG_COL // P)
        hgrn_gates(k, l, pj, kk, vt, o_acc)
        hgrn_scan(k, pj, kk, vt, o_acc)
        hgrn_readout(k, l, pj, o_acc, NT if ctx else SEQ)
    with ExitStack() as st:
        v6 = k.sb(st, "gq_v", [P, TT, 3, P])
        with ExitStack() as sp:
            pj = k.sb(sp, "gq_pj", [P, 5, NT])
            load_blocks(k, pj, GQ_COL // P)
            gqa_prepare(k, l, pj, v6)
        attention(k, gqa_tiles(ctx), GQ_COL // P, lambda b, half: (((b + half) // 2) * HD, GQ_COL // P + 3), v6, None, 2)
    with ExitStack() as st:
        v6 = k.sb(st, "na_v", [P, TT, 3, P])
        bias = k.sb(st, "na_bias", [P, 3, 2, (SLOTS + MID) * GRID_W])
        with ExitStack() as sp:
            pj = k.sb(sp, "na_pj", [P, 3, NT])
            load_blocks(k, pj, NA_COL // P + 6)
            na_prepare(k, l, pj, v6, bias[:])
        attention(k, na_tiles(ctx), NA_COL // P, lambda b, half: (half * HD, NA_COL // P + 3 + b), v6, bias, 5)


def build(nc, a, out):
    with ExitStack() as top:
        k = Kernel(nc, top, a, out)
        setup(k)
        for l in range(DEPTH):
            modulation(k, l)
        with ExitStack() as st:
            h_hi = k.sb(st, "h_hi", [P, KB, NT], F32R)
            h_lo = k.sb(st, "h_lo", [P, KB, NT], F32R)
            turn_in(k, h_hi, h_lo)
            project_in(k, 0, h_hi, h_lo)
        for l in range(DEPTH):
            ctx = l < DEPTH - 1
            tokens = NT if ctx else SEQ
            mix(k, l, ctx)
            with ExitStack() as st:
                h_hi = k.sb(st, "h_hi", [P, KB, NT], F32R)
                h_lo = k.sb(st, "h_lo", [P, KB, NT], F32R)
                y = k.sb(st, "y", [P, KB, NT])
                split_y(k, tokens, h_hi, h_lo)
                w_out = a["w_out"][l].rearrange("(j p) n -> p j n", p=P)
                linear(k, lambda u: w_out[:, :, bass.ds(u * P, P)], KB, tokens, h_hi, h_lo, y)
                residual_norm(k, l, 0, tokens, y, h_hi, h_lo, False)
                swiglu(k, l, tokens, h_hi, h_lo, y)
                residual_norm(k, l, 1, tokens, y, h_hi, h_lo, not ctx)
                if ctx:
                    project_in(k, l + 1, h_hi, h_lo)


INPUTS = ["x", "c", "ctx", "c_ctx", "w_ada", "b_ada", "w_in", "hgrn_lb_logits", "hgrn_norm", "gqa_q_norm", "gqa_k_norm",
          "na_rpb", "w_out", "w_ffn_in", "w_ffn_out", "ln_g", "ln_b"]


def constants():
    c = {}
    c["c_ident"] = np.eye(P, dtype=np.float32)
    c["c_mean_d"] = np.full((P, P), 1.0 / D, np.float32)
    c["c_mean_h"] = np.kron(np.eye(2), np.full((HD, HD), 1.0 / HD)).astype(np.float32)
    rot = np.zeros((P, P), np.float32)
    for i in range(0, P, 2):
        rot[i + 1, i] = -1.0
        rot[i, i + 1] = 1.0
    c["c_rot"] = rot
    t = np.arange(SEQ)
    n_pairs = HD // 4
    inv = np.exp(-np.log(np.float32(10000.0)) * np.arange(n_pairs, dtype=np.float32) / n_pairs).astype(np.float32)
    ang = np.concatenate([(t // GRID_W).astype(np.float32)[:, None] * inv, (t % GRID_W).astype(np.float32)[:, None] * inv], -1)
    pair = (np.arange(P) % HD) // 2
    c["c_cos"] = np.ascontiguousarray(np.cos(ang).astype(np.float32).T[pair])
    c["c_sin"] = np.ascontiguousarray(np.sin(ang).astype(np.float32).T[pair])
    keep = np.ones((P, NT), np.float32)
    keep[:, ::CHUNK] = 0.0
    c["c_keep"] = keep
    levels = np.zeros((2, P, NL, CHUNK), np.float32)
    for d in range(2):
        for s in range(CHUNK):
            for q in range(CHUNK):
                if s == q:
                    levels[d, s::CHUNK, LEVELS, q] = 1.0
                elif (s < q) == (d == 0):
                    levels[d, s::CHUNK, (s ^ q).bit_length() - 1, q] = 1.0
    c["c_levels"] = levels.reshape(2, P, NL * CHUNK)
    qc, kc = np.arange(GRID_W)[:, None], np.arange(GRID_W)[None, :]
    start = np.clip(qc - NA_KW // 2, 0, GRID_W - NA_KW)
    col = np.where((kc >= start) & (kc < start + NA_KW), 0.0, NEG).astype(np.float32)
    c["c_colmask"] = np.concatenate([col, col])
    mid = np.zeros((P, MID, GRID_W), np.float32)
    mid[:GRID_W, MID - 1] = NEG
    mid[GRID_W:, 0] = NEG
    c["c_midmask"] = mid.reshape(P, MID * GRID_W)
    return c


def kernel(**inputs):
    import concourse.bacc as bacc
    from concourse.bass_utils import run_bass_kernel_spmd

    nc = bacc.Bacc("TRN2", target_bir_lowering=False, num_devices=1)
    arrays = {f"in_{n}": np.ascontiguousarray(inputs[n]) for n in INPUTS}
    arrays.update({f"in_{n}": v for n, v in constants().items()})
    a = {n[3:]: nc.dram_tensor(n, v.shape, mybir.dt.from_np(v.dtype), kind="ExternalInput").ap() for n, v in arrays.items()}
    out = nc.dram_tensor("out", (1, SEQ, D), F32, kind="ExternalOutput").ap()
    build(nc, a, out)
    r = run_bass_kernel_spmd(nc, [arrays], core_ids=[0])
    return r.results[0]["out"]
```

```python
from contextlib import ExitStack

import concourse.bass as bass
from concourse import mybir
import numpy as np

F32 = mybir.dt.float32
F32R = mybir.dt.float32r
ALU = mybir.AluOpType
ACT = mybir.ActivationFunctionType
AX = mybir.AxisListType

P = 128
D = 1024
KB = D // P
SEQ, CTX = 1024, 256
NT = SEQ + CTX
TT = NT // P
DEPTH = 2
HD = 64
GRID_W = 64
ROWS = SEQ // GRID_W
FFN = ((8 * D + 3 * 256 - 1) // (3 * 256)) * 256
HB = FFN // P
N_MOD = 6
MB = N_MOD * KB
IN_W = 3072
ALPHA = (2 * DEPTH) ** 0.25
EPS = 1e-6
SCALE = HD ** -0.5
CHUNK = 64
LEVELS = 6
NL = LEVELS + 1
LOG_SHIFT = 64
NEG = -1e30
HG_COL, GQ_COL, NA_COL = 0, 1280, 1920
NA_KH, NA_KW = 8, 16
SLOTS = 14
MID = 9
CHUNKS = [(0, 512), (512, 512), (1024, 256)]


class Sem:

    def __init__(self, nc, stack, name):
        self.h = stack.enter_context(nc.semaphore(name))
        self.base = 0

    def at(self, n):
        return n + self.base

    def done(self, n):
        self.base += n


def token_chunks(tokens):
    return [c for c in CHUNKS if c[0] < tokens]


def in_pairs(e, n, body):
    if n // 2 > 1:
        with e.Fori(0, n // 2) as i:
            for s in range(2):
                body(i * 2 + s, s, i)
    else:
        for u in range(n // 2 * 2):
            body(u, u % 2, u // 2)
    if n % 2:
        body(n - 1, (n - 1) % 2, (n - 1) // 2)


class Kernel:
    def __init__(self, nc, stack, a, out):
        self.nc, self.a, self.out = nc, a, out
        self.stack = stack
        self.sems = {}
        self.tensors = 0
        sb, dram = self.sb, self.dram
        self.x_dram = dram("x_cm", [P, KB, NT])
        self.pj_dram = dram("proj_cm", [P, IN_W // P, NT])
        self.y_dram = dram("y_cm", [P, KB, NT])
        self.rpb_dram = dram("rpb_pad", [90, P])
        self.rpb_skew = dram("rpb_skew", [90, GRID_W, GRID_W])
        self.ident = sb(stack, "ident", [P, P])
        self.mean_d = sb(stack, "mean_d", [P, P])
        self.mean_h = sb(stack, "mean_h", [P, P])
        self.rot = sb(stack, "rot", [P, P])
        self.vecs = sb(stack, "vecs", [P, 96])
        self.b_ada = sb(stack, "b_ada", [P, DEPTH * MB])
        self.mods = sb(stack, "mods", [P, DEPTH, MB, 2])
        self.lb = sb(stack, "lb", [P, DEPTH, 4])
        self.omlb = sb(stack, "omlb", [P, DEPTH, 4])
        self.lbs = sb(stack, "lbs", [P, DEPTH, 4])
        self.fbias = sb(stack, "fbias", [P, 1])
        self.psum = stack.enter_context(nc.psum_tensor("psum", [P, 8, 512], F32))
        self.set_a = self.psum[:, 0:3].rearrange("p a b -> p (a b)")
        self.set_b = self.psum[:, 3:6].rearrange("p a b -> p (a b)")

    def sb(self, stack, name, shape, dt=F32):
        self.tensors += 1
        return stack.enter_context(self.nc.sbuf_tensor(f"{name}_{self.tensors}", shape, dt))

    def dram(self, name, shape):
        return self.nc.dram_tensor(name, shape, F32, kind="Internal").ap()

    def sem(self, name):
        if name not in self.sems:
            self.sems[name] = Sem(self.nc, self.stack, name)
        return self.sems[name]


V_C, V_LNG, V_LNB, V_LBL, V_QN, V_KN, V_HN = 0, 16, 48, 80, 88, 90, 92
V_ROWS = 94


def setup(k):
    nc, a = k.nc, k.a
    with ExitStack() as st:
        rows = k.sb(st, "vec_rows", [V_ROWS, P])
        ada = k.sb(st, "ada_rows", [DEPTH * MB, P])
        tmp = k.sb(st, "lb_tmp", [P, 8, 4])
        s_in, s_t, s_v, s_e, s_pad = k.sem("rows_loaded"), k.sem("rows_turned"), k.sem("vec_step"), k.sem("lb_exp"), k.sem("const_loaded")
        with nc.Block() as block:
            @block.sync
            def _(sp):
                for dst, src in (
                    (rows[V_C:V_C + 8], a["c"].rearrange("a (j p) -> (a j) p", p=P)),
                    (rows[V_C + 8:V_C + 16], a["c_ctx"].rearrange("(j p) -> j p", p=P)),
                    (rows[V_LNG:V_LNG + 32], a["ln_g"].rearrange("l w (j p) -> (l w j) p", p=P)),
                    (rows[V_LNB:V_LNB + 32], a["ln_b"].rearrange("l w (j p) -> (l w j) p", p=P)),
                    (rows[V_LBL:V_LBL + 8], a["hgrn_lb_logits"].rearrange("l d (j p) -> (l d j) p", p=P)),
                    (ada[:], a["b_ada"].rearrange("l (j p) -> (l j) p", p=P)),
                    (k.ident[:], a["c_ident"]), (k.mean_d[:], a["c_mean_d"]),
                    (k.mean_h[:], a["c_mean_h"]), (k.rot[:], a["c_rot"]),
                ):
                    sp.dma_start(dst, src).then_inc(s_in.h, 16)
                for row, name in ((V_QN, "gqa_q_norm"), (V_KN, "gqa_k_norm"), (V_HN, "hgrn_norm")):
                    for half in range(2):
                        sp.dma_start(rows[row:row + DEPTH, half * HD:(half + 1) * HD], a[name]).then_inc(s_in.h, 16)

            @block.tensor
            def _(pe):
                pe.wait_ge(s_in.h, 16 * 16)
                nc.tensor.transpose(k.psum[:, 0, 0:V_ROWS], rows[:], k.ident[0:V_ROWS, 0:V_ROWS])
                nc.tensor.transpose(k.psum[:, 1, 0:DEPTH * MB], ada[:], k.ident[0:DEPTH * MB, 0:DEPTH * MB]).then_inc(s_t.h, 1)

            @block.scalar
            def _(act):
                act.wait_ge(s_v.h, 3)
                nc.scalar.activation(tmp[:, 2:4], tmp[:, 0:2], ACT.Exp).then_inc(s_e.h, 1)
                act.wait_ge(s_v.h, 1)
                nc.scalar.activation(k.vecs[:, V_C:V_C + 16], k.vecs[:, V_C:V_C + 16], ACT.Silu).then_inc(s_e.h, 1)

            @block.vector
            def _(dve):
                n = [0]

                def step(ins):
                    ins.then_inc(s_v.h, 1)
                    n[0] += 1
                    dve.wait_ge(s_v.h, n[0])
                dve.wait_ge(s_t.h, 1)
                step(nc.vector.tensor_copy(k.vecs[:, 0:V_ROWS], k.psum[:, 0, 0:V_ROWS]))
                lg = k.vecs[:, V_LBL:V_LBL + 8].rearrange("p (l q) -> p l q", l=DEPTH)
                step(nc.vector.tensor_tensor(tmp[:, 4], lg[:, 0], lg[:, 1], ALU.max))
                step(nc.vector.tensor_tensor(tmp[:, 0:2], lg, tmp[:, 4:5].to_broadcast([P, 2, 4]), ALU.subtract))
                dve.wait_ge(s_e.h, 1)
                step(nc.vector.tensor_tensor(tmp[:, 4], tmp[:, 2], tmp[:, 3], ALU.add))
                step(nc.vector.reciprocal(tmp[:, 5], tmp[:, 4]))
                step(nc.vector.tensor_tensor(tmp[:, 0:2], tmp[:, 2:4], tmp[:, 5:6].to_broadcast([P, 2, 4]), ALU.mult))
                step(nc.vector.tensor_tensor(tmp[:, 6], tmp[:, 0], tmp[:, 1], ALU.add))
                step(nc.vector.tensor_tensor(k.lb[:, 0], tmp[:, 0], tmp[:, 0], ALU.subtract))
                step(nc.vector.tensor_tensor(k.lb[:, 1], tmp[:, 6], tmp[:, 0], ALU.subtract))
                step(nc.vector.tensor_scalar(k.lb[:], k.lb[:], 0.0, 1.0, ALU.max, ALU.min))
                step(nc.vector.tensor_scalar(k.omlb[:], k.lb[:], -1.0, 1.0, ALU.mult, ALU.add))
                step(nc.vector.tensor_scalar(k.lbs[:], k.lb[:], 2.0 ** LOG_SHIFT, None, ALU.mult))
                step(nc.vector.memset(k.fbias[:], -LOG_SHIFT * float(np.log(2.0))))
                step(nc.vector.tensor_copy(k.b_ada[:], k.psum[:, 1, 0:DEPTH * MB]))



class Modulation:
    RING = 4

    def __init__(self, k, stack, bank, ranges, W=256):
        self.k, self.bank, self.ranges, self.W = k, bank, ranges, W
        per = D // self.W
        self.pieces = [(l, v) for l, m0, m1 in ranges for v in range(m0 * per, m1 * per)]
        self.w = k.sb(stack, "ada_w", [P, self.RING, KB, self.W])
        self.s_w = [k.sem(f"ada_w_loaded{s}") for s in range(self.RING)]
        self.s_mm, self.s_v = k.sem("ada_mm"), k.sem("ada_out")
        self.c = k.vecs[:, V_C:V_C + 16].rearrange("p (t j) -> p j t", t=2)

    def load(self, sp, u):
        l, v = self.pieces[u]
        if u >= self.RING:
            sp.wait_ge(self.s_mm.h, self.s_mm.at(u - self.RING + 1))
        src = self.k.a["w_ada"][l].rearrange("(j p) n -> p j n", p=P)
        sp.dma_start(self.w[:, u % self.RING], src[:, :, v * self.W:(v + 1) * self.W]).then_inc(self.s_w[u % self.RING].h, 16)

    def product(self, pe, u):
        s_w = self.s_w[u % self.RING]
        pe.wait_ge(s_w.h, s_w.at(16 * (u // self.RING + 1)))
        for h in range(self.W // P):
            n = u * (self.W // P) + h
            for j in range(KB):
                ins = self.k.nc.tensor.matmul(self.k.psum[:, self.bank, 2 * n:2 * n + 2], self.w[:, u % self.RING, j, h * P:(h + 1) * P],
                                              self.c[:, j], start=(j == 0), stop=(j == KB - 1))
        ins.then_inc(self.s_mm.h, 1)

    def finish(self, dve):
        k = self.k
        self.steps = 0
        if not self.pieces:
            return
        dve.wait_ge(self.s_mm.h, self.s_mm.at(len(self.pieces)))
        first = n = 0
        for l, m0, m1 in self.ranges:
            count = (m1 - m0) * KB
            k.nc.vector.tensor_tensor(
                k.mods[:, l, m0 * KB:m1 * KB], k.psum[:, self.bank, 2 * first:2 * (first + count)].rearrange("p (j t) -> p j t", t=2),
                k.b_ada[:, l * MB + m0 * KB:l * MB + m1 * KB].unsqueeze(2).to_broadcast([P, count, 2]), ALU.add).then_inc(self.s_v.h, 1)
            first += count
            n += 1
        dve.wait_ge(self.s_v.h, self.s_v.at(n))
        for l, m0, m1 in self.ranges:
            for m in (1, 4):
                if m0 <= m < m1:
                    part = k.mods[:, l, m * KB:(m + 1) * KB]
                    k.nc.vector.tensor_scalar(part, part, 1.0, None, ALU.add).then_inc(self.s_v.h, 1)
                    n += 1
        self.steps = n

    def done(self):
        for s, s_w in enumerate(self.s_w):
            s_w.done(16 * len(self.pieces[s::self.RING]))
        self.s_mm.done(len(self.pieces))
        self.s_v.done(self.steps)


def turn_in(k, h_hi, h_lo, mod_ranges):
    nc = k.nc
    ROWS_IN = 4
    with ExitStack() as st:
        rows = k.sb(st, "x_rows", [P, ROWS_IN, D])
        xc = k.sb(st, "x_cm", [P, KB, NT])
        hm = k.sb(st, "h_mod", [P, 2, NT])
        mod = Modulation(k, st, 4, mod_ranges)
        n_m = len(mod.pieces)
        s_in = [k.sem(f"loaded{s}") for s in range(ROWS_IN)]
        s_out = k.sem("x_stored")
        s_t, s_x, s_m, s_hi, s_lo = (k.sem(x) for x in ("ln_turned", "ln_new_x", "ln_modulated", "ln_hi", "ln_lo"))
        with nc.Block() as block:
            @block.sync
            def _(sp):
                def load(t):
                    if t >= ROWS_IN:
                        sp.wait_ge(s_t.h, s_t.at(t - ROWS_IN + 1))
                    src = k.a["x"][0, t * P:(t + 1) * P] if t < SEQ // P else k.a["ctx"][0, t * P - SEQ:(t + 1) * P - SEQ]
                    sp.dma_start(rows[:, t % ROWS_IN], src).then_inc(s_in[t % ROWS_IN].h, 16)
                for t in range(ROWS_IN):
                    load(t)
                for t in range(TT):
                    sp.wait_ge(s_x.h, s_x.at(t + 1))
                    sp.dma_start(k.x_dram[:, :, t * P:(t + 1) * P], xc[:, :, t * P:(t + 1) * P]).then_inc(s_out.h, 16)
                    if t + ROWS_IN < TT:
                        load(t + ROWS_IN)
                sp.wait_ge(s_out.h, s_out.at(16 * TT))

            @block.tensor
            def _(pe):
                for t in range(TT):
                    pe.wait_ge(s_in[t % ROWS_IN].h, s_in[t % ROWS_IN].at(16 * (t // ROWS_IN + 1)))
                    if t >= 2:
                        pe.wait_ge(s_x.h, s_x.at(t - 1))
                    for j in range(KB):
                        ins = nc.tensor.transpose(k.psum[:, 2 * (t % 2) + j // 4, (j % 4) * P:(j % 4 + 1) * P],
                                                  rows[:, t % ROWS_IN, j * P:(j + 1) * P], k.ident[:])
                    ins.then_inc(s_t.h, 1)
                    for u in range(n_m * t // TT, n_m * (t + 1) // TT):
                        mod.product(pe, u)

            @block.vector
            def _(dve):
                for t in range(TT):
                    dve.wait_ge(s_t.h, s_t.at(t + 1))
                    nc.vector.tensor_copy(xc[:, :, t * P:(t + 1) * P],
                                          k.psum[:, 2 * (t % 2):2 * (t % 2) + 2].rearrange("p a (b q) -> p (a b) q", q=P)).then_inc(s_x.h, 1)
                mod.finish(dve)
                dve.wait_ge(mod.s_v.h, mod.s_v.at(mod.steps))
                dve.wait_ge(s_x.h, s_x.at(TT))
                for j in range(KB):
                    if j >= 2:
                        dve.wait_ge(s_lo.h, s_lo.at(j - 1))
                    for c, (t0, t1) in enumerate(((0, SEQ), (SEQ, NT))):
                        ins = nc.vector.tensor_scalar(hm[:, j % 2, t0:t1], xc[:, j, t0:t1], k.mods[:, 0, KB + j, c:c + 1],
                                                      k.mods[:, 0, j, c:c + 1], ALU.mult, ALU.add)
                    ins.then_inc(s_m.h, 1)

            @block.scalar
            def _(act):
                for u in range(n_m):
                    mod.load(act, u)
                for j in range(KB):
                    act.wait_ge(s_m.h, s_m.at(j + 1))
                    nc.scalar.copy(h_hi[:, j], hm[:, j % 2]).then_inc(s_hi.h, 1)

            @block.gpsimd
            def _(pool):
                for j in range(KB):
                    pool.wait_ge(s_hi.h, s_hi.at(j + 1))
                    nc.gpsimd.tensor_tensor(h_lo[:, j], hm[:, j % 2], h_hi[:, j].bitcast(F32), ALU.subtract).then_inc(s_lo.h, 1)
        mod.done()
    for s in range(ROWS_IN):
        s_in[s].done(16 * len(range(s, TT, ROWS_IN)))
    s_out.done(16 * TT)
    for x in (s_t, s_x):
        x.done(TT)
    for x in (s_m, s_hi, s_lo):
        x.done(KB)


def three_products(nc, out, chunks, w_hi, w_lo, h_hi, h_lo, start, stop):
    for n, (w, h) in enumerate(((w_hi, h_hi), (w_hi, h_lo), (w_lo, h_hi))):
        for t0, tn in chunks:
            ins = nc.tensor.matmul(out[:, t0:t0 + tn], w, h[:, t0:t0 + tn],
                                   start=start and n == 0, stop=stop and n == 2)
    return ins


def linear(k, src, units, tokens, h_hi, h_lo, y, split=False):
    nc = k.nc
    chunks = token_chunks(tokens)
    with ExitStack() as st:
        raw = k.sb(st, "w_raw", [P, 2, D])
        w_hi = k.sb(st, "w_hi", [P, 2, D], F32R)
        w_lo = k.sb(st, "w_lo", [P, 2, D], F32R)
        s_w = [k.sem(f"w_loaded{s}") for s in range(2)]
        s_hi, s_lo, s_mm, s_ev = (k.sem(x) for x in ("w_hi", "w_lo", "lin_products", "lin_out"))
        sets = (k.set_a, k.set_b)
        stage = k.sb(st, "lin_stage", [P, 2, NT]) if y is None else None
        s_st = [k.sem(f"lin_stored{s}") for s in range(2)]
        s_in = [k.sem(f"loaded{s}") for s in range(4)]
        s_yhi, s_ylo = k.sem("ln_hi"), k.sem("ln_lo")
        with nc.Block() as block:
            if y is None:
                @block.gpsimd
                def _(pool):
                    def store(u, s, turn):
                        pool.wait_ge(s_ev.h, s_ev.at(3) + u)
                        pool.dma_start(k.pj_dram[:, bass.ds(u, 1), 0:tokens].rearrange("p a t -> p (a t)"),
                                       stage[:, s, 0:tokens]).then_inc(s_st[s].h, 16)
                    in_pairs(pool, units, store)
                    for s in range(2):
                        pool.wait_ge(s_st[s].h, s_st[s].at(16 * ((units + 1 - s) // 2)))

            @block.sync
            def _(sp):
                for j in range(KB if split else 0):
                    sp.dma_start(y[:, j, 0:tokens], k.y_dram[:, j, 0:tokens]).then_inc(s_in[j // 2].h, 16)

                def load(u, s, turn):
                    sp.wait_ge(s_lo.h, s_lo.at(1) + u)
                    sp.dma_start(raw[:, s].rearrange("p (j q) -> p j q", j=KB), src(u)).then_inc(s_w[s].h, 16)
                in_pairs(sp, units, load)

            @block.scalar
            def _(act):
                for j in range(KB if split else 0):
                    act.wait_ge(s_in[j // 2].h, s_in[j // 2].at(32))
                    nc.scalar.copy(h_hi[:, j, 0:tokens], y[:, j, 0:tokens]).then_inc(s_yhi.h, 1)

                def hi(u, s, turn):
                    act.wait_ge(s_w[s].h, s_w[s].at(16) + turn * 16)
                    act.wait_ge(s_mm.h, s_mm.at(1) + u)
                    nc.scalar.copy(w_hi[:, s], raw[:, s]).then_inc(s_hi.h, 1)
                in_pairs(act, units, hi)

            @block.vector
            def _(dve):
                dve.sem_inc(s_lo.h, 2)
                dve.sem_inc(s_ev.h, 2)
                for j in range(KB if split else 0):
                    dve.wait_ge(s_yhi.h, s_yhi.at(j + 1))
                    nc.vector.tensor_tensor(h_lo[:, j, 0:tokens], y[:, j, 0:tokens], h_hi[:, j, 0:tokens].bitcast(F32), ALU.subtract).then_inc(s_ylo.h, 1)

                def lo(u, s):
                    dve.wait_ge(s_hi.h, s_hi.at(1) + u)
                    nc.vector.tensor_tensor(w_lo[:, s], raw[:, s], w_hi[:, s].bitcast(F32), ALU.subtract).then_inc(s_lo.h, 1)

                def evac(u, s):
                    dve.wait_ge(s_mm.h, s_mm.at(3) + u)
                    if y is None:
                        if not (isinstance(u, int) and u < 2):
                            dve.wait_ge(s_st[s].h, s_st[s].at(-8 * s) + u * 8)
                        dst = stage[:, s, 0:tokens]
                    else:
                        dst = y[:, bass.ds(u, 1), 0:tokens].rearrange("p a t -> p (a t)")
                    nc.vector.tensor_copy(dst, sets[s][:, 0:tokens]).then_inc(s_ev.h, 1)
                lo(0, 0)
                lo(1, 1)
                for s in range(2):
                    evac(s, s)
                    lo(s + 2, s)
                with dve.Fori(1, (units - 2) // 2) as i:
                    for s in range(2):
                        evac(i * 2 + s, s)
                        lo(i * 2 + s + 2, s)
                for u in range((units - 2) // 2 * 2, units):
                    evac(u, u % 2)
                    if u + 2 < units:
                        lo(u + 2, u % 2)

            @block.tensor
            def _(pe):
                pe.sem_inc(s_mm.h, 2)
                if split:
                    pe.wait_ge(s_ylo.h, s_ylo.at(KB))

                def unit(u, s, turn):
                    pe.wait_ge(s_lo.h, s_lo.at(3) + u)
                    pe.wait_ge(s_ev.h, s_ev.at(1) + u)
                    for j in range(KB):
                        cols = slice(j * P, (j + 1) * P)
                        ins = three_products(nc, sets[s], chunks, w_hi[:, s, cols], w_lo[:, s, cols],
                                             h_hi[:, j], h_lo[:, j], j == 0, j == KB - 1)
                    ins.then_inc(s_mm.h, 1)
                in_pairs(pe, units, unit)
    for s in range(2):
        s_w[s].done(16 * ((units + 1 - s) // 2))
        if y is None:
            s_st[s].done(16 * ((units + 1 - s) // 2))
    s_hi.done(units)
    for x in (s_lo, s_mm, s_ev):
        x.done(units + 2)
    if split:
        for x in s_in:
            x.done(32)
        s_yhi.done(KB)
        s_ylo.done(KB)


def residual_norm(k, l, sub, tokens, y, h_hi, h_lo, last, mod_ranges):
    nc = k.nc
    T = 256
    n_c = tokens // T
    gate = k.mods[:, l, (2 + 3 * sub) * KB:]
    if not last:
        l2, m2 = (l, 3) if sub == 0 else (l + 1, 0)
        shift, scale = k.mods[:, l2, m2 * KB:], k.mods[:, l2, (m2 + 1) * KB:]
    vec = V_LNG + (2 * l + sub) * KB
    g_ln, b_ln = k.vecs[:, vec:], k.vecs[:, vec + V_LNB - V_LNG:]
    with ExitStack() as st:
        xa = k.sb(st, "ln_x", [P, 4, KB, T])
        sq = k.sb(st, "ln_sq", [P, KB, T])
        rs = k.sb(st, "ln_rstd", [P, 2, T])
        hm = k.sb(st, "ln_h", [P, 2, KB, T])
        rows_out = k.sb(st, "out_rows", [P, 2, D]) if last else None
        mod = Modulation(k, st, 6, mod_ranges, W=P)
        s_st = [k.sem(f"out_stored{s}") for s in range(2)]
        s_in = [k.sem(f"loaded{s}") for s in range(4)]
        s_out = [k.sem(f"stored{s}") for s in range(4)]
        names = ("ln_alpha", "ln_z", "ln_mean", "ln_centred", "ln_square", "ln_var", "ln_var_eps", "ln_root", "ln_rstd", "ln_scaled",
                 "ln_new_x", "ln_modulated", "ln_hi", "ln_lo", "ln_turned")
        (s_al, s_z, s_mu, s_zc, s_sq, s_var, s_ve, s_root, s_rs, s_sc, s_x, s_m, s_hi, s_lo, s_t) = (k.sem(x) for x in names)

        def ys(c):
            return y[:, :, c * T:(c + 1) * T]

        def hs(h, c):
            return h[:, :, c * T:(c + 1) * T]

        def mod_step(u):
            return u * (n_c + 1) // len(mod.pieces)

        def every_block(x):
            return x.unsqueeze(1).to_broadcast([P, KB, T])
        TILES = T // P

        def rows_copy(e, op, c, t):
            g = c * TILES + t
            e.wait_ge(s_t.h, s_t.at(g + 1))
            if g >= 2:
                e.wait_ge(s_st[g % 2].h, 16 * (g // 2))
            op(rows_out[:, g % 2], k.psum[:, 4 + 2 * (g % 2):6 + 2 * (g % 2)].rearrange("p a b -> p (a b)")).then_inc(s_row[t].h, 1)
        s_row = [k.sem(f"rows_copied{t}") for t in range(TILES)]
        with nc.Block() as block:
            @block.sync
            def _(sp):
                def load(c):
                    if c >= 4 and last:
                        sp.wait_ge(s_t.h, s_t.at((c - 3) * TILES))
                    elif c >= 4:
                        sp.wait_ge(s_out[c % 4].h, s_out[c % 4].at(16 * (c // 4)))
                        sp.wait_ge(s_m.h, s_m.at(c - 3))
                    sp.dma_start(xa[:, c % 4], k.x_dram[:, :, c * T:(c + 1) * T]).then_inc(s_in[c % 4].h, 16)
                for c in range(min(4, n_c)):
                    load(c)
                for u in range(min(mod.RING, len(mod.pieces))):
                    mod.load(sp, u)
                for c in range(n_c):
                    if not last:
                        sp.wait_ge(s_x.h, s_x.at(c + 1))
                        sp.dma_start(k.x_dram[:, :, c * T:(c + 1) * T], xa[:, c % 4]).then_inc(s_out[c % 4].h, 16)
                    else:
                        for t in range(TILES):
                            g = c * TILES + t
                            sp.wait_ge(s_row[t].h, s_row[t].at(c + 1))
                            sp.dma_start(k.out[0, g * P:(g + 1) * P], rows_out[:, g % 2]).then_inc(s_st[g % 2].h, 16)
                    if c + 4 < n_c:
                        load(c + 4)
                if last:
                    for s in range(2):
                        sp.wait_ge(s_st[s].h, 16 * SEQ // P // 2)
                else:
                    for s in range(4):
                        sp.wait_ge(s_out[s].h, s_out[s].at(16 * len(range(s, n_c, 4))))

            @block.scalar
            def _(act):
                def alpha(c):
                    act.wait_ge(s_in[c % 4].h, s_in[c % 4].at(16 * (c // 4 + 1)))
                    nc.scalar.mul(xa[:, c % 4], xa[:, c % 4], ALPHA).then_inc(s_al.h, 1)

                def square(c):
                    act.wait_ge(s_zc.h, s_zc.at(c + 1))
                    if c >= 1:
                        act.wait_ge(s_var.h, s_var.at(c))
                    nc.scalar.activation(sq[:], ys(c), ACT.Square).then_inc(s_sq.h, 1)

                def root(c):
                    act.wait_ge(s_ve.h, s_ve.at(c + 1))
                    nc.scalar.activation(rs[:, c % 2], rs[:, c % 2], ACT.Sqrt).then_inc(s_root.h, 1)

                def finish(c):
                    act.wait_ge(s_sc.h, s_sc.at(c + 1))
                    for j in range(KB):
                        ins = nc.scalar.activation(xa[:, c % 4, j], y[:, j, c * T:(c + 1) * T], ACT.Identity,
                                                   bias=b_ln[:, j:j + 1], scale=g_ln[:, j:j + 1])
                    ins.then_inc(s_x.h, 1)

                def upper(c):
                    act.wait_ge(s_m.h, s_m.at(c + 1))
                    nc.scalar.copy(hs(h_hi, c), hm[:, c % 2]).then_inc(s_hi.h, 1)
                alpha(0)
                alpha(1)
                for c in range(n_c + 2):
                    if 1 <= c <= n_c:
                        root(c - 1)
                    if c < n_c:
                        square(c)
                    for u in range(mod.RING, len(mod.pieces)):
                        if mod_step(u - mod.RING) == c:
                            mod.load(act, u)
                    if c + 2 < n_c:
                        alpha(c + 2)
                    if c >= 2 and last:
                        rows_copy(act, nc.scalar.copy, c - 2, 0)
                    elif c >= 2:
                        upper(c - 2)
                    if 1 <= c <= n_c:
                        finish(c - 1)

            @block.gpsimd
            def _(pool):
                def lower(c):
                    pool.wait_ge(s_hi.h, s_hi.at(c + 1))
                    nc.gpsimd.tensor_tensor(hs(h_lo, c), hm[:, c % 2], hs(h_hi, c).bitcast(F32), ALU.subtract).then_inc(s_lo.h, 1)
                for c in range(n_c) if not last else ():
                    m = 0 if c * T < SEQ else 1
                    pool.wait_ge(s_x.h, s_x.at(c + 1))
                    if c >= 2:
                        pool.wait_ge(s_lo.h, s_lo.at(c - 1))
                    for j in range(KB):
                        ins = nc.gpsimd.tensor_scalar(hm[:, c % 2, j], xa[:, c % 4, j], scale[:, j, m:m + 1], shift[:, j, m:m + 1],
                                                      ALU.mult, ALU.add)
                    ins.then_inc(s_m.h, 1)
                    if c:
                        lower(c - 1)
                if not last:
                    lower(n_c - 1)

            def turn(pe, c):
                pe.wait_ge(s_x.h, s_x.at(c + 1))
                for t in range(TILES):
                    g = c * TILES + t
                    if g >= 2:
                        pe.wait_ge(s_row[t].h, s_row[t].at(c))
                    for j in range(KB):
                        ins = nc.tensor.transpose(k.psum[:, 4 + 2 * (g % 2) + j // 4, (j % 4) * P:(j % 4 + 1) * P],
                                                  xa[:, c % 4, j, t * P:(t + 1) * P], k.ident[:])
                    ins.then_inc(s_t.h, 1)

            @block.tensor
            def _(pe):
                def mean(c):
                    if c >= 2:
                        pe.wait_ge(s_zc.h, s_zc.at(c - 1))
                    for j in range(KB):
                        pe.wait_ge(s_z.h, s_z.at(c * KB + j + 1))
                        ins = nc.tensor.matmul(k.psum[:, c % 2, 0:T], k.mean_d[:], y[:, j, c * T:(c + 1) * T], start=j == 0, stop=j == KB - 1)
                    ins.then_inc(s_mu.h, 1)

                def variance(c):
                    pe.wait_ge(s_sq.h, s_sq.at(c + 1))
                    if c >= 2:
                        pe.wait_ge(s_ve.h, s_ve.at(c - 1))
                    for j in range(KB):
                        ins = nc.tensor.matmul(k.psum[:, 2 + c % 2, 0:T], k.mean_d[:], sq[:, j], start=j == 0, stop=j == KB - 1)
                    ins.then_inc(s_var.h, 1)
                mean(0)
                for c in range(n_c + 1):
                    for u in range(len(mod.pieces)):
                        if mod_step(u) == c:
                            mod.product(pe, u)
                    if c < n_c:
                        variance(c)
                    if c + 1 < n_c:
                        mean(c + 1)
                    if last and c >= 1:
                        turn(pe, c - 1)

            @block.vector
            def _(dve):
                def total(c):
                    m = 0 if c * T < SEQ else 1
                    dve.wait_ge(s_al.h, s_al.at(c + 1))
                    for j in range(KB):
                        yj = y[:, j, c * T:(c + 1) * T]
                        nc.vector.scalar_tensor_tensor(out=yj, in0=yj, scalar=gate[:, j, m:m + 1],
                                                       in1=xa[:, c % 4, j], op0=ALU.mult, op1=ALU.add).then_inc(s_z.h, 1)

                def centre(c):
                    dve.wait_ge(s_mu.h, s_mu.at(c + 1))
                    nc.vector.tensor_tensor(ys(c), ys(c), every_block(k.psum[:, c % 2, 0:T]), ALU.subtract).then_inc(s_zc.h, 1)

                def guard(c):
                    dve.wait_ge(s_var.h, s_var.at(c + 1))
                    nc.vector.tensor_scalar(rs[:, c % 2], k.psum[:, 2 + c % 2, 0:T], EPS, None, ALU.add).then_inc(s_ve.h, 1)

                def normalize(c):
                    dve.wait_ge(s_root.h, s_root.at(c + 1))
                    nc.vector.reciprocal(rs[:, c % 2], rs[:, c % 2]).then_inc(s_rs.h, 1)
                    dve.wait_ge(s_rs.h, s_rs.at(c + 1))
                    nc.vector.tensor_tensor(ys(c), ys(c), every_block(rs[:, c % 2]), ALU.mult).then_inc(s_sc.h, 1)

                total(0)
                for c in range(n_c + 2):
                    if 1 <= c <= n_c:
                        guard(c - 1)
                    if c < n_c:
                        centre(c)
                    if c + 1 < n_c:
                        total(c + 1)
                    if c >= 2 and last:
                        rows_copy(dve, nc.vector.tensor_copy, c - 2, 1)
                    if 1 <= c <= n_c:
                        normalize(c - 1)
                mod.finish(dve)
        mod.done()
    s_z.done(n_c * KB)
    for x in (s_al, s_zc, s_sq, s_var, s_sc, s_x, s_mu, s_ve, s_root, s_rs):
        x.done(n_c)
    for s in range(4):
        s_in[s].done(16 * len(range(s, n_c, 4)))
    if not last:
        for s in range(4):
            s_out[s].done(16 * len(range(s, n_c, 4)))
        for x in (s_m, s_hi, s_lo):
            x.done(n_c)


def swiglu(k, l, tokens, h_hi, h_lo, y):
    nc = k.nc
    chunks = token_chunks(tokens)
    w1 = k.a["w_ffn_in"][l].rearrange("(j p) n -> p j n", p=P)
    w2 = k.a["w_ffn_out"][l]
    with ExitStack() as st:
        raw = k.sb(st, "f_raw", [P, 3, D])
        w_hi = k.sb(st, "f_whi", [P, 3, D], F32R)
        w_lo = k.sb(st, "f_wlo", [P, 3, D], F32R)
        act_g = k.sb(st, "f_silu", [P, NT])
        hid = k.sb(st, "f_hid", [P, NT])
        u_hi = k.sb(st, "f_uhi", [P, 2, NT], F32R)
        u_lo = k.sb(st, "f_ulo", [P, 2, NT], F32R)
        kinds = ("gate", "up", "down")
        s_w = [k.sem(f"{x}_loaded") for x in kinds]
        s_hi = [k.sem(f"{x}_hi") for x in kinds]
        s_lo = [k.sem(f"{x}_lo") for x in kinds]
        s_mm = [k.sem(f"{x}_products") for x in kinds]
        s_silu, s_h, s_uhi, s_ulo, s_acc, s_out = (k.sem(x) for x in ("silu_done", "hidden_done", "hidden_hi", "hidden_lo", "acc_done", "down_out"))

        def sets(q):
            return (k.set_a, k.set_b)[q % 2][:, 0:tokens]
        with nc.Block() as block:
            @block.gpsimd
            def _(pool):
                for j in range(KB):
                    nc.gpsimd.memset(y[:, j, 0:tokens], 0.0).then_inc(k.sem("y_zero").h, 1)

            @block.sync
            def _(sp):
                def loads(j, first=False):
                    for n in range(3):
                        if not first:
                            sp.wait_ge(s_lo[n].h, s_lo[n].at(0) + j)
                        if n < 2:
                            cols = bass.ds(j * P + n * FFN, P)
                            sp.dma_start(raw[:, n].rearrange("p (j q) -> p j q", j=KB), w1[:, :, cols]).then_inc(s_w[n].h, 16)
                        else:
                            sp.dma_start(raw[:, n], w2[bass.ds(j * P, P), :]).then_inc(s_w[n].h, 16)
                loads(0, True)
                with sp.Fori(1, HB) as j:
                    loads(j)

            @block.scalar
            def _(act):
                def hi(n, j, first=False):
                    act.wait_ge(s_w[n].h, s_w[n].at(16) + j * 16)
                    if not first and n < 2:
                        act.wait_ge(s_mm[n].h, s_mm[n].at(0) + j)
                    elif not first:
                        act.wait_ge(s_out.h, s_out.at(0) + j * KB)
                    nc.scalar.copy(w_hi[:, n], raw[:, n]).then_inc(s_hi[n].h, 1)

                def block_j(j, q, first=False, more=True):
                    act.wait_ge(s_mm[0].h, s_mm[0].at(1) + j)
                    if not first:
                        act.wait_ge(s_h.h, s_h.at(0) + j)
                    nc.scalar.activation(act_g[:, 0:tokens], sets(0), ACT.Silu).then_inc(s_silu.h, 1)
                    if more:
                        hi(0, j + 1)
                        hi(1, j + 1)
                    act.wait_ge(s_h.h, s_h.at(1) + j)
                    if not (isinstance(j, int) and j < 2):
                        act.wait_ge(s_out.h, s_out.at(-KB) + j * KB)
                    nc.scalar.copy(u_hi[:, q, 0:tokens], hid[:, 0:tokens]).then_inc(s_uhi.h, 1)
                    hi(2, j, first)
                for n in range(2):
                    hi(n, 0, True)
                block_j(0, 0, True)
                block_j(1, 1)
                with act.Fori(1, HB // 2 - 1) as i:
                    for q in range(2):
                        block_j(i * 2 + q, q)
                block_j(HB - 2, 0)
                block_j(HB - 1, 1, more=False)

            @block.vector
            def _(dve):
                def lo(n, j):
                    dve.wait_ge(s_hi[n].h, s_hi[n].at(1) + j)
                    nc.vector.tensor_tensor(w_lo[:, n], raw[:, n], w_hi[:, n].bitcast(F32), ALU.subtract).then_inc(s_lo[n].h, 1)

                def gather(j):
                    for o in range(KB):
                        dve.wait_ge(s_out.h, s_out.at(1 + o) + j * KB)
                        nc.vector.tensor_tensor(y[:, o, 0:tokens], y[:, o, 0:tokens], sets(o), ALU.add).then_inc(s_acc.h, 1)

                def block_j(j, q, more=True):
                    if more:
                        lo(0, j + 1)
                    dve.wait_ge(s_silu.h, s_silu.at(1) + j)
                    dve.wait_ge(s_mm[1].h, s_mm[1].at(1) + j)
                    if not (isinstance(j, int) and j < 1):
                        dve.wait_ge(s_ulo.h, s_ulo.at(0) + j)
                    nc.vector.tensor_tensor(hid[:, 0:tokens], act_g[:, 0:tokens], sets(1), ALU.mult).then_inc(s_h.h, 1)
                    if not (isinstance(j, int) and j < 1):
                        gather(j - 1)
                    if more:
                        lo(1, j + 1)
                    dve.wait_ge(s_uhi.h, s_uhi.at(1) + j)
                    nc.vector.tensor_tensor(u_lo[:, q, 0:tokens], hid[:, 0:tokens], u_hi[:, q, 0:tokens].bitcast(F32), ALU.subtract).then_inc(s_ulo.h, 1)
                    lo(2, j)
                dve.wait_ge(k.sem("y_zero").h, k.sem("y_zero").at(KB))
                for n in range(2):
                    lo(n, 0)
                block_j(0, 0)
                block_j(1, 1)
                with dve.Fori(1, HB // 2 - 1) as i:
                    for q in range(2):
                        block_j(i * 2 + q, q)
                block_j(HB - 2, 0)
                block_j(HB - 1, 1, more=False)
                gather(HB - 1)

            @block.tensor
            def _(pe):
                def up(n, j):
                    pe.wait_ge(s_lo[n].h, s_lo[n].at(1) + j)
                    for b in range(KB):
                        cols = slice(b * P, (b + 1) * P)
                        ins = three_products(nc, sets(n), chunks, w_hi[:, n, cols], w_lo[:, n, cols], h_hi[:, b], h_lo[:, b], b == 0, b == KB - 1)
                    ins.then_inc(s_mm[n].h, 1)

                def down(j, q, last=False):
                    pe.wait_ge(s_lo[2].h, s_lo[2].at(1) + j)
                    pe.wait_ge(s_ulo.h, s_ulo.at(1) + j)
                    for o in range(KB):
                        if o == 0 and not last:
                            pe.wait_ge(s_silu.h, s_silu.at(2) + j)
                        elif o == 1 and not last:
                            pe.wait_ge(s_h.h, s_h.at(2) + j)
                        else:
                            pe.wait_ge(s_acc.h, s_acc.at(o - 1) + j * KB)
                        cols = slice(o * P, (o + 1) * P)
                        ins = three_products(nc, sets(o), chunks, w_hi[:, 2, cols], w_lo[:, 2, cols], u_hi[:, q], u_lo[:, q], True, True)
                        ins.then_inc(s_out.h, 1)

                def block_j(j, q):
                    if isinstance(j, int) and j == 1:
                        pe.wait_ge(s_silu.h, s_silu.at(1))
                    if not (isinstance(j, int) and j < 2):
                        pe.wait_ge(s_acc.h, s_acc.at(-2 * KB + KB - 1) + j * KB)
                    up(0, j)
                    if isinstance(j, int) and j == 1:
                        pe.wait_ge(s_h.h, s_h.at(1))
                    if not (isinstance(j, int) and j < 2):
                        pe.wait_ge(s_acc.h, s_acc.at(-KB) + j * KB)
                    up(1, j)
                    if not (isinstance(j, int) and j < 1):
                        down(j - 1, 1 - q)
                block_j(0, 0)
                block_j(1, 1)
                with pe.Fori(1, HB // 2) as i:
                    for q in range(2):
                        block_j(i * 2 + q, q)
                down(HB - 1, (HB - 1) % 2, last=True)
    for n in range(3):
        s_w[n].done(16 * HB)
        for x in (s_hi, s_lo, s_mm)[:3 if n < 2 else 2]:
            x[n].done(HB)
    for x in (s_silu, s_h, s_uhi, s_ulo):
        x.done(HB)
    for x in (s_acc, s_out):
        x.done(HB * KB)
    k.sem("y_zero").done(KB)



def window_start(pair):
    lo = min(max(2 * pair - NA_KH // 2, 0), ROWS - NA_KH)
    hi = min(max(2 * pair + 1 - NA_KH // 2, 0), ROWS - NA_KH)
    return lo, hi != lo


def gqa_tiles(ctx):
    tiles = [(q, [(0, 0, 512), (512, 512, 512), (1024, 1024, 256)], [(t * P, P, t) for t in range(TT)], None)
             for q in range(SEQ // P)]
    return tiles + (ctx_tiles() if ctx else [])


def ctx_tiles():
    return [(q, [(0, SEQ, CTX)], [(i * P, P, SEQ // P + i) for i in range(CTX // P)], None)
            for q in range(SEQ // P, TT)]


def na_tiles(ctx):
    tiles = []
    for pair in range(ROWS // 2):
        k0, differ = window_start(pair)
        local = (NA_KH + differ) * GRID_W
        pieces = [(0, k0 * GRID_W, 512)] + [(512, (k0 + NA_KH) * GRID_W, GRID_W)] * differ + [(local, SEQ, CTX)]
        keys = [(i * P, P, k0 // 2 + i) for i in range(4)]
        keys += [(local + i * P, P, SEQ // P + i) for i in range(CTX // P)] + [(512, GRID_W, k0 // 2 + 4)] * differ
        slot = SLOTS if differ else k0 - 2 * pair + NA_KH - 2
        tiles.append((pair, pieces, keys, (local, slot)))
    return tiles + (ctx_tiles() if ctx else [])


def attention(k, tiles, q_block, k_rows, v_all, bias, y_block):
    nc = k.nc
    work = [(half, t) for half in range(2) for t in tiles]
    n_t = len(work)
    groups = []
    for n, (_, t) in enumerate(work):
        groups += [(n, t[2][i:i + 4]) for i in range(0, len(t[2]), 4)]
    n_g = len(groups)
    assert n_t % 2 == 0 and n_g % 2 == 0
    of_tile = [[x for x in range(n_g) if groups[x][0] == n] for n in range(n_t)]
    n_q = max(t[0] for t in tiles) + 1
    copier = ["act", "act" if bias is not None else "dve"]
    stage_at = 1

    def width(t):
        return t[1][-1][0] + t[1][-1][2]
    with ExitStack() as st:
        raw = k.sb(st, "att_raw", [P, 2, 2, NT])
        qst = k.sb(st, "att_q", [P, 2, NT], F32R)
        khi = k.sb(st, "att_khi", [P, 2, NT], F32R)
        klo = k.sb(st, "att_klo", [P, 2, NT], F32R)
        vs = k.sb(st, "att_v", [P, 2, TT, HD])
        pr = k.sb(st, "att_p", [P, 2, NT])
        wb = max(width(t) for t in tiles)
        sbias = k.sb(st, "att_s", [P, 2, wb]) if bias is not None else None
        pt = k.sb(st, "att_pt", [P, 2, 512])
        o_n = k.sb(st, "att_o", [P, 3, n_q, P])
        nb = k.sb(st, "att_negmax", [P, 2])
        rsum = k.sb(st, "att_sum", [P, 2])
        rinv = k.sb(st, "att_inv", [P, 2])
        yb = k.sb(st, "att_y", [P, 2, NT])
        names = ("scores", "score_bias", "score_negmax", "probs", "p_turned", "pv", "sum_inv", "o_done", "y_turned", "y_copied")
        s_s, s_b, s_nb, s_p, s_t, s_pv, s_ri, s_o, s_yt, s_y = (k.sem(x) for x in names)
        s_pt = [k.sem(f"pt_copied{s}") for s in range(2)]
        s_qs = k.sem("q_scaled")
        s_st = [k.sem(f"stored{s}") for s in range(2)]
        s_raw = [k.sem(f"loaded{s}") for s in range(2)]
        s_hi = [k.sem(f"head_hi{s}") for s in range(2)]
        s_lo = [k.sem(f"head_lo{s}") for s in range(2)]
        s_v = [k.sem(f"head_v{s}") for s in range(2)]

        def score(slot):
            return (k.set_a, k.set_b)[slot]

        n_bias = sum(t[3] is not None for _, t in work)
        before = [sum(t[3] is not None for _, t in work[:n]) for n in range(n_t)]
        o_ps = k.psum[:, 6, 0:HD]

        def blocks(e, body):
            with e.Fori(0, 2) as b:
                body(b, False)
            body(2, True)

        def staging(b, n, last, stage):
            part = n % (n_t // 2) - stage_at
            if part in (0, 1) and n < n_t // 2:
                stage(b, 1, part)
            elif part in (0, 1) and not last:
                stage(b + 1, 0, part)

        with nc.Block() as block:
            @block.sync
            def _(sp):
                def load(b, half):
                    sp.wait_ge(s_lo[half].h, s_lo[half].at(1) + b)
                    k_p, k_b = k_rows(b, half)
                    for part in range(2):
                        rows = slice(part * HD, (part + 1) * HD)
                        sp.dma_start(raw[rows, half, 0], k.pj_dram[half * HD:(half + 1) * HD, bass.ds(q_block + b, 1)]
                                     .rearrange("p a t -> p (a t)")).then_inc(s_raw[half].h, 16)
                        sp.dma_start(raw[rows, half, 1], k.pj_dram[bass.ds(k_p, HD), bass.ds(k_b, 1)]
                                     .rearrange("p a t -> p (a t)")).then_inc(s_raw[half].h, 16)
                with sp.Fori(0, 3) as b:
                    load(b, 0)
                    load(b, 1)
                for b in range(3):
                    sp.wait_ge(s_y.h, s_y.at(b + 1))
                    sp.dma_start(k.y_dram[:, y_block + b, 0:n_q * P], yb[:, b % 2, 0:n_q * P]).then_inc(s_st[b % 2].h, 16)
                sp.wait_ge(s_st[0].h, s_st[0].at(32))
                sp.wait_ge(s_st[1].h, s_st[1].at(16))

            @block.gpsimd
            def _(pool):
                def stage(b, half):
                    if not (isinstance(b, int) and half == 0):
                        lower(b, half)
                    values(b, half)

                def lower(b, half):
                    pool.wait_ge(s_hi[half].h, s_hi[half].at(1) + b)
                    nc.gpsimd.tensor_tensor(klo[:, half], raw[:, half, 1], khi[:, half].bitcast(F32), ALU.subtract)
                    low = slice(HD, P)
                    nc.gpsimd.tensor_scalar(raw[:, half, 0], raw[:, half, 0], SCALE, None, ALU.mult).then_inc(s_qs.h, 1)
                    pool.wait_ge(s_qs.h, s_qs.at(half) + b * 2)
                    nc.gpsimd.tensor_tensor(qst[low, half], raw[low, half, 0], qst[low, half].bitcast(F32), ALU.subtract).then_inc(s_lo[half].h, 1)
                    pool.wait_ge(s_lo[half].h, s_lo[half].at(2) + b)

                def values(b, half):
                    if not isinstance(b, int):
                        pool.wait_ge(s_o.h, s_o.at(2 + (half + 1) * n_t // 2 - n_t) + b * n_t)
                    nc.gpsimd.tensor_copy(vs[:, half], v_all[:, :, bass.ds(b, 1), half * HD:(half + 1) * HD]
                                          .rearrange("p t a d -> p t (a d)")).then_inc(s_v[half].h, 1)
                stage(0, 0)
                stage(0, 1)
                with pool.Fori(1, 3) as b:
                    stage(b, 0)
                    stage(b, 1)

            @block.tensor
            def _(pe):
                pe.sem_inc(s_s.h, n_t)
                pe.sem_inc(s_pv.h, 2)
                pe.sem_inc(s_t.h, n_g)

                def scores(b, n):
                    half, t = work[n]
                    if n % (n_t // 2) == 0:
                        pe.wait_ge(s_lo[half].h, s_lo[half].at(2) + b)
                    pe.wait_ge(s_p.h, s_p.at(1 + n) + b * n_t)
                    q = qst[:, half, t[0] * P:(t[0] + 1) * P]
                    for col, tok, cnt in t[1]:
                        nc.tensor.matmul(score(n % 2)[:, col:col + cnt], q, khi[:, half, tok:tok + cnt], start=True, stop=False)
                        ins = nc.tensor.matmul(score(n % 2)[:, col:col + cnt], q, klo[:, half, tok:tok + cnt], start=False, stop=True)
                    ins.then_inc(s_s.h, 1)

                def turn(b, x):
                    n, keys = groups[x]
                    if x == of_tile[n][0]:
                        pe.wait_ge(s_p.h, s_p.at(3 + n) + b * n_t)
                    other = s_pt[1 - x % 2]
                    pe.wait_ge(other.h, other.at(1 + x // 2) + b * (n_g // 2))
                    for i, (col, rows, _) in enumerate(keys):
                        ins = nc.tensor.transpose(k.psum[0:rows, 7, i * P:(i + 1) * P], pr[:, n % 2, col:col + rows], k.ident[:])
                    ins.then_inc(s_t.h, 1)

                def product(b, x):
                    n, keys = groups[x]
                    half = work[n][0]
                    if x == of_tile[half * n_t // 2][0]:
                        pe.wait_ge(s_v[half].h, s_v[half].at(1) + b)
                    if x == of_tile[n][0]:
                        pe.wait_ge(s_o.h, s_o.at(2 + n) + b * n_t)
                    pe.wait_ge(s_pt[x % 2].h, s_pt[x % 2].at(1 + x % 2 + x // 2) + b * (n_g // 2))
                    for i, (_, rows, tile) in enumerate(keys):
                        ins = nc.tensor.matmul(o_ps, pt[0:rows, x % 2, i * P:(i + 1) * P], vs[0:rows, half, tile],
                                               start=x == of_tile[n][0] and i == 0, stop=x == of_tile[n][-1] and i == len(keys) - 1)
                    ins.then_inc(s_pv.h, 1)

                def body(b, last):
                    for x in range(n_g):
                        n = groups[x][0]
                        turn(b, x)
                        if x == of_tile[n][0] and n + 2 < n_t:
                            scores(b, n + 2)
                        elif x == of_tile[n][0] and not last:
                            scores(b + 1, n + 2 - n_t)
                        if x:
                            product(b, x - 1)
                    product(b, n_g - 1)
                scores(0, 0)
                scores(0, 1)
                blocks(pe, body)
                pe.wait_ge(s_o.h, s_o.at(2 + 3 * n_t))
                for b in range(3):
                    if b:
                        pe.wait_ge(s_y.h, s_y.at(b))
                    for q in range(n_q):
                        ins = nc.tensor.transpose(score(0)[:, q * P:(q + 1) * P], o_n[:, b, q], k.ident[:])
                    ins.then_inc(s_yt.h, 1)

            def copy(e, op, b, x):
                keys = groups[x][1]
                e.wait_ge(s_t.h, s_t.at(1 + n_g + x) + b * n_g)
                e.wait_ge(s_pv.h, s_pv.at(1 + x) + b * n_g)
                for c0, c1, rows in spans(keys):
                    ins = op(pt[0:rows, x % 2, c0:c1], k.psum[0:rows, 7, c0:c1])
                ins.then_inc(s_pt[x % 2].h, 1)

            @block.scalar
            def _(act):
                act.sem_inc(s_p.h, 2)

                def stage(b, half, part):
                    if part == 0:
                        act.wait_ge(s_raw[half].h, s_raw[half].at(64) + b * 64)
                        act.wait_ge(s_s.h, s_s.at((half + 1) * n_t // 2) + b * n_t)
                        nc.scalar.mul(qst[:, half], raw[:, half, 0], SCALE)
                    else:
                        nc.scalar.copy(khi[:, half], raw[:, half, 1]).then_inc(s_hi[half].h, 1)

                def probs(b, n):
                    t = work[n][1]
                    act.wait_ge(s_nb.h, s_nb.at(1 + n) + b * n_t)
                    prev = of_tile[n - 2][-1] - (n_g if n < 2 else 0)
                    act.wait_ge(s_t.h, s_t.at(1 + prev + n_g) + b * n_g)
                    src = sbias[:, n % 2, 0:width(t)] if t[3] else score(n % 2)[:, 0:width(t)]
                    nc.scalar.activation(pr[:, n % 2, 0:width(t)], src, ACT.Exp, bias=nb[:, n % 2:n % 2 + 1],
                                         accum_out=rsum[:, n % 2:n % 2 + 1]).then_inc(s_p.h, 1)

                def body(b, last):
                    for n in range(n_t):
                        xs = of_tile[n]
                        if copier[xs[0] % 2] == "act":
                            copy(act, nc.scalar.copy, b, xs[0])
                        if n + 1 < n_t:
                            probs(b, n + 1)
                        elif not last:
                            probs(b + 1, 0)
                        for x in xs[1:]:
                            if copier[x % 2] == "act":
                                copy(act, nc.scalar.copy, b, x)
                        staging(b, n, last, stage)
                stage(0, 0, 0)
                stage(0, 0, 1)
                probs(0, 0)
                blocks(act, body)

            @block.vector
            def _(dve):
                dve.sem_inc(s_pt[1].h, 1)
                dve.sem_inc(s_o.h, 2)
                for s in range(2):
                    dve.sem_inc(s_lo[s].h, 1)

                def negmax(b, n):
                    t = work[n][1]
                    dve.wait_ge(s_s.h, s_s.at(1 + n + n_t) + b * n_t)
                    dve.wait_ge(s_p.h, s_p.at(1 + n) + b * n_t)
                    if t[3]:
                        local, slot = t[3]
                        head = bias[:, bass.ds(b, 1), work[n][0], slot * GRID_W:slot * GRID_W + local].rearrange("p a t -> p (a t)")
                        nc.vector.tensor_tensor(sbias[:, n % 2, 0:local], score(n % 2)[:, 0:local], head, ALU.add)
                        nc.vector.tensor_copy(sbias[:, n % 2, local:width(t)], score(n % 2)[:, local:width(t)]).then_inc(s_b.h, 1)
                        dve.wait_ge(s_b.h, s_b.at(1 + before[n]) + b * n_bias)
                    src = sbias[:, n % 2, 0:width(t)] if t[3] else score(n % 2)[:, 0:width(t)]
                    nc.vector.tensor_reduce(nb[:, n % 2:n % 2 + 1], src, axis=AX.X, op=ALU.max, negate=True).then_inc(s_nb.h, 1)

                def inverse(b, n):
                    dve.wait_ge(s_p.h, s_p.at(3 + n) + b * n_t)
                    nc.vector.reciprocal(rinv[:, n % 2:n % 2 + 1], rsum[:, n % 2:n % 2 + 1]).then_inc(s_ri.h, 1)
                    dve.wait_ge(s_ri.h, s_ri.at(1 + n) + b * n_t)

                def result(b, n):
                    half, t = work[n]
                    dve.wait_ge(s_pv.h, s_pv.at(3 + of_tile[n][-1]) + b * n_g)
                    nc.vector.tensor_scalar(o_n[:, bass.ds(b, 1), t[0], half * HD:(half + 1) * HD].rearrange("p a t -> p (a t)"),
                                            o_ps, rinv[:, n % 2:n % 2 + 1], None, ALU.mult).then_inc(s_o.h, 1)

                def body(b, last):
                    for n in range(n_t):
                        xs = of_tile[n]
                        for x in xs:
                            if copier[x % 2] == "dve":
                                copy(dve, nc.vector.tensor_copy, b, x)
                        inverse(b, n)
                        if n + 2 < n_t:
                            negmax(b, n + 2)
                        elif not last:
                            negmax(b + 1, n + 2 - n_t)
                        result(b, n)
                dve.wait_ge(s_hi[0].h, s_hi[0].at(1))
                low = slice(HD, P)
                nc.vector.scalar_tensor_tensor(out=qst[low, 0], in0=raw[low, 0, 0], scalar=SCALE, in1=qst[low, 0].bitcast(F32),
                                               op0=ALU.mult, op1=ALU.subtract)
                nc.vector.tensor_tensor(klo[:, 0], raw[:, 0, 1], khi[:, 0].bitcast(F32), ALU.subtract).then_inc(s_lo[0].h, 1)
                negmax(0, 0)
                negmax(0, 1)
                blocks(dve, body)
                for b in range(3):
                    dve.wait_ge(s_yt.h, s_yt.at(b + 1))
                    if b >= 2:
                        dve.wait_ge(s_st[0].h, s_st[0].at(16))
                    nc.vector.tensor_copy(yb[:, b % 2, 0:n_q * P], score(0)[:, 0:n_q * P]).then_inc(s_y.h, 1)
    s_s.done(4 * n_t)
    s_b.done(3 * n_bias)
    s_qs.done(5)
    s_nb.done(3 * n_t)
    s_p.done(2 + 3 * n_t)
    s_t.done(4 * n_g)
    s_pv.done(2 + 3 * n_g)
    s_ri.done(3 * n_t)
    s_o.done(2 + 3 * n_t)
    s_yt.done(3)
    s_y.done(3)
    for s in range(2):
        s_pt[s].done(s + 3 * n_g // 2)
        s_st[s].done(32 - 16 * s)
        s_raw[s].done(3 * 64)
        s_hi[s].done(3)
        s_lo[s].done(4)
        s_v[s].done(3)


def spans(keys):
    out = []
    for i, (_, rows, _) in enumerate(keys):
        if out and out[-1][2] == rows:
            out[-1] = (out[-1][0], (i + 1) * P, rows)
        else:
            out.append((i * P, (i + 1) * P, rows))
    return out


def gqa_prepare(k, l, pj, v6, mod_ranges):
    nc = k.nc
    N = 4
    items = [(i, c) for i in range(N) for c in range(len(CHUNKS))]
    lat = [(i, c) for i, c in items if c < 2]
    with ExitStack() as st:
        cos = k.sb(st, "cos", [P, SEQ])
        sin = k.sb(st, "sin", [P, SEQ])
        sq = k.sb(st, "qk_sq", [P, 2, 512])
        rs = k.sb(st, "qk_rstd", [P, N, NT])
        t1 = k.sb(st, "rot_sin", [P, 2, 512])
        mod = Modulation(k, st, 6, mod_ranges)
        s_c, s_kd = k.sem("tables_loaded"), k.sem("qk_stored")
        s_sq, s_ms, s_e, s_rt, s_rc, s_n, s_ro, s_t1, s_cs, s_q, s_vt, s_v = (k.sem(x) for x in (
            "qk_square", "qk_mean", "qk_eps", "qk_root", "qk_rstd", "qk_normed", "qk_rotated", "rot_sin", "qk_cos", "qk_done", "v_turned", "v_copied"))
        with nc.Block() as block:
            @block.sync
            def _(sp):
                sp.dma_start(cos[:], k.a["c_cos"]).then_inc(s_c.h, 16)
                sp.dma_start(sin[:], k.a["c_sin"]).then_inc(s_c.h, 16)
                for u in range(len(mod.pieces)):
                    mod.load(sp, u)
                sp.wait_ge(s_q.h, s_q.at(len(lat)))
                for i in range(N):
                    sp.dma_start(k.pj_dram[:, GQ_COL // P + i], pj[:, i]).then_inc(s_kd.h, 16)
                sp.wait_ge(s_kd.h, s_kd.at(N * 16))

            @block.scalar
            def _(act):
                for n, (i, c) in enumerate(items):
                    t0, tn = CHUNKS[c]
                    if n >= 2:
                        act.wait_ge(s_ms.h, s_ms.at(n - 1))
                    nc.scalar.activation(sq[:, n % 2, 0:tn], pj[:, i, t0:t0 + tn], ACT.Square).then_inc(s_sq.h, 1)
                act.wait_ge(s_e.h, s_e.at(len(items)))
                for i in range(N):
                    nc.scalar.activation(rs[:, i], rs[:, i], ACT.Sqrt).then_inc(s_rt.h, 1)

            @block.tensor
            def _(pe):
                for n, (i, c) in enumerate(items):
                    tn = CHUNKS[c][1]
                    pe.wait_ge(s_sq.h, s_sq.at(n + 1))
                    if n >= 2:
                        pe.wait_ge(s_e.h, s_e.at(n - 1))
                    nc.tensor.matmul(k.psum[:, n % 2, 0:tn], k.mean_h[:], sq[:, n % 2, 0:tn], start=True, stop=True).then_inc(s_ms.h, 1)
                for t in range(TT):
                    if t >= 2:
                        pe.wait_ge(s_v.h, s_v.at(2 * (t - 1)))
                    nc.tensor.transpose(k.psum[:, 4 + t % 2, 0:P], pj[:, 4, t * P:(t + 1) * P], k.ident[:]).then_inc(s_vt.h, 1)
                for u in range(len(mod.pieces)):
                    mod.product(pe, u)
                for n, (i, c) in enumerate(lat):
                    t0, tn = CHUNKS[c]
                    pe.wait_ge(s_n.h, s_n.at(items.index((i, c)) + 1))
                    if n >= 2:
                        pe.wait_ge(s_t1.h, s_t1.at(n - 1))
                    nc.tensor.matmul(k.psum[:, 2 + n % 2, 0:tn], k.rot[:], pj[:, i, t0:t0 + tn], start=True, stop=True).then_inc(s_ro.h, 1)

            @block.vector
            def _(dve):
                for n, (i, c) in enumerate(items):
                    t0, tn = CHUNKS[c]
                    dve.wait_ge(s_ms.h, s_ms.at(n + 1))
                    nc.vector.tensor_scalar(rs[:, i, t0:t0 + tn], k.psum[:, n % 2, 0:tn], EPS, None, ALU.add).then_inc(s_e.h, 1)
                for t in range(TT):
                    dve.wait_ge(s_vt.h, s_vt.at(t + 1))
                    for kv in range(2):
                        dst = v6[:, t].rearrange("p a (h d) -> p (a h) d", h=2)[:, 3 * kv:3 * kv + 3]
                        nc.vector.tensor_copy(dst, k.psum[:, 4 + t % 2, kv * HD:(kv + 1) * HD].unsqueeze(1).to_broadcast([P, 3, HD])).then_inc(s_v.h, 1)
                for n, (i, c) in enumerate(items):
                    t0, tn = CHUNKS[c]
                    if c == 0:
                        dve.wait_ge(s_rt.h, s_rt.at(i + 1))
                        nc.vector.reciprocal(rs[:, i], rs[:, i]).then_inc(s_rc.h, 1)
                        dve.wait_ge(s_rc.h, s_rc.at(i + 1))
                    col = (V_QN if i < 3 else V_KN) + l
                    nc.vector.scalar_tensor_tensor(out=pj[:, i, t0:t0 + tn], in0=pj[:, i, t0:t0 + tn], scalar=k.vecs[:, col:col + 1],
                                                   in1=rs[:, i, t0:t0 + tn], op0=ALU.mult, op1=ALU.mult).then_inc(s_n.h, 1)
                dve.wait_ge(s_c.h, s_c.at(32))
                for n, (i, c) in enumerate(lat):
                    t0, tn = CHUNKS[c]
                    dve.wait_ge(s_ro.h, s_ro.at(n + 1))
                    nc.vector.tensor_tensor(t1[:, n % 2, 0:tn], k.psum[:, 2 + n % 2, 0:tn], sin[:, t0:t0 + tn], ALU.mult).then_inc(s_t1.h, 1)
                    nc.vector.tensor_tensor(pj[:, i, t0:t0 + tn], pj[:, i, t0:t0 + tn], cos[:, t0:t0 + tn], ALU.mult).then_inc(s_cs.h, 1)
                    dve.wait_ge(s_cs.h, s_cs.at(n + 1))
                    nc.vector.tensor_tensor(pj[:, i, t0:t0 + tn], pj[:, i, t0:t0 + tn], t1[:, n % 2, 0:tn], ALU.add).then_inc(s_q.h, 1)
                mod.finish(dve)
        mod.done()
    for x in (s_sq, s_ms, s_e, s_n):
        x.done(len(items))
    for x in (s_ro, s_t1, s_cs, s_q):
        x.done(len(lat))
    s_rt.done(N)
    s_rc.done(N)
    s_vt.done(TT)
    s_v.done(2 * TT)
    s_c.done(32)
    s_kd.done(N * 16)


def na_prepare(k, l, pj, v6, bias):
    nc = k.nc
    n_s = SLOTS + MID
    with ExitStack() as st:
        rows = k.sb(st, "rpb_rows", [90, P])
        colm = k.sb(st, "col_mask", [P, GRID_W])
        midm = k.sb(st, "mid_mask", [P, MID, GRID_W])
        s_sk = k.sem("rpb_skewed")
        s_z, s_r, s_pad, s_b, s_m, s_cm, s_mid, s_vt, s_v = (k.sem(x) for x in (
            "rpb_zero", "rpb_loaded", "rpb_padded", "bias_loaded", "masks_loaded", "bias_masked", "bias_middle", "nv_turned", "nv_copied"))
        b4 = bias.rearrange("p a h (s c) -> p (a h) s c", c=GRID_W)
        with nc.Block() as block:
            @block.gpsimd
            def _(pool):
                nc.gpsimd.memset(rows[:], 0.0).then_inc(s_z.h, 1)

            @block.sync
            def _(sp):
                sp.dma_start(colm[:], k.a["c_colmask"]).then_inc(s_m.h, 16)
                sp.dma_start(midm[:], k.a["c_midmask"].rearrange("p (s c) -> p s c", s=MID)).then_inc(s_m.h, 16)
                sp.wait_ge(s_z.h, s_z.at(1))
                mid = GRID_W - 1 - (NA_KW - 1)
                sp.dma_start(rows[:, mid:mid + 2 * NA_KW - 1], k.a["na_rpb"][l].rearrange("h r c -> (h r) c")).then_inc(s_r.h, 16)
                sp.wait_ge(s_r.h, s_r.at(16))
                sp.dma_start(k.rpb_dram, rows[:]).then_inc(s_pad.h, 16)
                sp.wait_ge(s_pad.h, s_pad.at(16))
                skewed = bass.AP(k.rpb_dram.tensor, GRID_W - 1, [[P, 90], [-1, GRID_W], [1, GRID_W]])
                sp.dma_start(k.rpb_skew, skewed).then_inc(s_sk.h, 16)
                sp.wait_ge(s_sk.h, s_sk.at(16))
                for h in range(6):
                    for par in range(2):
                        src = k.rpb_skew[h * 15 + 1 - par:h * 15 + 1 - par + SLOTS].rearrange("s c j -> c s j")
                        sp.dma_start(b4[par * GRID_W:(par + 1) * GRID_W, h, 0:SLOTS], src).then_inc(s_b.h, 16)
                sp.wait_ge(s_b.h, s_b.at(12 * 16))

            @block.tensor
            def _(pe):
                for t in range(TT):
                    if t >= 2:
                        pe.wait_ge(s_v.h, s_v.at(t - 1))
                    for b in range(3):
                        ins = nc.tensor.transpose(k.psum[:, t % 2, b * P:(b + 1) * P], pj[:, b, t * P:(t + 1) * P], k.ident[:])
                    ins.then_inc(s_vt.h, 1)

            @block.vector
            def _(dve):
                for t in range(TT):
                    dve.wait_ge(s_vt.h, s_vt.at(t + 1))
                    nc.vector.tensor_copy(v6[:, t].rearrange("p a d -> p (a d)"), k.psum[:, t % 2, 0:3 * P]).then_inc(s_v.h, 1)
                dve.wait_ge(s_m.h, s_m.at(32))
                dve.wait_ge(s_b.h, s_b.at(12 * 16))
                for h in range(6):
                    nc.vector.tensor_tensor(b4[:, h, 0:SLOTS], b4[:, h, 0:SLOTS], colm[:].unsqueeze(1).to_broadcast([P, SLOTS, GRID_W]), ALU.add).then_inc(s_cm.h, 1)
                for h in range(6):
                    dve.wait_ge(s_cm.h, s_cm.at(h + 1))
                    nc.vector.tensor_tensor(b4[:, h, SLOTS:n_s], b4[:, h, 2:2 + MID], midm[:], ALU.add).then_inc(s_mid.h, 1)
    s_z.done(1)
    s_r.done(16)
    s_pad.done(16)
    s_sk.done(16)
    s_b.done(12 * 16)
    s_m.done(32)
    s_cm.done(6)
    s_mid.done(6)
    s_vt.done(TT)
    s_v.done(TT)


GROUP = 4 * CHUNK
N_G = NT // GROUP


def hgrn_gates(k, l, pj, kk, vt, o_acc, mod_ranges):
    nc = k.nc
    with ExitStack() as st:
        e = k.sb(st, "gate_exp", [P, 2, NT])
        r = k.sb(st, "gate_inv", [P, 2, NT])
        keep = k.sb(st, "keep", [P, NT])
        mod = Modulation(k, st, 6, mod_ranges)
        s_k, s_si, s_cl, s_e, s_ln, s_st, s_vt, s_v, s_o, s_den, s_sum, s_log, s_fs = (k.sem(x) for x in (
            "keep_loaded", "silu_qg", "gate_clamped", "gate_exp", "gate_logs", "gate_step", "hv_turned", "hv_copied", "o_zero", "gate_denominator", "gate_log_sum", "gate_log", "gate_running_sum"))
        shift = 2.0 ** LOG_SHIFT
        n_steps = 4 * 5
        with nc.Block() as block:
            @block.gpsimd
            def _(pool):
                def denominator(i):
                    pool.wait_ge(s_e.h, s_e.at(i + 1))
                    nc.gpsimd.tensor_scalar(r[:, i % 2], e[:, i % 2], 1.0 / shift, None, ALU.add).then_inc(s_den.h, 1)
                denominator(0)
                denominator(1)
                for t in range(TT):
                    nc.gpsimd.memset(o_acc[:, t], 0.0).then_inc(s_o.h, 1)
                for i in range(4):
                    f = pj[:, 2 + i]
                    pool.wait_ge(s_ln.h, s_ln.at(i + 1))
                    nc.gpsimd.tensor_tensor(f, e[:, i % 2], r[:, i % 2], ALU.add).then_inc(s_sum.h, 1)
                    pool.wait_ge(s_sum.h, s_sum.at(i + 1))
                    nc.gpsimd.tensor_scalar(f, f, 0.0, None, ALU.min).then_inc(s_log.h, 1)
                    if i + 2 < 4:
                        denominator(i + 2)

            @block.sync
            def _(sp):
                sp.dma_start(keep[:], k.a["c_keep"]).then_inc(s_k.h, 16)
                for u in range(len(mod.pieces)):
                    mod.load(sp, u)

            @block.scalar
            def _(act):
                for b in (0, 1, 8, 9):
                    nc.scalar.activation(pj[:, b], pj[:, b], ACT.Silu).then_inc(s_si.h, 1)

                def exp(i):
                    act.wait_ge(s_cl.h, s_cl.at(i + 1))
                    nc.scalar.activation(e[:, i % 2], pj[:, 2 + i], ACT.Exp, scale=-1.0, bias=k.fbias[:]).then_inc(s_e.h, 1)
                exp(0)
                exp(1)
                for i in range(4):
                    act.wait_ge(s_st.h, s_st.at(5 * i + 5))
                    nc.scalar.activation(e[:, i % 2], e[:, i % 2], ACT.Ln)
                    nc.scalar.activation(r[:, i % 2], r[:, i % 2], ACT.Ln).then_inc(s_ln.h, 1)
                    if i + 2 < 4:
                        act.wait_ge(s_sum.h, s_sum.at(i + 1))
                        exp(i + 2)

            @block.tensor
            def _(pe):
                for t in range(TT):
                    if t >= 2:
                        pe.wait_ge(s_v.h, s_v.at(t - 1))
                    for b in range(2):
                        ins = nc.tensor.transpose(k.psum[:, t % 2, b * P:(b + 1) * P], pj[:, 6 + b, t * P:(t + 1) * P], k.ident[:])
                    ins.then_inc(s_vt.h, 1)
                for u in range(len(mod.pieces)):
                    mod.product(pe, u)

            @block.vector
            def _(dve):
                n = [0]

                def step(ins):
                    ins.then_inc(s_st.h, 1)
                    n[0] += 1
                    dve.wait_ge(s_st.h, s_st.at(n[0]))
                for i in range(4):
                    nc.vector.tensor_scalar(pj[:, 2 + i], pj[:, 2 + i], -88.0, None, ALU.max).then_inc(s_cl.h, 1)
                for t in range(TT):
                    dve.wait_ge(s_vt.h, s_vt.at(t + 1))
                    nc.vector.tensor_copy(vt[:, t], k.psum[:, t % 2, 0:2 * P]).then_inc(s_v.h, 1)
                dve.wait_ge(s_k.h, s_k.at(16))
                def sums(i):
                    dve.wait_ge(s_log.h, s_log.at(i + 1))
                    f = pj[:, 2 + i] if i < 2 else pj[:, 2 + i][:, ::-1]
                    nc.vector.tensor_tensor_scan(f, keep[:], f, 0.0, ALU.mult, ALU.add).then_inc(s_fs.h, 1)
                for i in range(4):
                    ei, ri = e[:, i % 2], r[:, i % 2]
                    omlb, lbs = k.omlb[:, l, i:i + 1], k.lbs[:, l, i:i + 1]
                    dve.wait_ge(s_den.h, s_den.at(i + 1))
                    step(nc.vector.reciprocal(ri, ri))
                    step(nc.vector.scalar_tensor_tensor(out=kk[:, i], in0=ei, scalar=omlb, in1=ri, op0=ALU.mult, op1=ALU.mult))
                    step(nc.vector.tensor_scalar(ri, ri, omlb, lbs, ALU.mult, ALU.add))
                    step(nc.vector.tensor_scalar(ei, ri, 1.0 / shift, 1.0 / shift, ALU.mult, ALU.max))
                    step(nc.vector.tensor_scalar(ri, ri, 1.0, None, ALU.min))
                    if i:
                        sums(i - 1)
                sums(3)
                dve.wait_ge(s_si.h, s_si.at(4))
                mod.finish(dve)
        mod.done()
    s_k.done(16)
    for x in (s_den, s_sum, s_log, s_fs):
        x.done(4)
    s_si.done(4)
    s_cl.done(4)
    s_e.done(4)
    s_ln.done(4)
    s_st.done(n_steps)
    s_vt.done(TT)
    s_v.done(TT)
    s_o.done(TT)


def hgrn_scan(k, pj, kk, vt, o_acc, ctx, mod_ranges):
    nc = k.nc
    steps = [(0, 0, SEQ), (1, 0, SEQ)]
    for i in range(1, N_G):
        steps += [(0, i, (i - 1) * GROUP), (1, i, (N_G - 1 - i) * GROUP)]
    N = len(steps)
    PAIRS = 2
    G = N * PAIRS
    g_out = 0 if ctx else 2 * PAIRS
    POOL_FACTORS = (3, 4, 5)
    with ExitStack() as st:
        z = k.sb(st, "z", [P, 2, LEVELS, 2, GROUP])
        kd = k.sb(st, "k_decayed", [P, 2, 2, GROUP])
        qd = k.sb(st, "q_decayed", [P, 3, 2, GROUP])
        kt = k.sb(st, "k_turned", [P, 2, 2, 2 * P])
        et = k.sb(st, "chunk_decay", [P, 3, 2, 4])
        mask = k.sb(st, "level_masks", [P, 2, NL * CHUNK])
        am = k.sb(st, "att_masked", [P, 4, NL * CHUNK])
        at = k.sb(st, "att_hg", [P, 2, 4, CHUNK])
        state = k.sb(st, "state", [P, 2, 4, 2, HD])
        mod = Modulation(k, st, 6, mod_ranges)
        s_mk, s_kdd, s_d, s_kx, s_ex, s_qx, s_x, s_kd, s_z, s_kt, s_kc, s_att, s_am, s_at, s_ds, s_os, s_oa, s_st, s_ad, s_s0, s_zp = (
            k.sem(x) for x in (
                "masks_in", "k_distances", "distances", "k_decays", "chunk_decays", "q_decays", "decays", "k_decayed",
                "z_ready", "k_turned", "k_copied", "att_ready", "att_masked", "att_summed", "state_add", "out_state", "out_att",
                "state_new", "out_added", "state_zero", "z_ready_pool"))

        def after(e, sem, n):
            if n > 0:
                e.wait_ge(sem.h, sem.at(n))

        def outputs(g):
            return max(0, g - g_out)

        def scored(g):
            return g >= g_out

        def view(x, lvl):
            return x.rearrange("p a (n s b) -> p (a n) s b", s=2, b=1 << lvl)

        def halves(x, lvl):
            return x.rearrange("p a (n s b) -> p a n s b", s=2, b=1 << lvl)

        def cum(q):
            d, _, tok = steps[q]
            return pj[:, 2 + 2 * d:4 + 2 * d, tok:tok + GROUP]

        def q_of(q):
            return pj[:, 0:2, steps[q][2]:steps[q][2] + GROUP]

        def k_of(q):
            d, _, tok = steps[q]
            return kk[:, 2 * d:2 * d + 2, tok:tok + GROUP]

        def pair(g):
            q, w = divmod(g, PAIRS)
            d, _, tok = steps[q]
            pr = w if d == 0 else PAIRS - 1 - w
            return q, w, d, pr, tok // P + pr
        z_used = [2 * outputs(PAIRS * (q - 1)) for q in range(N)]
        q_out = g_out // PAIRS

        def made(q):
            return max(0, q - q_out)

        def distance(q, lvl, out):
            b = 1 << lvl
            seam = b - 1 if steps[q][0] == 0 else b
            c4 = cum(q).rearrange("p a (n c) -> p a n c", c=2 * b)
            nc.gpsimd.tensor_tensor(out.rearrange("p a (n c) -> p a n c", c=2 * b), c4,
                                    c4[:, :, :, seam:seam + 1].to_broadcast([P, 2, GROUP // (2 * b), 2 * b]), ALU.subtract).then_inc(s_d.h, 1)

        def times(e, q, lvl):
            zl = halves(z[:, q % 2, lvl], lvl)
            for part in range(2):
                late = part == (1 if steps[q][0] == 0 else 0)
                ins = e.tensor_tensor(zl[:, :, :, part], zl[:, :, :, part], halves(q_of(q) if late else k_of(q), lvl)[:, :, :, part], ALU.mult)
            return ins
        with nc.Block() as block:
            @block.sync
            def _(sp):
                sp.dma_start(mask[:], k.a["c_levels"].rearrange("d p n -> p d n")).then_inc(s_mk.h, 16)
                for u in range(len(mod.pieces)):
                    mod.load(sp, u)

            @block.gpsimd
            def _(pool):
                nc.gpsimd.memset(state[:], 0.0).then_inc(s_s0.h, 1)

                def distances(q):
                    c3 = cum(q)
                    end = CHUNK - 1 if steps[q][0] == 0 else 0
                    after(pool, s_kt, q - 1)
                    for blk in range(2):
                        chunks = c3[:, blk].rearrange("p (n c) -> p n c", c=CHUNK)
                        ins = nc.gpsimd.tensor_tensor(kd[:, q % 2, blk].rearrange("p (n c) -> p n c", c=CHUNK), chunks,
                                                      chunks[:, :, end:end + 1].to_broadcast([P, 4, CHUNK]), ALU.subtract)
                    ins.then_inc(s_kdd.h, 1)
                    after(pool, s_att, z_used[q])
                    for lvl in range(LEVELS) if q >= q_out else ():
                        distance(q, lvl, z[:, q % 2, lvl])

                def factors(q):
                    if q < q_out:
                        return
                    for lvl in POOL_FACTORS:
                        after(pool, s_x, made(q) * LEVELS + lvl + 1)
                        ins = times(nc.gpsimd, q, lvl)
                    ins.then_inc(s_zp.h, 1)
                distances(0)
                distances(1)
                factors(0)
                factors(1)
                for q in range(2, N):
                    distances(q)
                    factors(q)

            @block.scalar
            def _(act):
                for q in range(N):
                    d = steps[q][0]
                    after(act, s_kdd, q + 1)
                    nc.scalar.activation(kd[:, q % 2], kd[:, q % 2], ACT.Exp, scale=-1.0).then_inc(s_kx.h, 1)
                    end = CHUNK - 1 if d == 0 else 0
                    after(act, s_st, 2 * PAIRS * (q - 2))
                    nc.scalar.activation(et[:, q % 3], cum(q).rearrange("p a (n c) -> p a n c", c=CHUNK)[:, :, :, end], ACT.Exp).then_inc(s_ex.h, 1)
                    for lvl in range(LEVELS) if q >= q_out else ():
                        after(act, s_d, made(q) * LEVELS + lvl + 1)
                        zl = view(z[:, q % 2, lvl], lvl)
                        for part in range(2):
                            late = part == (1 if d == 0 else 0)
                            ins = nc.scalar.activation(zl[:, :, part], zl[:, :, part], ACT.Exp, scale=1.0 if late else -1.0)
                        ins.then_inc(s_x.h, 1)
                    after(act, s_os, outputs(PAIRS * (q - 2)))
                    if q >= q_out:
                        nc.scalar.activation(qd[:, q % 3], cum(q), ACT.Exp).then_inc(s_qx.h, 1)
                    after(act, s_kt, q + 1)
                    after(act, s_ds, PAIRS * (q - 1))
                    nc.scalar.copy(kt[:, q % 2].rearrange("p a b -> p (a b)"), k.psum[:, 7]).then_inc(s_kc.h, 1)

            @block.vector
            def _(dve):
                dve.wait_ge(s_mk.h, s_mk.at(16))
                dve.wait_ge(s_s0.h, s_s0.at(1))

                def factors(q):
                    after(dve, s_kx, q + 1)
                    nc.vector.tensor_tensor(kd[:, q % 2], kd[:, q % 2], k_of(q), ALU.mult).then_inc(s_kd.h, 1)
                    if q < q_out:
                        return
                    for lvl in range(LEVELS):
                        if lvl not in POOL_FACTORS:
                            after(dve, s_x, made(q) * LEVELS + lvl + 1)
                            times(nc.vector, q, lvl)
                    after(dve, s_qx, made(q) + 1)
                    nc.vector.tensor_tensor(qd[:, q % 3], qd[:, q % 3], q_of(q), ALU.mult).then_inc(s_z.h, 1)
                factors(0)

                def masked(g):
                    o, d = outputs(g), pair(g)[2]
                    for h in range(2):
                        after(dve, s_att, 2 * o + h + 1)
                        after(dve, s_at, 2 * (o - 1) + h + 1)
                        nc.vector.tensor_tensor(am[:, 2 * h:2 * h + 2], k.psum[:, 2 * h:2 * h + 2, 0:NL * CHUNK],
                                                mask[:, d].unsqueeze(1).to_broadcast([P, 2, NL * CHUNK]), ALU.mult).then_inc(s_am.h, 1)

                def summed(g):
                    o = outputs(g)
                    after(dve, s_oa, o - 1)
                    for h in range(2):
                        after(dve, s_am, 2 * o + h + 1)
                        nc.vector.tensor_reduce(at[:, g % 2, 2 * h:2 * h + 2], am[:, 2 * h:2 * h + 2].rearrange("p u (l t) -> p u t l", l=NL),
                                                axis=AX.X, op=ALU.add).then_inc(s_at.h, 1)

                def gather(g):
                    q, w, d, pr, tile = pair(g)
                    o = outputs(g)
                    after(dve, s_oa, o + 1)
                    for c in range(2):
                        rows = slice(c * CHUNK, (c + 1) * CHUNK)
                        nc.vector.tensor_tensor(o_acc[rows, tile], o_acc[rows, tile], k.psum[rows, 4 + c, 0:256], ALU.add).then_inc(s_ad.h, 1)
                    after(dve, s_ad, 4 * o + 2)
                    for hh in range(2):
                        oh = o_acc[:, tile].rearrange("p (b h v) -> p b h v", b=2, h=2)[:, :, hh]
                        nc.vector.tensor_tensor(oh, oh, k.psum[:, 4 + hh, 256:384].rearrange("p (b v) -> p b v", b=2), ALU.add).then_inc(s_ad.h, 1)
                for g in range(G):
                    q, w, d, pr, tile = pair(g)
                    if scored(g):
                        masked(g)
                    if g and scored(g - 1):
                        gather(g - 1)
                    after(dve, s_ds, g + 1)
                    after(dve, s_ex, q + 1)
                    after(dve, s_os, outputs(g if w else g - 2))
                    for m in range(2):
                        c = m if d == 0 else 1 - m
                        n = 2 * w + m
                        after(dve, s_st, 2 * g if m == 0 else 2 * g + 1)
                        for blk in range(2):
                            ins = nc.vector.scalar_tensor_tensor(out=state[:, d, (n + 1) % 4, blk], in0=state[:, d, n, blk],
                                                                 scalar=et[:, q % 3, blk, 2 * pr + c:2 * pr + c + 1],
                                                                 in1=k.psum[:, 4 + c, 384 + blk * HD:384 + (blk + 1) * HD], op0=ALU.mult, op1=ALU.add)
                        ins.then_inc(s_st.h, 1)
                    if scored(g):
                        summed(g)
                    if w == 0 and q + 1 < N:
                        factors(q + 1)
                gather(G - 1)
                mod.finish(dve)

            @block.tensor
            def _(pe):
                def turn(q):
                    after(pe, s_kd, q + 1)
                    after(pe, s_kc, q)
                    for tile in range(2):
                        for blk in range(2):
                            ins = nc.tensor.transpose(k.psum[:, 7, (tile * 2 + blk) * P:(tile * 2 + blk + 1) * P],
                                                      kd[:, q % 2, blk, tile * P:(tile + 1) * P], k.ident[:])
                    ins.then_inc(s_kt.h, 1)

                def scores(g, half):
                    q, w, d, pr, tile = pair(g)
                    o = outputs(g)
                    if half == 0:
                        after(pe, s_z, made(q) + 1)
                        after(pe, s_zp, made(q) + 1)
                    after(pe, s_am, 2 * (o - 1) + half + 1)
                    for hh in range(2):
                        u = 2 * half + hh
                        rows = slice(hh * HD, (hh + 1) * HD)
                        for c in range(2):
                            toks = slice((2 * pr + c) * CHUNK, (2 * pr + c + 1) * CHUNK)
                            out = k.psum[c * CHUNK:(c + 1) * CHUNK, u]
                            for lvl in range(LEVELS):
                                zz = z[rows, q % 2, lvl, half, toks]
                                nc.tensor.matmul(out[:, lvl * CHUNK:(lvl + 1) * CHUNK], zz, zz, start=True, stop=True)
                            ins = nc.tensor.matmul(out[:, LEVELS * CHUNK:NL * CHUNK], k_of(q)[rows, half, toks], q_of(q)[rows, half, toks],
                                                   start=True, stop=True)
                    ins.then_inc(s_att.h, 1)

                def additions(g):
                    q, w, d, pr, tile = pair(g)
                    after(pe, s_kc, q + 1)
                    after(pe, s_ad, 4 * outputs(g))
                    after(pe, s_st, 2 * g)
                    for c in range(2):
                        rows = slice(c * CHUNK, (c + 1) * CHUNK)
                        for u in range(4):
                            blk, hh = u // 2, u % 2
                            cols = slice(u * HD, (u + 1) * HD)
                            ins = nc.tensor.matmul(k.psum[hh * HD:(hh + 1) * HD, 4 + c, 384 + blk * HD:384 + (blk + 1) * HD],
                                                   kt[rows, q % 2, pr, cols], vt[rows, tile, cols], start=True, stop=True)
                    ins.then_inc(s_ds.h, 1)
                turn(0)
                if scored(0):
                    scores(0, 0)
                    scores(0, 1)
                for g in range(G):
                    q, w, d, pr, tile = pair(g)
                    o = outputs(g)
                    more = g + 1 < G and scored(g + 1)
                    if w == 1 and q + 1 < N:
                        turn(q + 1)
                    if more:
                        scores(g + 1, 0)
                    additions(g)
                    if more:
                        scores(g + 1, 1)
                    for u in range(len(mod.pieces) * g // G, len(mod.pieces) * (g + 1) // G):
                        mod.product(pe, u)
                    if not scored(g):
                        continue
                    after(pe, s_z, made(q) + 1)
                    after(pe, s_st, 2 * g + 2)
                    for m in range(2):
                        c = m if d == 0 else 1 - m
                        toks = slice((2 * pr + c) * CHUNK, (2 * pr + c + 1) * CHUNK)
                        for u in range(4):
                            blk, hh = u // 2, u % 2
                            rows = slice(hh * HD, (hh + 1) * HD)
                            ins = nc.tensor.matmul(k.psum[c * CHUNK:(c + 1) * CHUNK, 4 + hh, 256 + blk * HD:256 + (blk + 1) * HD],
                                                   qd[rows, q % 3, blk, toks], state[rows, d, 2 * w + m, blk], start=True, stop=True)
                    ins.then_inc(s_os.h, 1)
                    after(pe, s_at, 2 * o + 2)
                    for c in range(2):
                        rows = slice(c * CHUNK, (c + 1) * CHUNK)
                        for u in range(4):
                            ins = nc.tensor.matmul(k.psum[rows, 4 + c, u * HD:(u + 1) * HD], at[rows, g % 2, u], vt[rows, tile, u * HD:(u + 1) * HD],
                                                   start=True, stop=True)
                    ins.then_inc(s_oa.h, 1)
        mod.done()
    s_mk.done(16)
    s_s0.done(1)
    for x in (s_kdd, s_kx, s_ex, s_kd, s_kt, s_kc):
        x.done(N)
    for x in (s_qx, s_z, s_zp):
        x.done(made(N))
    s_d.done(made(N) * LEVELS)
    s_x.done(made(N) * LEVELS)
    s_ds.done(G)
    s_st.done(2 * G)
    for x in (s_att, s_am, s_at):
        x.done(2 * outputs(G))
    for x in (s_os, s_oa):
        x.done(outputs(G))
    s_ad.done(4 * outputs(G))


def hgrn_readout(k, l, pj, o_acc, tokens):
    nc = k.nc
    n_t = tokens // P
    with ExitStack() as st:
        sq = k.sb(st, "o_sq", [P, TT, 2 * P])
        ms = k.sb(st, "o_ms", [P, TT * 4])
        yb = k.sb(st, "hg_y", [P, 2, NT])
        s_v, s_rt, s_t, s_y, s_st = k.sem("ro_step"), k.sem("ro_root"), k.sem("ro_turned"), k.sem("ro_done"), k.sem("ro_stored")
        work = [(b, t0) for b in range(2) for t0 in range(0, n_t, 4)]
        o4 = o_acc[:, 0:n_t].rearrange("p t (h v) -> p (t h) v", v=HD)
        q4 = sq[:, 0:n_t].rearrange("p t (h v) -> p (t h) v", v=HD)
        m = ms[:, 0:4 * n_t]
        with nc.Block() as block:
            @block.vector
            def _(dve):
                nc.vector.tensor_tensor(q4, o4, o4, ALU.mult).then_inc(s_v.h, 1)
                dve.wait_ge(s_v.h, s_v.at(1))
                nc.vector.tensor_reduce(m, q4, axis=AX.X, op=ALU.add).then_inc(s_v.h, 1)
                dve.wait_ge(s_v.h, s_v.at(2))
                nc.vector.tensor_scalar(m, m, 1.0 / HD, EPS, ALU.mult, ALU.add).then_inc(s_v.h, 1)
                dve.wait_ge(s_rt.h, s_rt.at(1))
                nc.vector.reciprocal(m, m).then_inc(s_v.h, 1)
                dve.wait_ge(s_v.h, s_v.at(4))
                nc.vector.tensor_tensor(o4, o4, m.unsqueeze(2).to_broadcast([P, 4 * n_t, HD]), ALU.mult).then_inc(s_v.h, 1)
                for n, (b, t0) in enumerate(work):
                    cnt = min(4, n_t - t0) * P
                    dve.wait_ge(s_t.h, s_t.at(n + 1))
                    nc.vector.scalar_tensor_tensor(out=yb[:, b, t0 * P:t0 * P + cnt], in0=k.psum[:, n % 2, 0:cnt], scalar=k.vecs[:, V_HN + l:V_HN + l + 1],
                                                   in1=pj[:, 8 + b, t0 * P:t0 * P + cnt], op0=ALU.mult, op1=ALU.mult).then_inc(s_y.h, 1)

            @block.scalar
            def _(act):
                act.wait_ge(s_v.h, s_v.at(3))
                nc.scalar.activation(m, m, ACT.Sqrt).then_inc(s_rt.h, 1)

            @block.tensor
            def _(pe):
                pe.wait_ge(s_v.h, s_v.at(5))
                for n, (b, t0) in enumerate(work):
                    if n >= 2:
                        pe.wait_ge(s_y.h, s_y.at(n - 1))
                    for t in range(t0, min(t0 + 4, n_t)):
                        ins = nc.tensor.transpose(k.psum[:, n % 2, (t - t0) * P:(t - t0 + 1) * P], o_acc[:, t, b * P:(b + 1) * P], k.ident[:])
                    ins.then_inc(s_t.h, 1)

            @block.sync
            def _(sp):
                sp.wait_ge(s_y.h, s_y.at(len(work)))
                sp.dma_start(k.y_dram[:, 0:2, 0:tokens], yb[:, :, 0:tokens]).then_inc(s_st.h, 16)
                sp.wait_ge(s_st.h, s_st.at(16))
    s_v.done(5)
    s_rt.done(1)
    s_t.done(len(work))
    s_y.done(len(work))
    s_st.done(16)


def load_blocks(k, dst, first):
    n = dst.shape[1]
    s = k.sem("blocks_loaded")
    with k.nc.Block() as block:
        @block.sync
        def _(sp):
            for i in range(n):
                sp.dma_start(dst[:, i], k.pj_dram[:, first + i]).then_inc(s.h, 16)
            sp.wait_ge(s.h, s.at(16 * n))
    s.done(16 * n)


def project_in(k, l, h_hi, h_lo):
    w_in = k.a["w_in"][l].rearrange("(j p) n -> p j n", p=P)
    linear(k, lambda u: w_in[:, :, bass.ds(u * P, P)], IN_W // P, NT, h_hi, h_lo, None)


def mix(k, l, ctx, mods):
    with ExitStack() as st:
        pj = k.sb(st, "hg_pj", [P, 10, NT])
        kk = k.sb(st, "hg_kk", [P, 4, NT])
        vt = k.sb(st, "hg_v", [P, TT, 2 * P])
        o_acc = k.sb(st, "hg_o", [P, TT, 2 * P])
        load_blocks(k, pj, HG_COL // P)
        hgrn_gates(k, l, pj, kk, vt, o_acc, mods["gates"])
        hgrn_scan(k, pj, kk, vt, o_acc, ctx, mods["scan"])
        hgrn_readout(k, l, pj, o_acc, NT if ctx else SEQ)
    with ExitStack() as st:
        v6 = k.sb(st, "gq_v", [P, TT, 3, P])
        with ExitStack() as sp:
            pj = k.sb(sp, "gq_pj", [P, 5, NT])
            load_blocks(k, pj, GQ_COL // P)
            gqa_prepare(k, l, pj, v6, mods["gqa"])
        attention(k, gqa_tiles(ctx), GQ_COL // P, lambda b, half: (((b + half) // 2) * HD, GQ_COL // P + 3), v6, None, 2)
    with ExitStack() as st:
        v6 = k.sb(st, "na_v", [P, TT, 3, P])
        bias = k.sb(st, "na_bias", [P, 3, 2, (SLOTS + MID) * GRID_W])
        with ExitStack() as sp:
            pj = k.sb(sp, "na_pj", [P, 3, NT])
            load_blocks(k, pj, NA_COL // P + 6)
            na_prepare(k, l, pj, v6, bias[:])
        attention(k, na_tiles(ctx), NA_COL // P, lambda b, half: (half * HD, NA_COL // P + 3 + b), v6, bias, 5)


MOD_PARTS = [
    {"gates": [(0, 2, 3)], "scan": [(0, 3, 4), (1, 1, 2)], "gqa": [(0, 4, 5)], "norm0": [(0, 5, 6), (1, 0, 1)], "norm1": [(1, 2, 4)]},
    {"gates": [(1, 4, 5)], "scan": [], "gqa": [(1, 5, 6)], "norm0": [], "norm1": []},
]


def build(nc, a, out):
    with ExitStack() as top:
        k = Kernel(nc, top, a, out)
        setup(k)
        with ExitStack() as st:
            h_hi = k.sb(st, "h_hi", [P, KB, NT], F32R)
            h_lo = k.sb(st, "h_lo", [P, KB, NT], F32R)
            turn_in(k, h_hi, h_lo, [(0, 0, 2)])
            project_in(k, 0, h_hi, h_lo)
        for l in range(DEPTH):
            ctx = l < DEPTH - 1
            tokens = NT if ctx else SEQ
            mix(k, l, ctx, MOD_PARTS[l])
            with ExitStack() as st:
                h_hi = k.sb(st, "h_hi", [P, KB, NT], F32R)
                h_lo = k.sb(st, "h_lo", [P, KB, NT], F32R)
                y = k.sb(st, "y", [P, KB, NT])
                w_out = a["w_out"][l].rearrange("(j p) n -> p j n", p=P)
                linear(k, lambda u: w_out[:, :, bass.ds(u * P, P)], KB, tokens, h_hi, h_lo, y, split=True)
                residual_norm(k, l, 0, tokens, y, h_hi, h_lo, False, MOD_PARTS[l]["norm0"])
                swiglu(k, l, tokens, h_hi, h_lo, y)
                residual_norm(k, l, 1, tokens, y, h_hi, h_lo, not ctx, MOD_PARTS[l]["norm1"])
                if ctx:
                    project_in(k, l + 1, h_hi, h_lo)


INPUTS = ["x", "c", "ctx", "c_ctx", "w_ada", "b_ada", "w_in", "hgrn_lb_logits", "hgrn_norm", "gqa_q_norm", "gqa_k_norm",
          "na_rpb", "w_out", "w_ffn_in", "w_ffn_out", "ln_g", "ln_b"]


def constants():
    c = {}
    c["c_ident"] = np.eye(P, dtype=np.float32)
    c["c_mean_d"] = np.full((P, P), 1.0 / D, np.float32)
    c["c_mean_h"] = np.kron(np.eye(2), np.full((HD, HD), 1.0 / HD)).astype(np.float32)
    rot = np.zeros((P, P), np.float32)
    for i in range(0, P, 2):
        rot[i + 1, i] = -1.0
        rot[i, i + 1] = 1.0
    c["c_rot"] = rot
    t = np.arange(SEQ)
    n_pairs = HD // 4
    inv = np.exp(-np.log(np.float32(10000.0)) * np.arange(n_pairs, dtype=np.float32) / n_pairs).astype(np.float32)
    ang = np.concatenate([(t // GRID_W).astype(np.float32)[:, None] * inv, (t % GRID_W).astype(np.float32)[:, None] * inv], -1)
    pair = (np.arange(P) % HD) // 2
    c["c_cos"] = np.ascontiguousarray(np.cos(ang).astype(np.float32).T[pair])
    c["c_sin"] = np.ascontiguousarray(np.sin(ang).astype(np.float32).T[pair])
    keep = np.ones((P, NT), np.float32)
    keep[:, ::CHUNK] = 0.0
    c["c_keep"] = keep
    levels = np.zeros((2, P, NL, CHUNK), np.float32)
    for d in range(2):
        for s in range(CHUNK):
            for q in range(CHUNK):
                if s == q:
                    levels[d, s::CHUNK, LEVELS, q] = 1.0
                elif (s < q) == (d == 0):
                    levels[d, s::CHUNK, (s ^ q).bit_length() - 1, q] = 1.0
    c["c_levels"] = levels.reshape(2, P, NL * CHUNK)
    qc, kc = np.arange(GRID_W)[:, None], np.arange(GRID_W)[None, :]
    start = np.clip(qc - NA_KW // 2, 0, GRID_W - NA_KW)
    col = np.where((kc >= start) & (kc < start + NA_KW), 0.0, NEG).astype(np.float32)
    c["c_colmask"] = np.concatenate([col, col])
    mid = np.zeros((P, MID, GRID_W), np.float32)
    mid[:GRID_W, MID - 1] = NEG
    mid[GRID_W:, 0] = NEG
    c["c_midmask"] = mid.reshape(P, MID * GRID_W)
    return c


def kernel(**inputs):
    import concourse.bacc as bacc
    from concourse.bass_utils import run_bass_kernel_spmd

    nc = bacc.Bacc("TRN2", target_bir_lowering=False, num_devices=1)
    arrays = {f"in_{n}": np.ascontiguousarray(inputs[n]) for n in INPUTS}
    arrays.update({f"in_{n}": v for n, v in constants().items()})
    a = {n[3:]: nc.dram_tensor(n, v.shape, mybir.dt.from_np(v.dtype), kind="ExternalInput").ap() for n, v in arrays.items()}
    out = nc.dram_tensor("out", (1, SEQ, D), F32, kind="ExternalOutput").ap()
    build(nc, a, out)
    r = run_bass_kernel_spmd(nc, [arrays], core_ids=[0])
    return r.results[0]["out"]
```
